# Optimizing a Trainium2 kernel written in Bass

```python
import math
import jax, jax.numpy as jnp
from jax import lax
import numpy as np

D_MODEL = 1024
BATCH = 1
SEQ = 2048
DEPTH = 1
DEC_BATCH = 8
DEC_SEQ = 16
PAST_LEN = 512

CHUNK = 64
D_MIX = D_MODEL
D_A = D_MIX // 2
G_A = 4
C_A = D_A // G_A
GMLP_BLOCK = 128
D_B = D_MIX - D_A
H_B = 4
DK = D_B // H_B
DV = DK
CONV_W = 4
D_QKV = 3 * D_B
DN_CHUNK = 64
D_FF = -(-8 * D_MODEL // (3 * 256)) * 256
D_IN = 2 * D_A + 4 * D_B + 2 * H_B
EPS = 1e-6

kernel_name = "hymba_gmlp_gated_deltanet_stream_step"

def rms_norm(x, g):
    xf = x.astype(jnp.float32)
    y = xf * lax.rsqrt(jnp.mean(xf * xf, axis=-1, keepdims=True) + EPS)
    return (y * g.astype(jnp.float32)).astype(x.dtype)

def l2norm(x):
    xf = x.astype(jnp.float32)
    return xf * lax.rsqrt(jnp.sum(xf * xf, axis=-1, keepdims=True) + EPS)

def causal_conv(xin, buf, w):
    L = xin.shape[1]
    xp = jnp.concatenate([buf.astype(xin.dtype), xin], axis=1)
    y = xp[:, 0:L] * w[0]
    for i in range(1, CONV_W):
        y = y + xp[:, i:i + L] * w[i]
    return y, xp[:, -(CONV_W - 1):]

def gmlp_spatial(u, v, w_s, b_s, blk):
    B, L, _ = v.shape
    nb = L // blk
    vb = v.reshape(B, nb, blk, G_A, C_A)
    ub = u.reshape(B, nb, blk, G_A, C_A)
    pos = jnp.arange(blk)
    mask = (pos[None, :] // CHUNK) <= (pos[:, None] // CHUNK)
    ws = jnp.where(mask, w_s[:, :blk, :blk], 0)
    s = jnp.einsum('gij,bnjgc->bnigc', ws, vb) + b_s[:, :blk].T[:, :, None]
    return (ub * s).reshape(B, L, D_A)

def gated_delta_chunked(q, k, v, g, beta, S0, chunk):
    B, L, H, _ = q.shape
    nc = L // chunk

    def blocks(t):
        return jnp.swapaxes(t.reshape((B, nc, chunk) + t.shape[2:]), 2, 3)

    q, k, v = blocks(q), blocks(k), blocks(v)
    beta = blocks(beta)
    bcum = jnp.cumsum(blocks(g), axis=-1)
    idx = jnp.arange(chunk)
    diff = bcum[..., :, None] - bcum[..., None, :]
    dec_strict = jnp.exp(jnp.where(idx[:, None] > idx[None, :], diff, -jnp.inf))
    dec_incl = jnp.exp(jnp.where(idx[:, None] >= idx[None, :], diff, -jnp.inf))
    M = beta[..., :, None] * jnp.einsum('bnhid,bnhjd->bnhij', k, k) * dec_strict
    T = M + jnp.eye(chunk, dtype=M.dtype)
    rhs = jnp.concatenate([v * beta[..., None], k * (beta * jnp.exp(bcum))[..., None]], axis=-1)
    sol = lax.linalg.triangular_solve(T, rhs, left_side=True, lower=True)
    u, w = sol[..., :DV], sol[..., DV:]
    attn = jnp.einsum('bnhid,bnhjd->bnhij', q, k) * dec_incl
    q_dec = q * jnp.exp(bcum)[..., None]
    b_last = bcum[..., -1:]
    k_dec = k * jnp.exp(b_last - bcum)[..., None]
    g_last = jnp.exp(b_last[..., 0])
    xs = tuple(jnp.moveaxis(t, 1, 0) for t in (u, w, attn, q_dec, k_dec, g_last))

    def step(S, inp):
        u_c, w_c, a_c, qd, kd, gl = inp
        delta = u_c - jnp.einsum('bhik,bhkv->bhiv', w_c, S)
        o = jnp.einsum('bhik,bhkv->bhiv', qd, S) + jnp.einsum('bhij,bhjv->bhiv', a_c, delta)
        S = gl[..., None, None] * S + jnp.einsum('bhik,bhiv->bhkv', kd, delta)
        return S, o

    S_fin, o = lax.scan(step, S0, xs)
    o = jnp.swapaxes(jnp.moveaxis(o, 0, 1), 2, 3).reshape(B, L, H, DV)
    return o, S_fin

def layer(x, conv_buf, S0, blk, w_in, conv_w, a_log, dt_bias, gdn_norm, gmlp_ws, gmlp_bs,
          gmlp_norm, w_o, norm1, norm2, w_gate, w_up, w_down):
    B, L, _ = x.shape
    h = rms_norm(x, norm1)
    p = h @ w_in
    o1 = 2 * D_A
    o2 = o1 + D_QKV
    o3 = o2 + D_B
    o4 = o3 + H_B
    u_a, v_a, qkv, z, b_raw, a_raw = jnp.split(p, [D_A, o1, o2, o3, o4], axis=-1)
    u_a = jax.nn.gelu(u_a)
    v_a = jax.nn.gelu(v_a)
    y_a = gmlp_spatial(u_a, v_a, gmlp_ws, gmlp_bs, blk)
    y_a = rms_norm(y_a.reshape(B, L, G_A, C_A), gmlp_norm.reshape(G_A, C_A)).reshape(B, L, D_A)
    qkv_c, new_buf = causal_conv(qkv, conv_buf, conv_w)
    qkv_c = jax.nn.silu(qkv_c)
    q, k, v = jnp.split(qkv_c, 3, axis=-1)
    q = l2norm(q.reshape(B, L, H_B, DK)) * (DK ** -0.5)
    k = l2norm(k.reshape(B, L, H_B, DK))
    v = v.reshape(B, L, H_B, DV).astype(jnp.float32)
    beta = jax.nn.sigmoid(b_raw.astype(jnp.float32))
    g = -jnp.exp(a_log.astype(jnp.float32)) * jax.nn.softplus(a_raw.astype(jnp.float32) + dt_bias.astype(jnp.float32))
    chunk = DN_CHUNK if L % DN_CHUNK == 0 else L
    o, S_new = gated_delta_chunked(q, k, v, g, beta, S0.astype(jnp.float32), chunk)
    o = rms_norm(o, gdn_norm) * jax.nn.silu(z.reshape(B, L, H_B, DV).astype(jnp.float32))
    y_b = o.reshape(B, L, D_B).astype(x.dtype)
    x = x + jnp.concatenate([y_a, y_b], axis=-1) @ w_o
    h2 = rms_norm(x, norm2)
    x = x + (jax.nn.silu(h2 @ w_gate) * (h2 @ w_up)) @ w_down
    return x, new_buf, S_new.astype(S0.dtype), v_a

def setup_inputs(seed: int = 0) -> dict:
    key = jax.random.key(seed)
    ks = jax.random.split(key, 24)

    def nrm(k, shape, s):
        return jax.random.normal(k, shape, jnp.float32) * s

    dt = jnp.exp(jax.random.uniform(ks[7], (DEPTH, H_B), jnp.float32, math.log(1e-3), math.log(1e-1)))
    return {
        "x_prompt": nrm(ks[0], (BATCH, SEQ, D_MODEL), 1.0),
        "x_sample": nrm(ks[1], (DEC_BATCH, DEC_SEQ, D_MODEL), 1.0),
        "state_gdn": nrm(ks[2], (DEPTH, DEC_BATCH, H_B, DK, DV), 0.3),
        "state_conv": nrm(ks[3], (DEPTH, DEC_BATCH, CONV_W - 1, D_QKV), 1.0),
        "w_in": nrm(ks[4], (DEPTH, D_MODEL, D_IN), D_MODEL ** -0.5),
        "conv_w": nrm(ks[5], (DEPTH, CONV_W, D_QKV), CONV_W ** -0.5),
        "a_log": jnp.log(jax.random.uniform(ks[6], (DEPTH, H_B), jnp.float32, 1.0, 16.0)),
        "dt_bias": dt + jnp.log(-jnp.expm1(-dt)),
        "gdn_norm": 1.0 + nrm(ks[8], (DEPTH, DV), 0.05),
        "gmlp_ws": nrm(ks[9], (DEPTH, G_A, GMLP_BLOCK, GMLP_BLOCK), GMLP_BLOCK ** -0.5),
        "gmlp_bs": 1.0 + nrm(ks[10], (DEPTH, G_A, GMLP_BLOCK), 0.05),
        "gmlp_norm": 1.0 + nrm(ks[11], (DEPTH, D_A), 0.05),
        "w_o": nrm(ks[12], (DEPTH, D_MIX, D_MODEL), D_MIX ** -0.5),
        "norm1": 1.0 + nrm(ks[13], (DEPTH, D_MODEL), 0.05),
        "norm2": 1.0 + nrm(ks[14], (DEPTH, D_MODEL), 0.05),
        "w_gate": nrm(ks[15], (DEPTH, D_MODEL, D_FF), D_MODEL ** -0.5),
        "w_up": nrm(ks[16], (DEPTH, D_MODEL, D_FF), D_MODEL ** -0.5),
        "w_down": nrm(ks[17], (DEPTH, D_FF, D_MODEL), D_FF ** -0.5),
        "final_norm": 1.0 + nrm(ks[18], (D_MODEL,), 0.05),
    }

def reference(x_prompt, x_sample, state_gdn, state_conv, w_in, conv_w, a_log, dt_bias, gdn_norm,
              gmlp_ws, gmlp_bs, gmlp_norm, w_o, norm1, norm2, w_gate, w_up, w_down, final_norm):
    xp = x_prompt
    xs = x_sample
    bp = xp.shape[0]
    gdn_p, conv_p, gdn_s, conv_s, v_s = [], [], [], [], []
    for l in range(DEPTH):
        params = (w_in[l], conv_w[l], a_log[l], dt_bias[l], gdn_norm[l], gmlp_ws[l], gmlp_bs[l],
                  gmlp_norm[l], w_o[l], norm1[l], norm2[l], w_gate[l], w_up[l], w_down[l])
        buf0 = jnp.zeros((bp, CONV_W - 1, D_QKV), xp.dtype)
        S0 = jnp.zeros((bp, H_B, DK, DV), state_gdn.dtype)
        xp, cb, Sp, _ = layer(xp, buf0, S0, GMLP_BLOCK, *params)
        gdn_p.append(Sp)
        conv_p.append(cb)
        xs, cbs, Ss, va = layer(xs, state_conv[l], state_gdn[l], xs.shape[1], *params)
        gdn_s.append(Ss)
        conv_s.append(cbs)
        v_s.append(va)
    y_prompt = rms_norm(xp, final_norm)
    y_sample = rms_norm(xs, final_norm)
    return (y_prompt, y_sample, jnp.stack(gdn_p), jnp.stack(conv_p), jnp.stack(gdn_s), jnp.stack(conv_s), jnp.stack(v_s))


_drawn_inputs = setup_inputs


def setup_inputs(seed=0):
    import zlib

    import numpy as np

    out = dict(_drawn_inputs(seed))
    spreads = {}
    factors = {'gdn_norm': 3.014, 'gmlp_bs': 3.867}
    for name, (base, spread) in spreads.items():
        noise = np.random.default_rng([zlib.crc32(name.encode()), seed]).standard_normal(out[name].shape)
        drawn = base * np.exp(spread * noise) if base else spread * noise
        out[name] = __import__('jax').numpy.asarray(drawn.astype(out[name].dtype))
    for name, factor in factors.items():
        out[name] = (out[name] * factor).astype(out[name].dtype)
    return out
```

```python
import math
from contextlib import ExitStack

import concourse.bass as bass
from concourse import mybir

P = 128
D_MODEL = 1024
SEQ = 2048
DEC_BATCH, DEC_SEQ = 8, 16
CHUNK = 64
D_A = 512
G_A = 4
C_A = D_A // G_A
H_B = 4
DK = DV = 128
D_B = H_B * DV
CONV_W = 4
EPS = 1e-6
LEVELS = 7
LEVELS_OF = {P: 6, DEC_SEQ: 3}
COLS = 8 + G_A + 1 + CONV_W * 12
CUTS = [(2 * D_A, 2 * D_A + D_B), (2 * D_A + D_B, 2 * D_A + 2 * D_B), (2 * D_A + 2 * D_B, 2 * D_A + 3 * D_B),
        (D_A, 2 * D_A), (2 * D_A + 3 * D_B, 2 * D_A + 4 * D_B + 2 * H_B), (0, D_A)]
CUT_OF = {"q": 0, "k": 1, "v": 2, "va": 3, "z": 4, "ba": 4, "u": 5}

ALU = mybir.AluOpType
ACT = mybir.ActivationFunctionType
F32 = mybir.dt.float32
F32R = mybir.dt.float32r


def mix_setup(nc, ctx, w_in):
    def sb(name, shape, dt=F32):
        return ctx.enter_context(nc.sbuf_tensor(name, shape, dt))

    KC = D_MODEL // P
    return dict(
        w_in=sb("w_in_sb", [P, KC, w_in.shape[1]]),
        ident=sb("ident", [P, P]),
        ones=sb("ones", [P, P]),
        upto=sb("upto", [P, P]),
        after=sb("after", [P, P]),
        link=sb("link", [P, LEVELS, P]),
        cols=sb("cols", [P, COLS]),
        dt_bias=sb("dt_bias_sb", [P, H_B]),
        neg_a=sb("neg_a", [P, H_B]),
        eps=sb("eps", [P, 1]),
        ln_scale=sb("ln_scale", [P, 1]),
    )


def mix_phase(nc, sh, a, sample):
    TILES = 1 if sample else a["x"].shape[0]
    KC = D_MODEL // P
    C = DEC_SEQ if sample else P
    B = P // C
    LV = LEVELS_OF[C]
    COL_U, COL_VA, COL_QKV, COL_Z, COL_BA = 0, D_A, 2 * D_A, 2 * D_A + 3 * D_B, 2 * D_A + 4 * D_B
    W = H_B * P
    tag = "_s" if sample else "_p"

    with nc.cleanup_on_exit(), ExitStack() as ctx:
        def sb(name, shape, dt=F32):
            return ctx.enter_context(nc.sbuf_tensor(name + tag, shape, dt))

        def sem(name):
            return nc.alloc_semaphore(name=name + tag)

        CIN = 12 * B * (CONV_W - 1 + C)
        xf = sb("xf", [P, D_MODEL])
        early = sb("early", [P, max(CIN + 4 * P + D_MODEL, H_B * B * P if sample else 0)])
        cin = early[:, 0:CIN].rearrange("p (c b r) -> p c b r", c=12, b=B)
        conv = early[:, CIN:CIN + 4 * P].rearrange("p (c i) -> p c i", c=4)
        h = early[:, CIN + 4 * P:CIN + 4 * P + D_MODEL]
        if sample:
            S = early[:, 0:H_B * B * P].rearrange("p (h b v) -> p h b v", h=H_B, b=B)
        else:
            S = sb("S", [P, H_B, B, P])[:]
        hT = sb("hT", [P, KC, P])
        tails = sb("tails", [P, 12, B * (CONV_W - 1)])
        act3 = [sb(f"silu_{x}", [P, H_B, P]) for x in "qkv"]
        sq = [sb(f"sq_{x}", [P, H_B, P]) for x in "qk"]
        z = sb("z", [P, 1 if sample else 2, H_B, P])
        u = sb("u", [P, G_A, P])
        va = sb("va", [P, D_A])
        small = sb("small", [P, 8, H_B])
        g = sb("g", [P, 2, H_B])
        beta = sb("beta", [P, 2, H_B])
        g_upto = sb("g_upto", [P, H_B, P])
        beta_diag = sb("beta_diag", [P, H_B, P])
        g_of = sb("g_of", [P, H_B, B]) if sample else None
        decay = sb("decay", [P, H_B, P])
        eb = sb("eb", [P, H_B, P])
        gates = sb("gates", [P, 3 * H_B + (H_B * B if sample else 0)])
        beta_eb = sb("beta_eb", [P, H_B])
        r_k = sb("r_k", [P, H_B, P])
        r_q = sb("r_q", [P, H_B, P])
        knbq = sb("knbq", [P, 3, H_B, P])
        kn, kb, qn = knbq[:, 0], knbq[:, 1], knbq[:, 2]
        tail_rows = knbq[0:B * (CONV_W - 1)].rearrange("p a h i -> p (a h i)")
        q_dec = sb("q_dec", [P, H_B, P])
        v_beta = sb("v_beta", [P, H_B, P])
        k_beta = sb("k_beta", [P, H_B, P])
        k_dec = sb("k_dec", [P, H_B, P])
        mt = sb("mt", [P, H_B, P])
        attn = sb("attn", [P, H_B, P])
        lt = sb("lt", [P, 2, H_B, P])
        X = sb("X", [P, H_B, P])
        XT = sb("XT", [P, H_B, P])
        LX = sb("LX", [P, H_B, P])
        w_neg = mt
        delta = LX
        ya = sb("ya", [P, G_A, P])
        sq_out = sb("sq_out", [P, H_B, P])
        o_norm = eb
        yT = xf[:].rearrange("p (c i) -> p c i", c=KC) if sample else sb("yT", [P, KC, P])[:]
        ssum = sb("ssum_m", [P, 1])
        rstd = sb("rstd_m", [P, 1])
        ws_in = sq[0]
        wsT = sb("wsT", [P, G_A, P])
        bs = sb("bs", [P, G_A, P])
        if sample:
            rows_in = sb("rows_in", [COLS, P])
            a_log = sb("a_log", [P, H_B])
            conv_in = tail_rows
            stream = sb("stream", [P, B])
            same = sb("same", [P, P])
            delta_T = kb
            delta_of = hT
            bs_in = act3[2]

        def bank(name):
            return ctx.enter_context(nc.psum_tensor(name + tag, [P, 512], F32))

        pr = [bank("pr0"), bank("pr1")]
        gb = [bank(f"gb{i}") for i in range(5)]
        gs = bank("gs")
        heads = [x[:].rearrange("p (h i) -> p h i", h=H_B) for x in gb]

        names = """set_loaded set_masks rows_turned cols_ready a_exp a_ready ws_turned ws_copied ws_ready bs_ready
            cin_turned cin_ready ws_loaded states_in x_loaded squared ln_x rstd_ready h_ready h_turned hT_ready
            ba_done xa_ready eb_raw nax_ready ex_ready lnx_ready sp_ready g_ready b1_ready beta_ready
            g_upto_ready beta_diag_ready g_of_ready
            va_pe z_pe u_pe va_done z_done u_done
            decay_pe eb_pe small_pe ssk_pe ssq_pe bb_pe gates_ready decay_exp decay_ready eb_ready
            ln_k rk_ready ln_q rq_ready kn_ready kb_ready qn_ready q_dec_ready beta_eb_ready
            v_turned k_turned kk_pe qk_pe v_beta_ready k_beta_ready k_dec_ready mt_ready attn_ready
            xt_neg xt_ready x_turned x_ready
            sa_pe ya_bias ya_mul sq_a ssa_pe ln_a ra_ready ya_ready
            w_pe w_ready delta_pe delta_ready deltaT_pe deltaT_ready o_pe sq_o_ready sso_pe ln_o ro_ready
            o_norm_ready y_ready s_pe s_ready y_stored va_stored s_stored
            tail_ready tail_turned rows_ready rows_stored""".split()
        s = {x: sem(x) for x in names}
        qkv_pe = [sem(f"{x}_pe") for x in "qkv"]
        raw = [sem(f"raw_{x}") for x in "qkv"]
        tap = [sem(f"taps_{x}") for x in "qkv"]
        head_kept = [sem(f"head_kept_{x}") for x in "qkv"]
        lt_ready, lx_pe, lx_ready = sem("lt_ready"), sem("lx_pe"), sem("lx_ready")
        xlx_pe, xlxT_pe, x_new, xT_new = sem("xlx_pe"), sem("xlxT_pe"), sem("x_new"), sem("xT_new")
        silu = [sem(f"silu_done_{x}") for x in "qkv"]
        sq_ready = [sem(f"sq_ready_{x}") for x in "qk"]
        w_cut = [sem(f"w_cut{i}") for i in range(len(CUTS))] if sample else []
        mask_step = sem("mask_step")
        if sample:
            dm_ready, sh_pe, sh_ready = sem("dm_ready"), sem("sh_pe"), sem("sh_ready")

        def past(eng, semaphore, count):
            if not (isinstance(count, int) and count <= 0):
                eng.wait_ge(semaphore, count)

        def levels(m, l):
            return m * LV + l + 1

        def over_heads(mask):
            return mask.rearrange("p (a i) -> p a i", a=1).to_broadcast([P, H_B, P])

        block = ctx.enter_context(nc.Block())

        @block.sync
        def _(sp):
            n_set = 0
            if sample:
                sp.dma_start(xf[:], a["x"][0]).then_inc(s["x_loaded"], 16)
                sp.dma_start(rows_in[0:8], a["norm1"].rearrange("(c p) -> c p", p=P)).then_inc(s["set_loaded"], 16)
                sp.dma_start(rows_in[8:12], a["gmlp_norm"].rearrange("(c p) -> c p", p=P)).then_inc(s["set_loaded"], 16)
                sp.dma_start(rows_in[12:13], a["gdn_norm"].rearrange("(c p) -> c p", p=P)).then_inc(s["set_loaded"], 16)
                sp.dma_start(rows_in[13:COLS], a["conv_w"].rearrange("i (c p) -> (i c) p", p=P)).then_inc(s["set_loaded"], 16)
                sp.dma_start(sh["dt_bias"][:], a["dt_bias"].rearrange("(a n) -> a n", a=1).to_broadcast([P, H_B])).then_inc(s["set_loaded"], 16)
                sp.dma_start(a_log[:], a["a_log"].rearrange("(a n) -> a n", a=1).to_broadcast([P, H_B])).then_inc(s["set_loaded"], 16)
                sp.dma_start(conv_in[:], a["state_conv"].rearrange("b r n -> (b r) n")).then_inc(s["set_loaded"], 16)
                sp.dma_start(bs_in[:], a["gmlp_bs"].rearrange("(a g) i -> a g i", a=1).to_broadcast([P, G_A, P])).then_inc(s["set_loaded"], 16)
                n_set = 8
                w_dram = a["w_in"].rearrange("(c p) n -> p c n", p=P)
                for i, (lo, hi) in enumerate(CUTS):
                    sp.dma_start(sh["w_in"][:, :, lo:hi], w_dram[:, :, lo:hi]).then_inc(w_cut[i], 16)
                sp.wait_ge(s["set_masks"], 1)
                for b in range(B):
                    sp.dma_start(ws_in[b * C:(b + 1) * C, :, b * C:(b + 1) * C],
                                 a["gmlp_ws"][:, 0:C, 0:C].rearrange("g i j -> i g j")).then_inc(s["ws_loaded"], 16)
                sp.wait_ge(s["tail_ready"], 1)
                sp.wait_ge(silu[2], 1)
                sp.wait_ge(s["h_turned"], 1)
                for h_ in range(H_B):
                    sp.dma_start(S[:, h_], a["state_gdn"][:, h_].rearrange("b k v -> k b v")).then_inc(s["states_in"], 16)
            else:
                sp.dma_start(xf[:], a["x"][0]).then_inc(s["x_loaded"], 16)
                sp.dma_start(ws_in[:], a["gmlp_ws"].rearrange("g i j -> i g j")).then_inc(s["set_loaded"], 16)
                sp.dma_start(bs[:], a["gmlp_bs"].rearrange("(a g) i -> a g i", a=1).to_broadcast([P, G_A, P])).then_inc(s["set_loaded"], 16)
                sp.wait_ge(s["h_ready"], 1)
                sp.dma_start(xf[:], a["x"][1]).then_inc(s["x_loaded"], 16)

            def tile(m, ahead):
                if ahead:
                    sp.wait_ge(s["h_ready"], m + 2)
                    sp.dma_start(xf[:], a["x"][m + 2] if isinstance(m, int) else
                                 a["x"][bass.ds(m + 2, 1)].rearrange("a p n -> (a p) n")).then_inc(s["x_loaded"], 16)
                sp.wait_ge(s["y_ready"], m + 1)
                sp.wait_ge(s["ya_ready"], m + 1)
                dst = a["y"][m] if isinstance(m, int) else a["y"][bass.ds(m, 1)].rearrange("a p n -> (a p) n")
                sp.dma_start(dst, yT[:].rearrange("p c i -> p (c i)")).then_inc(s["y_stored"], 16)

            if sample:
                sp.wait_ge(s["va_done"], 1)
                sp.dma_start(a["new_v"], va[:]).then_inc(s["va_stored"], 16)
                tile(0, False)
                sp.wait_ge(sh_ready, H_B)
                for h_ in range(H_B):
                    sp.dma_start(a["new_gdn"][:, h_].rearrange("b k v -> k b v"), S[:, h_]).then_inc(s["s_stored"], 16)
                sp.wait_ge(s["va_stored"], 16)
            else:
                tile(0, True)
                with sp.Fori(1, TILES - 3, 2) as m:
                    tile(m, True)
                    tile(m + 1, True)
                tile(TILES - 3, True)
                tile(TILES - 2, False)
                tile(TILES - 1, False)
                sp.wait_ge(s["s_ready"], TILES)
                sp.dma_start(a["new_gdn"].rearrange("h k v -> k h v"), S[:, :, 0, :]).then_inc(s["s_stored"], 16)
            sp.wait_ge(s["rows_ready"], 3)
            sp.dma_start(a["new_conv"], tail_rows[:]).then_inc(s["rows_stored"], 16)
            sp.wait_ge(s["y_stored"], 16 * TILES)
            sp.wait_ge(s["s_stored"], 16 * H_B if sample else 16)
            sp.wait_ge(s["rows_stored"], 16)

        @block.gpsimd
        def _(pool):
            steps = [0]

            def step(inst):
                inst.then_inc(mask_step, 1)
                steps[0] += 1
                pool.wait_ge(mask_step, steps[0])

            def keep(view, pattern, base, per_partition, op=ALU.is_ge):
                step(pool.affine_select(out=view, in_=view, compare_op=op, fill=0.0, base=base, pattern=pattern,
                                        channel_multiplier=per_partition))

            if sample:
                step(pool.memset(sh["eps"][:], EPS))
                step(pool.memset(sh["ln_scale"][:], -0.5 * math.log(DK)))
                step(pool.memset(sh["ones"][:], 1.0))
                step(pool.memset(sh["ident"][:], 1.0))
                keep(sh["ident"][:], [[-1, P]], 0, 1)
                keep(sh["ident"][:], [[1, P]], 0, -1)
                pool.memset(ws_in[:], 0.0).then_inc(s["set_masks"], 1)
                step(pool.memset(same[:], 1.0))
                v = same[:].rearrange("p (b r) -> p b r", r=C)
                keep(v, [[-C, B], [0, C]], 0, 1)
                keep(v, [[C, B], [0, C]], C - 1, -1)
                step(pool.memset(stream[:], 1.0))
                keep(stream[:], [[-C, B]], 0, 1)
                keep(stream[:], [[C, B]], C - 1, -1)
                step(pool.memset(sh["link"][:], 0.0))
                for l in range(LEVELS):
                    b = 1 << l
                    v = sh["link"][:, l, :].rearrange("p (n s r) -> p n s r", s=2, r=b)[:, :, 1, :]
                    step(pool.memset(v, 1.0))
                    keep(v, [[-2 * b, P // (2 * b)], [0, b]], 0, 1)
                    keep(v, [[2 * b, P // (2 * b)], [0, b]], b - 1, -1)
            for t_, pat, mul, op in ((sh["upto"], [[1, P]], -1, ALU.is_ge), (sh["after"], [[-1, P]], 1, ALU.is_gt)):
                if sample:
                    step(pool.tensor_copy(t_[:], same[:]))
                else:
                    step(pool.memset(t_[:], 1.0))
                keep(t_[:], pat, 0, mul, op)
            if not sample:
                step(pool.memset(cin[:, :, :, 0:CONV_W - 1], 0.0))
                step(pool.memset(S[:], 0.0))
            pool.memset(small[:], 0.0).then_inc(s["set_masks"], 1)

            def tile(m):
                for l in range(LV):
                    pool.wait_ge(s["mt_ready"], m + 1)
                    if l >= 2:
                        pool.wait_ge(lx_pe, levels(m, l - 2))
                    elif not sample:
                        past(pool, lx_pe, levels(m, l - 2))
                    pool.tensor_tensor(lt[:, l % 2], mt[:], over_heads(sh["link"][:, l + 1, :]), ALU.mult)\
                        .then_inc(lt_ready, 1)

            if sample:
                tile(0)
            else:
                tile(0)
                with pool.Fori(1, TILES - 3, 2) as m:
                    tile(m)
                    tile(m + 1)
                for m in range(TILES - 3, TILES):
                    tile(m)

        @block.scalar
        def _(act):
            def front(m):
                act.wait_ge(s["x_loaded"], 16 * (m + 1))
                past(act, s["h_turned"], m)
                act.activation(h[:], xf[:], ACT.Square, accum_out=ssum[:]).then_inc(s["squared"], 1)
                act.wait_ge(s["squared"], m + 1)
                act.activation(rstd[:], ssum[:], ACT.Ln, bias=sh["eps"][:], scale=1.0 / D_MODEL).then_inc(s["ln_x"], 1)
                act.wait_ge(s["ln_x"], m + 1)
                act.activation(rstd[:], rstd[:], ACT.Exp, scale=-0.5).then_inc(s["rstd_ready"], 1)

            def gates_raw(m):
                act.wait_ge(s["ba_done"], m + 1)
                past(act, s["b1_ready"], m)
                act.activation(small[:, 0, :], gs[:, 0:H_B], ACT.Exp, scale=-1.0).then_inc(s["eb_raw"], 1)
                act.wait_ge(s["nax_ready"], m + 1)
                act.activation(small[:, 3, :], small[:, 2, :], ACT.Exp).then_inc(s["ex_ready"], 1)
                act.wait_ge(s["ex_ready"], m + 1)
                act.activation(small[:, 4, :], small[:, 3, :], ACT.Ln, bias=1.0).then_inc(s["lnx_ready"], 1)

            def keep_raw(j, m):
                act.wait_ge(qkv_pe[j], m + 1)
                if sample:
                    act.wait_ge(s["bs_ready"], 1)
                else:
                    past(act, head_kept[j], m)
                for c in range(4):
                    last = act.activation(cin[:, 4 * j + c, :, CONV_W - 1:],
                                          pr[j % 2][:, c * P:(c + 1) * P].rearrange("p (b r) -> p b r", b=B), ACT.Copy)
                last.then_inc(raw[j], 1)

            def silu_of(j, m):
                act.wait_ge(tap[j], (m + 1) * CONV_W)
                past(act, [s["qn_ready"], s["kn_ready"], s["v_turned"]][j], m)
                act.activation(act3[j][:], conv[:], ACT.Silu).then_inc(silu[j], 1)
                if j < 2:
                    act.wait_ge(silu[j], m + 1)
                    past(act, [s["ssq_pe"], s["ssk_pe"]][j], m)
                    act.activation(sq[j][:], act3[j][:], ACT.Square).then_inc(sq_ready[j], 1)

            def gelu_v(m):
                act.wait_ge(s["va_pe"], m + 1)
                past(act, s["sa_pe"], m)
                act.activation(va[:], pr[1][:], ACT.Gelu_apprx_tanh).then_inc(s["va_done"], 1)

            def silu_z(m, par):
                act.wait_ge(s["z_pe"], m + 1)
                past(act, s["y_ready"], m - 1)
                act.activation(z[:, par], pr[0][:].rearrange("p (c i) -> p c i", i=P), ACT.Silu).then_inc(s["z_done"], 1)

            def gelu_u(m):
                act.wait_ge(s["u_pe"], m + 1)
                past(act, s["ya_mul"], m)
                act.activation(u[:], pr[1][:].rearrange("p (c i) -> p c i", i=P), ACT.Gelu_apprx_tanh)\
                   .then_inc(s["u_done"], 1)

            def rsqrt(dst, src, count, ln_sem, ready, m, scale, bias):
                act.wait_ge(count, m + 1)
                act.activation(dst[:], src, ACT.Ln, bias=sh["eps"][:], scale=scale).then_inc(ln_sem, 1)
                act.wait_ge(ln_sem, m + 1)
                if bias is None:
                    act.activation(dst[:], dst[:], ACT.Exp, scale=-0.5).then_inc(ready, 1)
                else:
                    act.activation(dst[:], dst[:], ACT.Exp, scale=-0.5, bias=bias).then_inc(ready, 1)

            def decays(m):
                act.wait_ge(s["decay_pe"], m + 1)
                past(act, s["attn_ready"], m)
                act.activation(decay[:], heads[0], ACT.Exp).then_inc(s["decay_exp"], 1)
                act.wait_ge(s["eb_pe"], m + 1)
                past(act, s["y_ready"], m)
                act.activation(eb[:], heads[1], ACT.Exp).then_inc(s["eb_ready"], 1)
                act.wait_ge(s["small_pe"], m + 1)
                past(act, s["s_ready"], m)
                n = gates.shape[1]
                act.activation(gates[:], gs[:, 16:16 + n], ACT.Exp).then_inc(s["gates_ready"], 1)
                past(act, s["kn_ready"], m)
                past(act, s["o_norm_ready"], m)
                rsqrt(r_k, heads[3], s["ssk_pe"], s["ln_k"], s["rk_ready"], m, 1.0, None)
                past(act, s["ya_ready"], m)
                rsqrt(r_q, heads[2], s["ssq_pe"], s["ln_q"], s["rq_ready"], m, 1.0, sh["ln_scale"][:])

            def v_and_x(m, par):
                act.wait_ge(s["v_turned"], m + 1)
                past(act, s["delta_pe"], m)
                for h_ in range(H_B):
                    last = act.activation(v_beta[:, h_], heads[0][:, h_], ACT.Copy, scale=beta[:, par, h_:h_ + 1])
                last.then_inc(s["v_beta_ready"], 1)
                act.wait_ge(s["x_turned"], m + 1)
                act.activation(X[:], heads[4], ACT.Copy).then_inc(s["x_ready"], 1)

            def level(l, m):
                act.wait_ge(lx_pe, levels(m, l))
                act.activation(LX[:], heads[0], ACT.Copy).then_inc(lx_ready, 1)

            def gmlp_square(m):
                act.wait_ge(s["ya_mul"], m + 1)
                past(act, s["sso_pe"], m)
                act.activation(sq_out[:], ya[:], ACT.Square).then_inc(s["sq_a"], 1)

            def scan(m):
                act.wait_ge(s["w_pe"], m + 1)
                act.activation(w_neg[:], heads[0], ACT.Copy, scale=-1.0).then_inc(s["w_ready"], 1)
                if sample:
                    act.wait_ge(s["delta_pe"], m + 1)
                    act.activation(delta_T[:], heads[1], ACT.Copy).then_inc(s["deltaT_ready"], 1)
                    act.wait_ge(s["deltaT_pe"], m + 1)
                    act.activation(delta[:], heads[0], ACT.Copy).then_inc(s["delta_ready"], 1)
                else:
                    act.wait_ge(s["delta_pe"], m + 1)
                    act.activation(delta[:], heads[1], ACT.Copy).then_inc(s["delta_ready"], 1)

            def out(m):
                act.wait_ge(s["o_pe"], m + 1)
                act.wait_ge(s["ssa_pe"], m + 1)
                act.activation(sq_out[:], heads[2], ACT.Square).then_inc(s["sq_o_ready"], 1)
                act.wait_ge(s["kn_ready"], m + 1)
                rsqrt(r_k, heads[4], s["sso_pe"], s["ln_o"], s["ro_ready"], m, 1.0 / DV, None)

            def tile(m, par, project, fronts):
                decays(m)
                if project:
                    gates_raw(m + 1)
                v_and_x(m, par)
                if project:
                    keep_raw(0, m + 1)
                for l in range(LV):
                    level(l, m)
                    if l == 0:
                        gmlp_square(m)
                        if project:
                            keep_raw(1, m + 1)
                    if l == 2:
                        act.wait_ge(s["kn_ready"], m + 1)
                        act.wait_ge(s["qn_ready"], m + 1)
                        rsqrt(r_q, heads[4], s["ssa_pe"], s["ln_a"], s["ra_ready"], m, 1.0 / C_A, None)
                        if project:
                            silu_of(0, m + 1)
                            keep_raw(2, m + 1)
                    if l == 4 and project:
                        gelu_v(m + 1)
                        silu_of(1, m + 1)
                scan(m)
                if project:
                    silu_of(2, m + 1)
                    silu_z(m + 1, 1 - par)
                out(m)
                if project:
                    gelu_u(m + 1)
                if fronts:
                    front(m + 2)

            def project_alone(m, par):
                gates_raw(m)
                for j in range(3):
                    keep_raw(j, m)
                    silu_of(j, m)
                gelu_v(m)
                silu_z(m, par)
                gelu_u(m)

            if sample:
                act.wait_ge(s["set_loaded"], 16 * 8)
                act.activation(sh["neg_a"][:], a_log[:], ACT.Exp).then_inc(s["a_exp"], 1)
                act.wait_ge(s["set_masks"], 2)
                front(0)
                for j in range(3):
                    keep_raw(j, 0)
                    silu_of(j, 0)
                gelu_v(0)
                silu_z(0, 0)
                gates_raw(0)
                gelu_u(0)
                tile(0, 0, False, False)
            else:
                act.wait_ge(s["set_masks"], 1)
                front(0)
                project_alone(0, 0)
                front(1)
                tile(0, 0, True, True)
                with act.Fori(1, TILES - 3, 2) as m:
                    tile(m, 1, True, True)
                    tile(m + 1, 0, True, True)
                tile(TILES - 3, 1, True, True)
                tile(TILES - 2, 0, True, False)
                tile(TILES - 1, 1, False, False)
            act.wait_ge(s["tail_turned"], 1)
            for j in range(3):
                act.activation(tail_rows[:, j * D_B:(j + 1) * D_B], gb[j][0:B * (CONV_W - 1), :], ACT.Copy)\
                   .then_inc(s["rows_ready"], 1)

        @block.vector
        def _(dve):
            def front(m):
                dve.wait_ge(s["rstd_ready"], m + 1)
                dve.tensor_scalar(h[:], xf[:], rstd[:, 0:1], None, ALU.mult).then_inc(s["h_ready"], 1)

            def h_columns(m):
                dve.wait_ge(s["h_turned"], m + 1)
                for i in range(2):
                    last = dve.tensor_tensor(hT[:, 4 * i:4 * i + 4], pr[i][:].rearrange("p (c i) -> p c i", i=P),
                                             sh["cols"][:, 4 * i:4 * i + 4].rearrange("p (c a) -> p c a", a=1)
                                             .to_broadcast([P, 4, P]), ALU.mult)
                last.then_inc(s["hT_ready"], 1)

            def gates_raw(m, par):
                dve.wait_ge(s["eb_raw"], m + 1)
                dve.tensor_tensor(small[:, 1, :], gs[:, H_B:2 * H_B], sh["dt_bias"][:], ALU.add).then_inc(s["xa_ready"], 1)
                dve.wait_ge(s["xa_ready"], m + 1)
                dve.scalar_tensor_tensor(out=small[:, 2, :], in0=small[:, 1, :], scalar=-1.0, in1=small[:, 1, :],
                                         op0=ALU.mult, op1=ALU.min).then_inc(s["nax_ready"], 1)
                dve.wait_ge(s["eb_raw"], m + 1)
                dve.tensor_scalar(small[:, 5, :], small[:, 0, :], 1.0, None, ALU.add).then_inc(s["b1_ready"], 1)
                dve.wait_ge(s["b1_ready"], m + 1)
                past(dve, s["beta_eb_ready"], m - 1)
                past(dve, s["v_beta_ready"], m - 1)
                dve.reciprocal(beta[:, par, :], small[:, 5, :]).then_inc(s["beta_ready"], 1)
                dve.wait_ge(s["lnx_ready"], m + 1)
                dve.scalar_tensor_tensor(out=small[:, 6, :], in0=small[:, 1, :], scalar=0.0, in1=small[:, 4, :],
                                         op0=ALU.max, op1=ALU.add).then_inc(s["sp_ready"], 1)
                dve.wait_ge(s["sp_ready"], m + 1)
                past(dve, s["small_pe"], m - 1)
                dve.tensor_tensor(g[:, par, :], small[:, 6, :], sh["neg_a"][:], ALU.mult).then_inc(s["g_ready"], 1)

            def gates_spread(m, par):
                def wide(x):
                    return x[:, par, :].rearrange("p (h a) -> p h a", a=1).to_broadcast([P, H_B, P])

                dve.wait_ge(s["g_ready"], m + 1)
                past(dve, s["eb_pe"], m)
                past(dve, s["decay_pe"], m)
                dve.tensor_tensor(g_upto[:], over_heads(sh["upto"][:]), wide(g), ALU.mult).then_inc(s["g_upto_ready"], 1)
                dve.wait_ge(s["beta_ready"], m + 1)
                past(dve, s["bb_pe"], m)
                dve.tensor_tensor(beta_diag[:], over_heads(sh["ident"][:]), wide(beta), ALU.mult)\
                   .then_inc(s["beta_diag_ready"], 1)
                if sample:
                    dve.tensor_tensor(g_of[:], stream[:].rearrange("p (a b) -> p a b", a=1).to_broadcast([P, H_B, B]),
                                      g[:, par, :].rearrange("p (h a) -> p h a", a=1).to_broadcast([P, H_B, B]),
                                      ALU.mult).then_inc(s["g_of_ready"], 1)

            def conv_tap(j, i, m):
                if i == 0:
                    dve.wait_ge(raw[j], m + 1)
                    if j > 0:
                        dve.wait_ge(silu[j - 1], m + 1)
                    else:
                        past(dve, silu[2], m)
                else:
                    dve.wait_ge(tap[j], m * CONV_W + i)
                for c in range(4):
                    o = conv[:, c].rearrange("p (b r) -> p b r", b=B)
                    x = cin[:, 4 * j + c, :, i:i + C]
                    w = sh["cols"][:, 13 + 12 * i + 4 * j + c:14 + 12 * i + 4 * j + c]
                    if i == 0:
                        last = dve.tensor_scalar(o, x, w, None, ALU.mult)
                    else:
                        last = dve.scalar_tensor_tensor(out=o, in0=x, scalar=w, in1=o, op0=ALU.mult, op1=ALU.add)
                last.then_inc(tap[j], 1)
                if i == CONV_W - 1 and not sample:
                    dve.wait_ge(tap[j], (m + 1) * CONV_W)
                    dve.tensor_copy(cin[:, 4 * j:4 * j + 4, 0, 0:CONV_W - 1], cin[:, 4 * j:4 * j + 4, 0, C:])\
                       .then_inc(head_kept[j], 1)

            def start(m, par):
                dve.wait_ge(s["decay_exp"], m + 1)
                dve.tensor_tensor(decay[:], decay[:], over_heads(sh["upto"][:]), ALU.mult).then_inc(s["decay_ready"], 1)
                dve.wait_ge(s["gates_ready"], m + 1)
                dve.tensor_tensor(beta_eb[:], beta[:, par, :], gates[:, 0:H_B], ALU.mult).then_inc(s["beta_eb_ready"], 1)
                dve.wait_ge(s["rk_ready"], m + 1)
                past(dve, s["k_turned"], m)
                past(dve, s["qk_pe"], m)
                dve.tensor_tensor(kn[:], act3[1][:], r_k[:], ALU.mult).then_inc(s["kn_ready"], 1)
                dve.wait_ge(s["kn_ready"], m + 1)
                dve.wait_ge(s["bb_pe"], m + 1)
                dve.tensor_tensor(kb[:], heads[4], kn[:], ALU.mult).then_inc(s["kb_ready"], 1)
                dve.wait_ge(s["rq_ready"], m + 1)
                dve.tensor_tensor(qn[:], act3[0][:], r_q[:], ALU.mult).then_inc(s["qn_ready"], 1)
                dve.wait_ge(s["qn_ready"], m + 1)
                dve.wait_ge(s["eb_ready"], m + 1)
                past(dve, s["o_pe"], m)
                dve.tensor_tensor(q_dec[:], qn[:], eb[:], ALU.mult).then_inc(s["q_dec_ready"], 1)

            def products(m):
                dve.wait_ge(s["kk_pe"], m + 1)
                dve.wait_ge(s["decay_ready"], m + 1)
                past(dve, s["delta_pe"], m)
                dve.tensor_tensor(mt[:], heads[2], decay[:], ALU.mult).then_inc(s["mt_ready"], 1)
                dve.wait_ge(s["mt_ready"], m + 1)
                dve.scalar_tensor_tensor(out=XT[:], in0=mt[:], scalar=-1.0, in1=over_heads(sh["link"][:, 0, :]),
                                         op0=ALU.mult, op1=ALU.mult).then_inc(s["xt_neg"], 1)
                dve.wait_ge(s["xt_neg"], m + 1)
                dve.tensor_tensor(XT[:], XT[:], over_heads(sh["ident"][:]), ALU.add).then_inc(s["xt_ready"], 1)
                dve.wait_ge(s["k_turned"], m + 1)
                dve.wait_ge(s["beta_eb_ready"], m + 1)
                past(dve, s["w_pe"], m)
                past(dve, s["s_pe"], m)
                for h_ in range(H_B):
                    last = dve.tensor_scalar(k_beta[:, h_], heads[1][:, h_], beta_eb[:, h_:h_ + 1], None, ALU.mult)
                last.then_inc(s["k_beta_ready"], 1)
                for h_ in range(H_B):
                    last = dve.tensor_scalar(k_dec[:, h_], heads[1][:, h_], gates[:, H_B + h_:H_B + h_ + 1], None, ALU.mult)
                last.then_inc(s["k_dec_ready"], 1)
                dve.wait_ge(s["qk_pe"], m + 1)
                past(dve, s["o_pe"], m)
                dve.tensor_tensor(attn[:], heads[3], decay[:], ALU.mult).then_inc(s["attn_ready"], 1)

            def level(l, m):
                if l < LV - 1:
                    dve.wait_ge(xlx_pe, m * (LV - 1) + l + 1)
                    if l == 0:
                        dve.wait_ge(s["x_ready"], m + 1)
                    else:
                        dve.wait_ge(x_new, m * (LV - 1) + l)
                    dve.tensor_tensor(X[:], X[:], heads[1], ALU.subtract).then_inc(x_new, 1)
                dve.wait_ge(xlxT_pe, levels(m, l))
                if l == 0:
                    dve.wait_ge(s["xt_ready"], m + 1)
                else:
                    dve.wait_ge(xT_new, levels(m, l - 1))
                dve.tensor_tensor(XT[:], XT[:], heads[2], ALU.subtract).then_inc(xT_new, 1)

            def gmlp(m):
                dve.wait_ge(s["sa_pe"], m + 1)
                past(dve, s["ya_ready"], m)
                dve.tensor_tensor(ya[:], heads[3], bs[:], ALU.add).then_inc(s["ya_bias"], 1)
                dve.wait_ge(s["ya_bias"], m + 1)
                dve.wait_ge(s["u_done"], m + 1)
                dve.tensor_tensor(ya[:], ya[:], u[:], ALU.mult).then_inc(s["ya_mul"], 1)

            def gmlp_out(m):
                dve.wait_ge(s["ra_ready"], m + 1)
                past(dve, s["y_stored"], 16 * m)
                for c in range(G_A):
                    last = dve.scalar_tensor_tensor(out=yT[:, c], in0=ya[:, c], scalar=sh["cols"][:, 8 + c:9 + c],
                                                    in1=r_q[:, c], op0=ALU.mult, op1=ALU.mult)
                last.then_inc(s["ya_ready"], 1)

            def state(m):
                if not sample:
                    dve.wait_ge(s["s_pe"], m + 1)
                    dve.wait_ge(s["o_pe"], m + 1)
                    dve.wait_ge(s["gates_ready"], m + 1)
                    for h_ in range(H_B):
                        last = dve.scalar_tensor_tensor(out=S[:, h_, 0], in0=S[:, h_, 0],
                                                        scalar=gates[:, 2 * H_B + h_:2 * H_B + h_ + 1],
                                                        in1=heads[3][:, h_], op0=ALU.mult, op1=ALU.add)
                    last.then_inc(s["s_ready"], 1)
                    return
                dve.wait_ge(s["delta_ready"], 1)
                for h_ in range(H_B):
                    if h_ > 0:
                        dve.wait_ge(sh_pe, h_)
                    dve.tensor_tensor(delta_of[:], delta[:, h_:h_ + 1].to_broadcast([P, B, P]),
                                      stream[:].rearrange("p (b a) -> p b a", a=1).to_broadcast([P, B, P]), ALU.mult)\
                       .then_inc(dm_ready, 1)
                    dve.wait_ge(sh_pe, h_ + 1)
                    dve.wait_ge(s["o_pe"], 1)
                    for b in range(B):
                        c = 3 * H_B + h_ * B + b
                        last = dve.scalar_tensor_tensor(out=S[:, h_, b], in0=S[:, h_, b], scalar=gates[:, c:c + 1],
                                                        in1=pr[b // 4][:, (b % 4) * P:(b % 4 + 1) * P],
                                                        op0=ALU.mult, op1=ALU.add)
                    last.then_inc(sh_ready, 1)

            def out(m, par):
                dve.wait_ge(s["ro_ready"], m + 1)
                dve.scalar_tensor_tensor(out=o_norm[:], in0=heads[2], scalar=sh["cols"][:, 12:13], in1=r_k[:],
                                         op0=ALU.mult, op1=ALU.mult).then_inc(s["o_norm_ready"], 1)
                dve.wait_ge(s["o_norm_ready"], m + 1)
                dve.wait_ge(s["z_done"], m + 1)
                dve.tensor_tensor(yT[:, G_A:], o_norm[:], z[:, par], ALU.mult).then_inc(s["y_ready"], 1)

            def tile(m, par, project, fronts):
                start(m, par)
                if project:
                    h_columns(m + 1)
                    gates_raw(m + 1, 1 - par)
                products(m)
                gmlp(m)
                n_taps = 3 * CONV_W
                for l in range(LV):
                    for i in (2 * l, 2 * l + 1):
                        if project and i < n_taps:
                            conv_tap(i // CONV_W, i % CONV_W, m + 1)
                    level(l, m)
                    if l == 3 or (LV < 4 and l == LV - 1):
                        gmlp_out(m)
                if project:
                    gates_spread(m + 1, 1 - par)
                state(m)
                out(m, par)
                if fronts:
                    front(m + 2)

            if sample:
                dve.wait_ge(s["rows_turned"], 1)
                dve.tensor_copy(sh["cols"][:], gb[1][:, 0:COLS]).then_inc(s["cols_ready"], 1)
                dve.wait_ge(s["a_exp"], 1)
                dve.tensor_scalar(sh["neg_a"][:], sh["neg_a"][:], -1.0, None, ALU.mult).then_inc(s["a_ready"], 1)
                dve.wait_ge(s["cin_turned"], 1)
                dve.tensor_copy(cin[:, :, :, 0:CONV_W - 1],
                                gb[2][:, 0:12 * B * (CONV_W - 1)].rearrange("p (c b r) -> p c b r", c=12, b=B))\
                   .then_inc(s["cin_ready"], 1)
                dve.wait_ge(s["set_loaded"], 16 * 8)
                dve.tensor_copy(bs[:].rearrange("p g (b r) -> p g b r", b=B),
                                bs_in[:, :, 0:C].rearrange("p g (a r) -> p g a r", a=1).to_broadcast([P, G_A, B, C]))\
                   .then_inc(s["bs_ready"], 1)
                dve.wait_ge(s["bs_ready"], 1)
                dve.wait_ge(s["cols_ready"], 1)
                dve.wait_ge(s["a_ready"], 1)
            dve.wait_ge(s["ws_turned"], 1)
            dve.tensor_copy(wsT[:], heads[0]).then_inc(s["ws_copied"], 1)
            dve.wait_ge(s["ws_copied"], 1)
            if sample:
                dve.engine_nop().then_inc(s["ws_ready"], 1)
            else:
                for lo in range(CHUNK, P, CHUNK):
                    last = dve.memset(wsT[lo:lo + CHUNK, :, 0:lo], 0.0)
                last.then_inc(s["ws_ready"], 1)
                dve.wait_ge(s["set_loaded"], 32)
            dve.wait_ge(s["set_masks"], 2 if sample else 1)
            front(0)
            if sample:
                h_columns(0)
                for j in range(3):
                    for i in range(CONV_W):
                        conv_tap(j, i, 0)
                dve.tensor_copy(tails[:].rearrange("p c (b r) -> p c b r", b=B), cin[:, :, :, C:]).then_inc(s["tail_ready"], 1)
                gates_raw(0, 0)
                gates_spread(0, 0)
                tile(0, 0, False, False)
            else:
                h_columns(0)
                gates_raw(0, 0)
                gates_spread(0, 0)
                for j in range(3):
                    for i in range(CONV_W):
                        conv_tap(j, i, 0)
                front(1)
                tile(0, 0, True, True)
                with dve.Fori(1, TILES - 3, 2) as m:
                    tile(m, 1, True, True)
                    tile(m + 1, 0, True, True)
                tile(TILES - 3, 1, True, True)
                tile(TILES - 2, 0, True, False)
                tile(TILES - 1, 1, False, False)
                for j in range(3):
                    dve.wait_ge(head_kept[j], TILES)
                dve.tensor_copy(tails[:], cin[:, :, 0, 0:CONV_W - 1]).then_inc(s["tail_ready"], 1)

        @block.tensor
        def _(pe):
            def turn_h(m):
                pe.wait_ge(s["h_ready"], m + 1)
                past(pe, s["z_done"], m)
                past(pe, s["u_done"], m)
                for k in range(KC):
                    last = pe.transpose(pr[k // 4][:, (k % 4) * P:(k % 4 + 1) * P], h[:, k * P:(k + 1) * P], sh["ident"][:])
                last.then_inc(s["h_turned"], 1)

            def gate_columns(m):
                pe.wait_ge(s["hT_ready"], m + 1)
                past(pe, s["gates_ready"], m)
                past(pe, s["eb_raw"], m)
                past(pe, s["xa_ready"], m)
                if sample:
                    pe.wait_ge(w_cut[CUT_OF["ba"]], 16)
                for k in range(KC):
                    last = pe.matmul(gs[:, 0:2 * H_B], hT[:, k], sh["w_in"][:, k, COL_BA:COL_BA + 2 * H_B],
                                     start=(k == 0), stop=(k == KC - 1))
                last.then_inc(s["ba_done"], 1)

            def columns(bank_, c, col):
                for k in range(KC):
                    last = pe.matmul(bank_[:, c * P:(c + 1) * P], sh["w_in"][:, k, col + c * P:col + (c + 1) * P], hT[:, k],
                                     start=(k == 0), stop=(k == KC - 1))
                return last

            def qkv_columns(j, c, m):
                if c == 0:
                    pe.wait_ge(s["hT_ready"] if j < 2 else raw[0], m + 1)
                    if sample:
                        pe.wait_ge(w_cut[CUT_OF["qkv"[j]]], 16)
                last = columns(pr[j % 2], c, COL_QKV + j * D_B)
                if c == 3:
                    last.then_inc(qkv_pe[j], 1)

            def va_columns(part, m):
                if part == 0:
                    pe.wait_ge(raw[1], m + 1)
                    if sample:
                        pe.wait_ge(w_cut[CUT_OF["va"]], 16)
                for k in (2 * part, 2 * part + 1):
                    last = pe.matmul(pr[1][:], hT[:, k], sh["w_in"][:, k, COL_VA:COL_VA + D_A],
                                     start=(k == 0), stop=(k == KC - 1))
                if part == 3:
                    last.then_inc(s["va_pe"], 1)

            def z_columns(c, m):
                if c == 0:
                    pe.wait_ge(raw[2], m + 1)
                    if sample:
                        pe.wait_ge(w_cut[CUT_OF["z"]], 16)
                last = columns(pr[0], c, COL_Z)
                if c == 3:
                    last.then_inc(s["z_pe"], 1)

            def u_columns(c, m):
                if c == 0:
                    pe.wait_ge(s["va_done"], m + 1)
                    if sample:
                        pe.wait_ge(w_cut[CUT_OF["u"]], 16)
                last = columns(pr[1], c, COL_U)
                if c == 3:
                    last.then_inc(s["u_pe"], 1)

            def start(m, par):
                flat = "p h i -> p (h i)"
                pe.wait_ge(s["g_upto_ready"], m + 1)
                past(pe, s["w_ready"], m)
                pe.matmul(gb[0][:], sh["after"][:], g_upto[:].rearrange(flat), start=True, stop=True).then_inc(s["decay_pe"], 1)
                past(pe, s["delta_ready"], m)
                pe.matmul(gb[1][:], sh["ones"][:], g_upto[:].rearrange(flat), start=True, stop=True).then_inc(s["eb_pe"], 1)
                past(pe, s["gates_ready"], m)
                pe.wait_ge(s["g_ready"], m + 1)
                for i, mask in enumerate((sh["upto"], sh["after"], sh["ones"])):
                    last = pe.matmul(gs[:, 16 + i * H_B:16 + (i + 1) * H_B], mask[:], g[:, par, :], start=True, stop=True)
                if sample:
                    pe.wait_ge(s["g_of_ready"], 1)
                    last = pe.matmul(gs[:, 16 + 3 * H_B:16 + 3 * H_B + H_B * B], sh["ones"][:],
                                     g_of[:].rearrange("p h b -> p (h b)"), start=True, stop=True)
                last.then_inc(s["small_pe"], 1)
                pe.wait_ge(sq_ready[1], m + 1)
                past(pe, s["s_ready"], m)
                pe.matmul(gb[3][:], sh["ones"][:], sq[1][:].rearrange(flat), start=True, stop=True).then_inc(s["ssk_pe"], 1)
                pe.wait_ge(s["beta_diag_ready"], m + 1)
                past(pe, s["ln_o"], m)
                pe.matmul(gb[4][:], sh["ones"][:], beta_diag[:].rearrange(flat), start=True, stop=True).then_inc(s["bb_pe"], 1)
                pe.wait_ge(sq_ready[0], m + 1)
                past(pe, s["o_norm_ready"], m)
                pe.matmul(gb[2][:], sh["ones"][:], sq[0][:].rearrange(flat), start=True, stop=True).then_inc(s["ssq_pe"], 1)

            def products(m):
                pe.wait_ge(silu[2], m + 1)
                pe.wait_ge(s["decay_exp"], m + 1)
                for h_ in range(H_B):
                    last = pe.transpose(heads[0][:, h_], act3[2][:, h_], sh["ident"][:])
                last.then_inc(s["v_turned"], 1)
                pe.wait_ge(s["kn_ready"], m + 1)
                pe.wait_ge(s["eb_ready"], m + 1)
                for h_ in range(H_B):
                    last = pe.transpose(heads[1][:, h_], kn[:, h_], sh["ident"][:])
                last.then_inc(s["k_turned"], 1)
                pe.wait_ge(s["kb_ready"], m + 1)
                pe.wait_ge(s["ln_q"], m + 1)
                for h_ in range(H_B):
                    last = pe.matmul(heads[2][:, h_], kn[:, h_], kb[:, h_], start=True, stop=True)
                last.then_inc(s["kk_pe"], 1)
                pe.wait_ge(s["qn_ready"], m + 1)
                pe.wait_ge(s["ln_k"], m + 1)
                for h_ in range(H_B):
                    last = pe.matmul(heads[3][:, h_], kn[:, h_], qn[:, h_], start=True, stop=True)
                last.then_inc(s["qk_pe"], 1)

            def turn_x(m):
                pe.wait_ge(s["xt_ready"], m + 1)
                pe.wait_ge(s["kb_ready"], m + 1)
                for h_ in range(H_B):
                    last = pe.transpose(heads[4][:, h_], XT[:, h_], sh["ident"][:])
                last.then_inc(s["x_turned"], 1)

            def level_lx(l, m):
                pe.wait_ge(lt_ready, levels(m, l))
                if l > 0:
                    pe.wait_ge(x_new, m * (LV - 1) + l)
                else:
                    pe.wait_ge(s["x_ready"], m + 1)
                    pe.wait_ge(s["v_beta_ready"], m + 1)
                for h_ in range(H_B):
                    last = pe.matmul(heads[0][:, h_], lt[:, l % 2, h_], X[:, h_], start=True, stop=True)
                last.then_inc(lx_pe, 1)

            def level_xlx(l, m):
                pe.wait_ge(lx_ready, levels(m, l))
                if l == 0:
                    pe.wait_ge(s["xt_ready"], m + 1)
                else:
                    pe.wait_ge(xT_new, levels(m, l - 1))
                if l < LV - 1:
                    if l == 0:
                        pe.wait_ge(s["k_dec_ready"], m + 1)
                    for h_ in range(H_B):
                        last = pe.matmul(heads[1][:, h_], XT[:, h_], LX[:, h_], start=True, stop=True)
                    last.then_inc(xlx_pe, 1)
                for h_ in range(H_B):
                    last = pe.matmul(heads[2][:, h_], LX[:, h_], XT[:, h_], start=True, stop=True)
                last.then_inc(xlxT_pe, 1)

            def gmlp(m):
                pe.wait_ge(s["va_done"], m + 1)
                pe.wait_ge(s["attn_ready"], m + 1)
                for c in range(G_A):
                    last = pe.matmul(heads[3][:, c], va[:, c * C_A:(c + 1) * C_A], wsT[:, c], start=True, stop=True)
                last.then_inc(s["sa_pe"], 1)

            def gmlp_norm(m):
                pe.wait_ge(s["sq_a"], m + 1)
                pe.wait_ge(s["x_ready"], m + 1)
                pe.matmul(gb[4][:], sh["ones"][:], sq_out[:].rearrange("p h i -> p (h i)"), start=True, stop=True)\
                  .then_inc(s["ssa_pe"], 1)

            def w(m):
                pe.wait_ge(xT_new, levels(m, LV - 1))
                pe.wait_ge(s["k_beta_ready"], m + 1)
                for h_ in range(H_B):
                    last = pe.matmul(heads[0][:, h_], k_beta[:, h_], XT[:, h_], start=True, stop=True)
                last.then_inc(s["w_pe"], 1)

            def scan(m):
                pe.wait_ge(s["w_ready"], m + 1)
                pe.wait_ge(s["v_beta_ready"], m + 1)
                pe.wait_ge(x_new, (m + 1) * (LV - 1))
                if not sample:
                    past(pe, s["s_ready"], m)
                    for h_ in range(H_B):
                        pe.matmul(heads[1][:, h_], XT[:, h_], v_beta[:, h_], start=True, stop=False)
                        last = pe.matmul(heads[1][:, h_], w_neg[:, h_], S[:, h_, 0], start=False, stop=True)
                    last.then_inc(s["delta_pe"], 1)
                    return
                pe.wait_ge(s["states_in"], 16 * H_B)
                for h_ in range(H_B):
                    pe.matmul(heads[1][:, h_], v_beta[:, h_], XT[:, h_], start=True, stop=True)
                    for b in range(B):
                        own = slice(b * C, (b + 1) * C)
                        last = pe.matmul(heads[1][:, h_, own], S[:, h_, b], w_neg[:, h_, own], start=False,
                                         stop=True, skip_group_check=True)
                last.then_inc(s["delta_pe"], 1)
                pe.wait_ge(s["deltaT_ready"], 1)
                for h_ in range(H_B):
                    last = pe.transpose(heads[0][:, h_], delta_T[:, h_], sh["ident"][:])
                last.then_inc(s["deltaT_pe"], 1)

            def outputs(m):
                pe.wait_ge(s["delta_ready"], m + 1)
                pe.wait_ge(s["q_dec_ready"], m + 1)
                pe.wait_ge(s["attn_ready"], m + 1)
                for h_ in range(H_B):
                    pe.matmul(heads[2][:, h_], delta[:, h_], attn[:, h_], start=True, stop=True)
                    for b in range(B):
                        own = slice(b * C, (b + 1) * C)
                        last = pe.matmul(heads[2][:, h_, own], S[:, h_, b], q_dec[:, h_, own], start=False,
                                         stop=True, skip_group_check=True)
                last.then_inc(s["o_pe"], 1)

            def state(m):
                pe.wait_ge(s["k_dec_ready"], m + 1)
                if not sample:
                    pe.wait_ge(s["ya_bias"], m + 1)
                    for h_ in range(H_B):
                        last = pe.matmul(heads[3][:, h_], k_dec[:, h_], delta[:, h_], start=True, stop=True)
                    last.then_inc(s["s_pe"], 1)
                    return
                pe.wait_ge(s["u_done"], 1)
                pe.wait_ge(s["z_done"], 1)
                for h_ in range(H_B):
                    pe.wait_ge(dm_ready, h_ + 1)
                    if h_ > 0:
                        pe.wait_ge(sh_ready, h_)
                    for i in range(2):
                        last = pe.matmul(pr[i][:], k_dec[:, h_],
                                         delta_of[:, 4 * i:4 * i + 4].rearrange("p b i -> p (b i)"), start=True, stop=True)
                    last.then_inc(sh_pe, 1)

            def out_norm(m):
                pe.wait_ge(s["sq_o_ready"], m + 1)
                pe.wait_ge(s["ln_a"], m + 1)
                pe.matmul(gb[4][:], sh["ones"][:], sq_out[:].rearrange("p h i -> p (h i)"), start=True, stop=True)\
                  .then_inc(s["sso_pe"], 1)

            def tile(m, par, project):
                start(m, par)
                if project:
                    turn_h(m + 1)
                    gate_columns(m + 1)
                    for c in range(4):
                        qkv_columns(0, c, m + 1)
                products(m)
                if project:
                    qkv_columns(1, 0, m + 1)
                    qkv_columns(1, 1, m + 1)
                turn_x(m)
                gmlp(m)
                if project:
                    qkv_columns(1, 2, m + 1)
                    qkv_columns(1, 3, m + 1)
                for l in range(LV):
                    level_lx(l, m)
                    if project:
                        between(2 * l, m + 1)
                    level_xlx(l, m)
                    if l == 1:
                        gmlp_norm(m)
                    if project:
                        between(2 * l + 1, m + 1)
                w(m)
                if project:
                    u_columns(0, m + 1)
                scan(m)
                if project:
                    u_columns(1, m + 1)
                outputs(m)
                state(m)
                if project:
                    u_columns(2, m + 1)
                out_norm(m)
                if project:
                    u_columns(3, m + 1)

            def between(i, m):
                if i < 4:
                    qkv_columns(2, i, m)
                elif i < 8:
                    va_columns(i - 4, m)
                else:
                    z_columns(i - 8, m)

            pe.wait_ge(s["set_masks"], 2 if sample else 1)
            pe.wait_ge(s["set_loaded"], 16 * (8 if sample else 2))
            if sample:
                pe.transpose(gb[1][:, 0:COLS], rows_in[:], sh["ident"][0:COLS, 0:COLS]).then_inc(s["rows_turned"], 1)
                n = B * (CONV_W - 1)
                for c in range(12):
                    last = pe.transpose(gb[2][:, c * n:(c + 1) * n], conv_in[:, c * P:(c + 1) * P], sh["ident"][0:n, 0:n])
                last.then_inc(s["cin_turned"], 1)
                pe.wait_ge(s["ws_loaded"], 16 * B)
            for c in range(G_A):
                last = pe.transpose(heads[0][:, c], ws_in[:, c], sh["ident"][:])
            last.then_inc(s["ws_turned"], 1)
            pe.wait_ge(s["ws_ready"], 1)
            if sample:
                pe.wait_ge(s["cols_ready"], 1)
                pe.wait_ge(s["cin_ready"], 1)
            turn_h(0)
            if not sample:
                gate_columns(0)
            for j in range(3):
                for c in range(4):
                    qkv_columns(j, c, 0)
            for part in range(4):
                va_columns(part, 0)
            for c in range(4):
                z_columns(c, 0)
            if sample:
                gate_columns(0)
            for c in range(4):
                u_columns(c, 0)
            if sample:
                tile(0, 0, False)
            else:
                tile(0, 0, True)
                with pe.Fori(1, TILES - 3, 2) as m:
                    tile(m, 1, True)
                    tile(m + 1, 0, True)
                tile(TILES - 3, 1, True)
                tile(TILES - 2, 0, True)
                tile(TILES - 1, 1, False)
            pe.wait_ge(s["tail_ready"], 1)
            pe.wait_ge(s["y_ready"], TILES)
            pe.wait_ge(sh_ready if sample else s["s_ready"], H_B if sample else TILES)
            for c in range(12):
                last = pe.transpose(gb[c // 4][0:B * (CONV_W - 1), (c % 4) * P:(c % 4 + 1) * P], tails[:, c], sh["ident"][:])
            last.then_inc(s["tail_turned"], 1)


def out_phase(nc, x_tiles, mixed, w_o, norm2_row, w_gate, w_up, w_down, final_norm, y_tiles):
    TILES = len(x_tiles)
    KC = D_MODEL // P
    FC = w_gate.shape[1] // P
    PER = 2
    BLOCKS = FC // PER
    GROUP = 6
    QUARTERS = 4
    QC = D_MODEL // QUARTERS
    USES = BLOCKS + QUARTERS // PER
    NH = D_MODEL // 512
    groups = [(g, min(GROUP, TILES - g)) for g in range(0, TILES, GROUP)]

    wg_dram = w_gate.rearrange("(c p) f -> p c f", p=P)
    wu_dram = w_up.rearrange("(c p) f -> p c f", p=P)
    wo_dram = w_o.rearrange("(c p) n -> p c n", p=P)
    wd_dram = w_down.rearrange("(c p) n -> p c n", p=P)

    with nc.cleanup_on_exit(), ExitStack() as ctx:
        def sb(name, shape, dt=F32):
            return ctx.enter_context(nc.sbuf_tensor(name, shape, dt))

        def sem(name):
            return nc.alloc_semaphore(name=name)

        acc = sb("acc", [P, GROUP, D_MODEL])
        h2 = sb("h2", [P, D_MODEL])
        squares = sb("squares_b", [P, D_MODEL])
        mraw = sb("mraw", [P, 2, KC, P])
        h2s = sb("h2s", [P, KC, P])
        h2_hi = sb("h2_hi", [P, KC, GROUP * P], F32R)
        h2_lo = sb("h2_lo", [P, KC, GROUP * P], F32R)
        wraw = sb("wraw", [P, PER, 2, KC, P])
        w_hi = sb("w_hi", [P, PER, 2, KC, P], F32R)
        w_lo = sb("w_lo", [P, PER, 2, KC, P], F32R)
        wdraw = sb("wdraw", [P, PER, D_MODEL])
        wd_hi = sb("wd_hi", [P, PER, D_MODEL], F32R)
        wd_lo = sb("wd_lo", [P, PER, D_MODEL], F32R)
        gate_act = sb("gate_act", [P, 2, GROUP * P // 2])
        act = sb("act", [P, 2, GROUP * P // 2])
        act_hi = sb("act_hi", [P, PER, GROUP * P], F32R)
        act_lo = sb("act_lo", [P, PER, GROUP * P], F32R)
        norm2_in = sb("norm2_in", [KC, P])
        norm2 = sb("norm2", [P, KC])
        fnorm = sb("fnorm", [P, D_MODEL])
        ident = sb("ident_b", [P, P])
        eps = sb("eps_b", [P, 1])
        ssum = sb("ssum", [P, 1])
        lnv = sb("lnv", [P, 1])
        rstd = sb("rstd", [P, 1])
        fssum = sb("fssum", [P, 1])
        flnv = sb("flnv", [P, 1])
        frstd = sb("frstd", [P, 1])

        gate_ps = [ctx.enter_context(nc.psum_tensor(f"gate_ps{i}", [P, 512], F32)) for i in range(2)]
        up_ps = [ctx.enter_context(nc.psum_tensor(f"up_ps{i}", [P, 512], F32)) for i in range(2)]
        down_ps = [ctx.enter_context(nc.psum_tensor(f"down_ps{i}", [P, NH, 512], F32)) for i in range(2)]

        setup_loaded = sem("setup_loaded_b")
        zeroed = sem("zeroed_b")
        ident_ready = sem("ident_ready_b")
        norm2_turned = sem("norm2_turned")
        norm2_ready = sem("norm2_ready")
        x_loaded = [sem(f"x_loaded_b{t}") for t in range(GROUP)]
        m_loaded = [sem(f"m_loaded{i}") for i in range(2)]
        m_hi_ready = sem("m_hi_ready")
        m_lo_ready = sem("m_lo_ready")
        wo_pe = sem("wo_pe")
        wo_added = sem("wo_added")
        squared = sem("squared_b")
        ln_done = sem("ln_done_b")
        rstd_ready = sem("rstd_ready_b")
        h2_ready = sem("h2_ready")
        h2_turned = sem("h2_turned")
        h2s_ready = sem("h2s_ready")
        h2_hi_ready = sem("h2_hi_ready")
        h2_lo_ready = sem("h2_lo_ready")
        w_loaded = [sem(f"w_loaded{c}") for c in range(PER)]
        w_hi_ready = [sem(f"w_hi_ready{c}") for c in range(PER)]
        w_lo_ready = [sem(f"w_lo_ready{c}") for c in range(PER)]
        wd_loaded = sem("wd_loaded")
        wd_hi_ready = sem("wd_hi_ready")
        wd_lo_ready = sem("wd_lo_ready")
        gate_done = [[sem(f"gate_done{c}{h}") for h in range(2)] for c in range(PER)]
        up_done = [[sem(f"up_done{c}{h}") for h in range(2)] for c in range(PER)]
        silu_done = [[sem(f"silu_done{c}{h}") for h in range(2)] for c in range(PER)]
        act_ready = [[sem(f"act_ready{c}{h}") for h in range(2)] for c in range(PER)]
        act_hi_ready = [[sem(f"act_hi_ready{c}{h}") for h in range(2)] for c in range(PER)]
        act_lo_ready = [[sem(f"act_lo_ready{c}{h}") for h in range(2)] for c in range(PER)]
        down_done = [sem(f"down_done{t}") for t in range(GROUP)]
        added = [sem(f"added{t}") for t in range(GROUP)]
        fsquared = sem("fsquared")
        fln_done = sem("fln_done")
        frstd_ready = sem("frstd_ready")
        scaled = sem("scaled")
        y_ready = sem("y_ready")
        y_stored = [sem(f"y_stored{t}") for t in range(GROUP)]

        def blocks_of(t, gi):
            return BLOCKS * sum(1 for _, n in groups[:gi] if t < n)

        def last_in(t, n):
            return n - 1 - (n - 1 - t) % 2

        def uses(m, gi):
            return m + (gi + 1) * (USES - BLOCKS)

        block = ctx.enter_context(nc.Block())

        @block.sync
        def _(sp):
            def load_quarter(q, m):
                c = q % PER
                sp.wait_ge(w_lo_ready[c], m) if m > 0 else None
                for a in range(2):
                    half_k = slice(a * KC // 2, (a + 1) * KC // 2)
                    sp.dma_start(wraw[:, c, a].rearrange("p k i -> p (k i)").rearrange("p (k i) -> p k i", k=KC // 2),
                                 wo_dram[:, half_k, q * QC:(q + 1) * QC]).then_inc(w_loaded[c], 16)

            def load_block(b, gi):
                m = b + gi * BLOCKS
                for c in range(PER):
                    sp.wait_ge(w_lo_ready[c], uses(m, gi))
                    cols = bass.ds((b * PER + c) * P, P)
                    sp.dma_start(wraw[:, c, 0], wg_dram[:, :, cols]).then_inc(w_loaded[c], 16)
                    sp.dma_start(wraw[:, c, 1], wu_dram[:, :, cols]).then_inc(w_loaded[c], 16)
                if not (isinstance(m, int) and m == 0):
                    sp.wait_ge(wd_lo_ready, m)
                sp.dma_start(wdraw[:], wd_dram[:, bass.ds(b * PER, PER), :]).then_inc(wd_loaded, 16)

            def load_mixed(k):
                if k >= 2:
                    sp.wait_ge(m_lo_ready, k - 1)
                sp.dma_start(mraw[:, k % 2].rearrange("p k i -> p (k i)"), mixed[k]).then_inc(m_loaded[k % 2], 16)

            sp.dma_start(norm2_in[:], norm2_row.rearrange("(c p) -> c p", p=P)).then_inc(setup_loaded, 16)
            sp.dma_start(fnorm[:], final_norm.rearrange("(a n) -> a n", a=1).to_broadcast([P, D_MODEL]))\
              .then_inc(setup_loaded, 16)
            for gi, (g, n) in enumerate(groups):
                if gi == 0:
                    load_quarter(0, 0)
                    load_mixed(0)
                    load_mixed(1)
                    load_quarter(1, 0)
                    for t in range(n):
                        sp.dma_start(acc[:, t, :], x_tiles[t]).then_inc(x_loaded[t], 16)
                for t in range(2, n):
                    load_mixed(g + t)
                for q in range(2, QUARTERS):
                    load_quarter(q, gi * USES + q // PER)
                load_block(0, gi)
                with sp.Fori(1, BLOCKS) as b:
                    load_block(b, gi)
                if gi + 1 < len(groups):
                    for q in range(2):
                        load_quarter(q, (gi + 1) * USES)
                    load_mixed(g + n)
                    load_mixed(g + n + 1)
                for t in range(n):
                    sp.wait_ge(y_ready, g + t + 1)
                    sp.dma_start(y_tiles[g + t], acc[:, t, :]).then_inc(y_stored[t], 16)
                if gi + 1 < len(groups):
                    for t in range(groups[gi + 1][1]):
                        sp.wait_ge(y_stored[t], 16 * (gi + 1))
                        sp.dma_start(acc[:, t, :], x_tiles[g + n + t]).then_inc(x_loaded[t], 16)
            for t in range(GROUP):
                sp.wait_ge(y_stored[t], 16 * sum(1 for _, n in groups if t < n))

        @block.gpsimd
        def _(pool):
            pool.memset(eps[:], EPS).then_inc(zeroed, 1)
            pool.memset(ident[:], 0.0).then_inc(zeroed, 1)
            pool.wait_ge(zeroed, 2)
            pool.affine_select(out=ident[:], in_=ident[:], compare_op=ALU.not_equal, fill=1.0, base=0,
                               pattern=[[-1, P]], channel_multiplier=1).then_inc(ident_ready, 1)

        @block.scalar
        def _(act_e):
            def split_columns(c, m, used=None, count=0):
                act_e.wait_ge(w_loaded[c], (m + 1) * 32)
                if used is not None:
                    act_e.wait_ge(used, count)
                act_e.activation(w_hi[:, c], wraw[:, c], ACT.Copy).then_inc(w_hi_ready[c], 1)

            def split_rows(m):
                act_e.wait_ge(wd_loaded, (m + 1) * 16)
                act_e.activation(wd_hi[:], wdraw[:], ACT.Copy).then_inc(wd_hi_ready, 1)

            def hidden(c, h, m, half):
                act_e.wait_ge(gate_done[c][h], m + 1)
                act_e.activation(gate_act[:, h, 0:half], gate_ps[h][:, 0:half], ACT.Silu)\
                     .then_inc(silu_done[c][h], 1)
                act_e.wait_ge(act_ready[c][h], m + 1)
                act_e.activation(act_hi[:, c, h * half:(h + 1) * half], act[:, h, 0:half], ACT.Copy)\
                     .then_inc(act_hi_ready[c][h], 1)

            def split_mixed(gi, g, t):
                k = g + t
                act_e.wait_ge(m_loaded[k % 2], 16 * (k // 2 + 1))
                if gi > 0 and t == 0:
                    act_e.wait_ge(up_done[PER - 1][1], gi * BLOCKS)
                act_e.activation(h2_hi[:, :, t * P:(t + 1) * P], mraw[:, k % 2], ACT.Copy).then_inc(m_hi_ready, 1)

            act_e.wait_ge(zeroed, 1)
            for gi, (g, n) in enumerate(groups):
                half = n * P // 2
                if gi == 0:
                    split_columns(0, 0)
                split_mixed(gi, g, 0)
                if gi == 0:
                    split_columns(1, 0)
                for t in range(1, n):
                    split_mixed(gi, g, t)
                for q in range(3):
                    split_columns(q % PER, gi * USES + 1 + q // PER, wo_pe, QUARTERS * g + (q + 1) * n)
                for t in range(n):
                    act_e.wait_ge(wo_added, QUARTERS * g + (QUARTERS - 1) * n + t + 1)
                    act_e.activation(squares[:], acc[:, t, :], ACT.Square, accum_out=ssum[:]).then_inc(squared, 1)
                    act_e.wait_ge(squared, g + t + 1)
                    act_e.activation(lnv[:], ssum[:], ACT.Ln, bias=eps[:], scale=1.0 / D_MODEL).then_inc(ln_done, 1)
                    act_e.wait_ge(ln_done, g + t + 1)
                    if g + t > 0:
                        act_e.wait_ge(h2_ready, g + t)
                    act_e.activation(rstd[:], lnv[:], ACT.Exp, scale=-0.5).then_inc(rstd_ready, 1)
                    act_e.wait_ge(h2s_ready, g + t + 1)
                    act_e.activation(h2_hi[:, :, t * P:(t + 1) * P], h2s[:], ACT.Copy).then_inc(h2_hi_ready, 1)
                    if t == 1:
                        split_columns(1, gi * USES + 2, wo_pe, QUARTERS * (g + n))
                        if gi > 0:
                            last_tile = groups[gi - 1][1] - 1
                            act_e.wait_ge(down_done[last_tile], blocks_of(last_tile, gi))
                        split_rows(gi * BLOCKS)

                def block_of(b, ahead):
                    m = b + gi * BLOCKS
                    hidden(0, 0, m, half)
                    hidden(0, 1, m, half)
                    if ahead:
                        split_columns(0, uses(m, gi) + 1, up_done[0][1], m + 1)
                    hidden(1, 0, m, half)
                    hidden(1, 1, m, half)
                    if ahead:
                        split_columns(1, uses(m, gi) + 1, up_done[1][1], m + 1)
                        if not (isinstance(b, int) and b == BLOCKS - 1):
                            act_e.wait_ge(down_done[n - 1], b + blocks_of(n - 1, gi) + 1)
                            split_rows(m + 1)

                block_of(0, True)
                with act_e.Fori(1, BLOCKS - 1) as b:
                    block_of(b, True)
                block_of(BLOCKS - 1, gi + 1 < len(groups))
                for t in range(n):
                    act_e.wait_ge(added[t], blocks_of(t, gi + 1))
                    act_e.activation(squares[:], acc[:, t, :], ACT.Square, accum_out=fssum[:]).then_inc(fsquared, 1)
                    act_e.wait_ge(fsquared, g + t + 1)
                    act_e.activation(flnv[:], fssum[:], ACT.Ln, bias=eps[:], scale=1.0 / D_MODEL).then_inc(fln_done, 1)
                    act_e.wait_ge(fln_done, g + t + 1)
                    if g + t > 0:
                        act_e.wait_ge(y_ready, g + t)
                    act_e.activation(frstd[:], flnv[:], ACT.Exp, scale=-0.5).then_inc(frstd_ready, 1)

        @block.vector
        def _(dve):
            def split_columns(c, m):
                dve.wait_ge(w_hi_ready[c], m + 1)
                dve.tensor_tensor(w_lo[:, c], wraw[:, c], w_hi[:, c].bitcast(F32), ALU.subtract)\
                   .then_inc(w_lo_ready[c], 1)

            def split_rows(m):
                dve.wait_ge(wd_hi_ready, m + 1)
                dve.tensor_tensor(wd_lo[:], wdraw[:], wd_hi[:].bitcast(F32), ALU.subtract).then_inc(wd_lo_ready, 1)

            def hidden(c, h, m, half):
                dve.wait_ge(silu_done[c][h], m + 1)
                dve.wait_ge(up_done[c][h], m + 1)
                dve.tensor_tensor(act[:, h, 0:half], up_ps[h][:, 0:half], gate_act[:, h, 0:half], ALU.mult)\
                   .then_inc(act_ready[c][h], 1)
                dve.wait_ge(act_hi_ready[c][h], m + 1)
                dve.wait_ge(act_ready[c][h], m + 1)
                dve.tensor_tensor(act_lo[:, c, h * half:(h + 1) * half], act[:, h, 0:half],
                                  act_hi[:, c, h * half:(h + 1) * half].bitcast(F32), ALU.subtract)\
                   .then_inc(act_lo_ready[c][h], 1)

            def add_tile(t, m):
                dve.wait_ge(down_done[t], m + 1)
                if not (isinstance(m, int) and m == 0):
                    dve.wait_ge(added[t], m)
                dve.tensor_tensor(acc[:, t, :], down_ps[t % 2][:].rearrange("p a b -> p (a b)"), acc[:, t, :],
                                  ALU.add).then_inc(added[t], 1)

            def block_of(b, gi, n, ahead):
                m = b + gi * BLOCKS
                half = n * P // 2
                hidden(0, 0, m, half)
                hidden(0, 1, m, half)
                if ahead:
                    split_columns(0, uses(m, gi) + 1)
                hidden(1, 0, m, half)
                hidden(1, 1, m, half)
                for t in range(n):
                    add_tile(t, b + blocks_of(t, gi))
                    if t == 1 and ahead:
                        split_columns(1, uses(m, gi) + 1)
                if not (isinstance(b, int) and b == BLOCKS - 1):
                    split_rows(m + 1)

            def split_mixed(g, t):
                dve.wait_ge(m_hi_ready, g + t + 1)
                dve.tensor_tensor(h2_lo[:, :, t * P:(t + 1) * P], mraw[:, (g + t) % 2],
                                  h2_hi[:, :, t * P:(t + 1) * P].bitcast(F32), ALU.subtract).then_inc(m_lo_ready, 1)

            def add_quarter(q, gi, g, n):
                for t in range(n):
                    if q == 0:
                        dve.wait_ge(x_loaded[t], 16 * (gi + 1))
                    i = q * n + t
                    dve.wait_ge(wo_pe, QUARTERS * g + i + 1)
                    part = acc[:, t, q * QC:(q + 1) * QC]
                    dve.tensor_tensor(part, down_ps[i % 2][:, 0, 0:QC], part, ALU.add).then_inc(wo_added, 1)

            dve.wait_ge(norm2_turned, 1)
            dve.tensor_copy(norm2[:], down_ps[0][:, 0, 0:KC]).then_inc(norm2_ready, 1)
            dve.wait_ge(norm2_ready, 1)
            dve.wait_ge(setup_loaded, 32)
            for gi, (g, n) in enumerate(groups):
                if gi == 0:
                    split_columns(0, 0)
                split_mixed(g, 0)
                if gi == 0:
                    split_columns(1, 0)
                for t in range(1, n):
                    split_mixed(g, t)
                add_quarter(0, gi, g, n)
                split_columns(0, gi * USES + 1)
                add_quarter(1, gi, g, n)
                split_columns(1, gi * USES + 1)
                add_quarter(2, gi, g, n)
                split_columns(0, gi * USES + 2)
                add_quarter(3, gi, g, n)
                for t in range(n):
                    dve.wait_ge(rstd_ready, g + t + 1)
                    if g + t > 0:
                        dve.wait_ge(h2_turned, g + t)
                    dve.tensor_scalar(h2[:], acc[:, t, :], rstd[:, 0:1], None, ALU.mult).then_inc(h2_ready, 1)
                    dve.wait_ge(h2_turned, g + t + 1)
                    dve.tensor_tensor(h2s[:], down_ps[t % 2][:].rearrange("p a (b c) -> p (a b) c", c=P),
                                      norm2[:].rearrange("p (c a) -> p c a", a=1).to_broadcast([P, KC, P]),
                                      ALU.mult).then_inc(h2s_ready, 1)
                    dve.wait_ge(h2s_ready, g + t + 1)
                    dve.wait_ge(h2_hi_ready, g + t + 1)
                    dve.tensor_tensor(h2_lo[:, :, t * P:(t + 1) * P], h2s[:],
                                      h2_hi[:, :, t * P:(t + 1) * P].bitcast(F32), ALU.subtract)\
                       .then_inc(h2_lo_ready, 1)
                    if t == 1:
                        split_columns(1, gi * USES + 2)
                        split_rows(gi * BLOCKS)
                block_of(0, gi, n, True)
                with dve.Fori(1, BLOCKS - 1) as b:
                    block_of(b, gi, n, True)
                block_of(BLOCKS - 1, gi, n, gi + 1 < len(groups))
                for t in range(n):
                    dve.wait_ge(frstd_ready, g + t + 1)
                    dve.scalar_tensor_tensor(out=acc[:, t, :], in0=acc[:, t, :], scalar=frstd[:, 0:1], in1=fnorm[:],
                                             op0=ALU.mult, op1=ALU.mult).then_inc(y_ready, 1)

        @block.tensor
        def _(pe):
            def three(out, w_h, w_l, x_h, x_l, start, stop):
                pe.matmul(out, w_h, x_h, start=start, stop=False)
                pe.matmul(out, w_h, x_l, start=False, stop=False)
                return pe.matmul(out, w_l, x_h, start=False, stop=stop)

            def past(semaphore, count):
                if not (isinstance(count, int) and count == 0):
                    pe.wait_ge(semaphore, count)

            def hidden(c, h, m, half):
                cols = slice(h * half, (h + 1) * half)
                before = (PER - 1, m) if c == 0 else (c - 1, m + 1)
                past(silu_done[before[0]][h], before[1])
                for k in range(KC):
                    last = three(gate_ps[h][:, 0:half], w_hi[:, c, 0, k], w_lo[:, c, 0, k],
                                 h2_hi[:, k, cols], h2_lo[:, k, cols], k == 0, k == KC - 1)
                last.then_inc(gate_done[c][h], 1)
                past(act_ready[before[0]][h], before[1])
                for k in range(KC):
                    last = three(up_ps[h][:, 0:half], w_hi[:, c, 1, k], w_lo[:, c, 1, k],
                                 h2_hi[:, k, cols], h2_lo[:, k, cols], k == 0, k == KC - 1)
                last.then_inc(up_done[c][h], 1)

            def down(t, b, gi, n, m):
                half = n * P // 2
                if t >= 2:
                    pe.wait_ge(added[t - 2], b + blocks_of(t - 2, gi) + 1)
                else:
                    past(added[last_in(t, n)], b + blocks_of(last_in(t, n), gi))
                for c in range(PER):
                    for h in range(2):
                        if h * half < (t + 1) * P and (h + 1) * half > t * P:
                            pe.wait_ge(act_lo_ready[c][h], m + 1)
                for a in range(NH):
                    for c in range(PER):
                        last = three(down_ps[t % 2][:, a, :], act_hi[:, c, t * P:(t + 1) * P],
                                     act_lo[:, c, t * P:(t + 1) * P], wd_hi[:, c, a * 512:(a + 1) * 512],
                                     wd_lo[:, c, a * 512:(a + 1) * 512], c == 0, c == PER - 1)
                last.then_inc(down_done[t], 1)

            def block_of(b, gi, n):
                m = b + gi * BLOCKS
                half = n * P // 2
                for c in range(PER):
                    pe.wait_ge(w_lo_ready[c], uses(m, gi) + 1)
                    for h in range(2):
                        hidden(c, h, m, half)
                pe.wait_ge(wd_lo_ready, m + 1)
                for t in range(n):
                    down(t, b, gi, n, m)

            pe.wait_ge(ident_ready, 1)
            pe.wait_ge(setup_loaded, 32)
            pe.transpose(down_ps[0][:, 0, 0:KC], norm2_in[:], ident[0:KC, 0:KC]).then_inc(norm2_turned, 1)
            pe.wait_ge(norm2_ready, 1)
            for gi, (g, n) in enumerate(groups):
                for q in range(QUARTERS):
                    c = q % PER
                    quarter = [w[:, c].rearrange("p a k i -> p (a k i)").rearrange("p (k i) -> p k i", k=KC)
                               for w in (w_hi, w_lo)]
                    pe.wait_ge(w_lo_ready[c], gi * USES + q // PER + 1)
                    for t in range(n):
                        i = q * n + t
                        if i >= 2:
                            pe.wait_ge(wo_added, QUARTERS * g + i - 1)
                        elif gi > 0:
                            before = last_in(i, groups[gi - 1][1])
                            pe.wait_ge(added[before], blocks_of(before, gi))
                        if q == 0:
                            pe.wait_ge(m_lo_ready, g + t + 1)
                        own = slice(t * P, (t + 1) * P)
                        for k in range(KC):
                            last = three(down_ps[i % 2][:, 0, 0:QC], h2_hi[:, k, own], h2_lo[:, k, own],
                                         quarter[0][:, k], quarter[1][:, k], k == 0, k == KC - 1)
                        last.then_inc(wo_pe, 1)
                for t in range(n):
                    pe.wait_ge(h2_ready, g + t + 1)
                    if t >= 2:
                        pe.wait_ge(h2s_ready, g + t - 1)
                    else:
                        pe.wait_ge(wo_added, QUARTERS * (g + n))
                    for k in range(KC):
                        last = pe.transpose(down_ps[t % 2][:, k // 4, (k % 4) * P:(k % 4 + 1) * P],
                                            h2[:, k * P:(k + 1) * P], ident[:])
                    last.then_inc(h2_turned, 1)
                pe.wait_ge(h2_lo_ready, g + n)
                block_of(0, gi, n)
                with pe.Fori(1, BLOCKS) as b:
                    block_of(b, gi, n)


def stream_step(nc, t, outs, scratch):
    y_prompt, y_sample, gdn_prompt, conv_prompt, gdn_sample, conv_sample, v_sample = outs
    x_prompt = t["x_prompt"][0].rearrange("(a p) n -> a p n", p=P)
    x_sample = t["x_sample"].rearrange("b t n -> (b t) n").rearrange("(a p) n -> a p n", p=P)
    n_prompt = x_prompt.shape[0]
    weights = {k: t[k][0] for k in ("w_in", "conv_w", "a_log", "dt_bias", "gdn_norm", "gmlp_ws", "gmlp_bs",
                                    "gmlp_norm", "norm1")}
    with ExitStack() as ctx:
        shared = mix_setup(nc, ctx, weights["w_in"])
        mix_phase(nc, shared, dict(
            x=x_sample, y=scratch[n_prompt:], new_gdn=gdn_sample[0], new_conv=conv_sample[0].rearrange("b r n -> (b r) n"),
            new_v=v_sample[0].rearrange("b t n -> (b t) n"), state_gdn=t["state_gdn"][0],
            state_conv=t["state_conv"][0], **weights), True)
        mix_phase(nc, shared, dict(
            x=x_prompt, y=scratch[0:n_prompt], new_gdn=gdn_prompt[0, 0], new_conv=conv_prompt[0, 0], **weights), False)
    y_p = y_prompt[0].rearrange("(a p) n -> a p n", p=P)
    out_phase(nc, [x_prompt[i] for i in range(n_prompt)] + [x_sample[0]], scratch, t["w_o"][0], t["norm2"][0],
              t["w_gate"][0], t["w_up"][0], t["w_down"][0], t["final_norm"],
              [y_p[i] for i in range(n_prompt)] + [y_sample.rearrange("b t n -> (b t) n")])


def kernel(**inputs):
    import concourse.bacc as bacc
    import numpy as np
    from concourse.bass_utils import run_bass_kernel_spmd

    nc = bacc.Bacc("TRN2", target_bir_lowering=False, num_devices=1)
    arrays, tensors = {}, {}
    for name, value in inputs.items():
        arrays["in_" + name] = np.ascontiguousarray(value)
        tensors[name] = nc.dram_tensor("in_" + name, value.shape, F32, kind="ExternalInput").ap()
    shapes = [inputs["x_prompt"].shape, inputs["x_sample"].shape, (1, 1, H_B, DK, DV), (1, 1, CONV_W - 1, 3 * D_B),
              (1, DEC_BATCH, H_B, DK, DV), (1, DEC_BATCH, CONV_W - 1, 3 * D_B), (1, DEC_BATCH, DEC_SEQ, D_A)]
    outs = [nc.dram_tensor(f"out_{i}", shape, F32, kind="ExternalOutput").ap() for i, shape in enumerate(shapes)]
    tiles = SEQ // P + DEC_BATCH * DEC_SEQ // P
    scratch = nc.dram_tensor("mixed_tiles", (tiles, P, D_MODEL), F32, kind="Internal").ap()
    stream_step(nc, tensors, outs, scratch)
    result = run_bass_kernel_spmd(nc, [arrays], core_ids=[0]).results[0]
    return tuple(result[f"out_{i}"] for i in range(len(shapes)))
```

```python
import math
from contextlib import ExitStack

import concourse.bass as bass
from concourse import mybir

P = 128
D_MODEL = 1024
SEQ = 2048
DEC_BATCH, DEC_SEQ = 8, 16
CHUNK = 64
D_A = 512
G_A = 4
C_A = D_A // G_A
H_B = 4
DK = DV = 128
D_B = H_B * DV
CONV_W = 4
EPS = 1e-6
LEVELS = 7
LEVELS_OF = {P: 6, DEC_SEQ: 3}
COLS = 8 + G_A + 1 + CONV_W * 12
CUTS = [(2 * D_A, 2 * D_A + D_B), (2 * D_A + D_B, 2 * D_A + 2 * D_B), (2 * D_A + 2 * D_B, 2 * D_A + 3 * D_B),
        (D_A, 2 * D_A), (2 * D_A + 3 * D_B, 2 * D_A + 4 * D_B + 2 * H_B), (0, D_A)]
CUT_OF = {"q": 0, "k": 1, "v": 2, "va": 3, "z": 4, "ba": 4, "u": 5}

ALU = mybir.AluOpType
ACT = mybir.ActivationFunctionType
F32 = mybir.dt.float32
F32R = mybir.dt.float32r


def mix_setup(nc, ctx, w_in):
    def sb(name, shape, dt=F32):
        return ctx.enter_context(nc.sbuf_tensor(name, shape, dt))

    KC = D_MODEL // P
    return dict(
        w_in=sb("w_in_sb", [P, KC, w_in.shape[1]]),
        ident=sb("ident", [P, P]),
        ones=sb("ones", [P, P]),
        upto=sb("upto", [P, P]),
        after=sb("after", [P, P]),
        link=sb("link", [P, LEVELS, P]),
        cols=sb("cols", [P, COLS]),
        dt_bias=sb("dt_bias_sb", [P, H_B]),
        neg_a=sb("neg_a", [P, H_B]),
        eps=sb("eps", [P, 1]),
        ln_scale=sb("ln_scale", [P, 1]),
    )


def mix_phase(nc, sh, a, sample):
    TILES = 1 if sample else a["x"].shape[0]
    KC = D_MODEL // P
    C = DEC_SEQ if sample else P
    B = P // C
    LV = LEVELS_OF[C]
    COL_U, COL_VA, COL_QKV, COL_Z, COL_BA = 0, D_A, 2 * D_A, 2 * D_A + 3 * D_B, 2 * D_A + 4 * D_B
    W = H_B * P
    tag = "_s" if sample else "_p"

    with nc.cleanup_on_exit(), ExitStack() as ctx:
        def sb(name, shape, dt=F32):
            return ctx.enter_context(nc.sbuf_tensor(name + tag, shape, dt))

        def sem(name):
            return nc.alloc_semaphore(name=name + tag)

        CIN = 12 * B * (CONV_W - 1 + C)
        xf = sb("xf", [P, D_MODEL])
        early = sb("early", [P, max(CIN + 4 * P + D_MODEL, H_B * B * P if sample else 0)])
        cin = early[:, 0:CIN].rearrange("p (c b r) -> p c b r", c=12, b=B)
        conv = early[:, CIN:CIN + 4 * P].rearrange("p (c i) -> p c i", c=4)
        h = early[:, CIN + 4 * P:CIN + 4 * P + D_MODEL]
        if sample:
            S = early[:, 0:H_B * B * P].rearrange("p (h b v) -> p h b v", h=H_B, b=B)
        else:
            S = sb("S", [P, H_B, B, P])[:]
        hT = sb("hT", [P, 1 if sample else 2, KC, P])
        tails = sb("tails", [P, 12, B * (CONV_W - 1)])
        act3 = [sb(f"silu_{x}", [P, H_B, P]) for x in "qkv"]
        sq = [sb(f"sq_{x}", [P, H_B, P]) for x in "qk"]
        z = sb("z", [P, 1 if sample else 2, H_B, P])
        u = sb("u", [P, G_A, P])
        va = sb("va", [P, D_A])
        small = sb("small", [P, 8, H_B])
        g = sb("g", [P, 2, H_B])
        beta = sb("beta", [P, 2, H_B])
        g_upto = sb("g_upto", [P, H_B, P])
        beta_diag = sb("beta_diag", [P, H_B, P])
        g_of = sb("g_of", [P, H_B, B]) if sample else None
        decay = sb("decay", [P, H_B, P])
        eb = sb("eb", [P, H_B, P])
        gates = sb("gates", [P, 3 * H_B + (H_B * B if sample else 0)])
        beta_eb = sb("beta_eb", [P, H_B])
        r_k = sb("r_k", [P, H_B, P])
        r_q = sb("r_q", [P, H_B, P])
        knbq = sb("knbq", [P, 3, H_B, P])
        kn, kb, qn = knbq[:, 0], knbq[:, 1], knbq[:, 2]
        tail_rows = knbq[0:B * (CONV_W - 1)].rearrange("p a h i -> p (a h i)")
        q_dec = sb("q_dec", [P, H_B, P])
        v_beta = sb("v_beta", [P, H_B, P])
        k_beta = sb("k_beta", [P, H_B, P])
        k_dec = sb("k_dec", [P, H_B, P])
        mt = sb("mt", [P, H_B, P])
        attn = sb("attn", [P, H_B, P])
        lt = sb("lt", [P, 2, H_B, P])
        X = sb("X", [P, H_B, P])
        XT = sb("XT", [P, H_B, P])
        LX = [sb(f"LX{l}", [P, H_B, P]) for l in range(LV)]
        w_neg = mt
        delta = XT
        ya = sb("ya", [P, G_A, P])
        sq_gmlp = sq[1]
        sq_o = X
        o_norm = eb
        yT = xf[:].rearrange("p (c i) -> p c i", c=KC) if sample else sb("yT", [P, KC, P])[:]
        ssum = sb("ssum_m", [P, 1])
        rstd = sb("rstd_m", [P, 1])
        ws_in = sq[0]
        wsT = sb("wsT", [P, G_A, P])
        bs = sb("bs", [P, G_A, P])
        if sample:
            rows_in = sb("rows_in", [COLS, P])
            a_log = sb("a_log", [P, H_B])
            conv_in = tail_rows
            stream = sb("stream", [P, B])
            same = sb("same", [P, P])
            delta_T = kb
            delta_of = hT[:, 0]
            bs_in = act3[2]

        def bank(name):
            return ctx.enter_context(nc.psum_tensor(name + tag, [P, 512], F32))

        pr = [bank("pr0"), bank("pr1")]
        gb = [bank(f"gb{i}") for i in range(5)]
        gs = bank("gs")
        heads = [x[:].rearrange("p (h i) -> p h i", h=H_B) for x in gb]

        names = """set_loaded set_masks rows_turned cols_ready a_exp a_ready ws_turned ws_copied ws_ready bs_ready
            cin_turned cin_ready ws_loaded states_in x_loaded squared ln_x rstd_ready h_ready h_turned hT_ready
            ba_done xa_ready eb_raw nax_ready ex_ready lnx_ready sp_ready g_ready b1_ready beta_ready
            g_upto_ready beta_diag_ready g_of_ready
            va_pe z_pe u_pe va_done z_done u_done
            decay_pe eb_pe small_pe ssk_pe ssq_pe bb_pe gates_ready decay_exp decay_ready eb_ready
            ln_k rk_ready ln_q rq_ready kn_ready kb_ready qn_ready q_dec_ready beta_eb_ready
            v_turned k_turned kk_pe qk_pe v_beta_ready k_beta_ready k_dec_ready mt_ready attn_ready
            xt_neg xt_ready x_turned x_ready
            sa_pe ya_bias ya_mul sq_a ssa_pe ln_a ra_ready ya_ready
            w_pe w_ready delta_pe delta_ready deltaT_pe deltaT_ready o_pe sq_o_ready sso_pe ln_o ro_ready
            o_norm_ready y_ready s_pe s_ready y_stored va_stored s_stored
            tail_ready tail_turned rows_ready rows_stored""".split()
        s = {x: sem(x) for x in names}
        qkv_pe = [sem(f"{x}_pe") for x in "qkv"]
        raw = [sem(f"raw_{x}") for x in "qkv"]
        tap = [sem(f"taps_{x}") for x in "qkv"]
        head_kept = [sem(f"head_kept_{x}") for x in "qkv"]
        lt_ready, lx_pe, lx_ready = sem("lt_ready"), sem("lx_pe"), sem("lx_ready")
        xlx_pe, xlxT_pe, x_new, xT_new = sem("xlx_pe"), sem("xlxT_pe"), sem("x_new"), sem("xT_new")
        silu = [sem(f"silu_done_{x}") for x in "qkv"]
        sq_ready = [sem(f"sq_ready_{x}") for x in "qk"]
        w_cut = [sem(f"w_cut{i}") for i in range(len(CUTS))] if sample else []
        mask_step = sem("mask_step")
        if sample:
            dm_ready, sh_pe, sh_ready = sem("dm_ready"), sem("sh_pe"), sem("sh_ready")

        def past(eng, semaphore, count):
            if not (isinstance(count, int) and count <= 0):
                eng.wait_ge(semaphore, count)

        def levels(m, l):
            return m * LV + l + 1

        def halves(x, l, s_):
            return x.rearrange("p h (n s r) -> p (h n) s r", s=2, r=2 << l)[:, :, s_, :]

        def half_bank(bank_, l):
            return bank_[:, 0:W // 2].rearrange("p (n r) -> p n r", r=2 << l)

        def over_heads(mask):
            return mask.rearrange("p (a i) -> p a i", a=1).to_broadcast([P, H_B, P])

        block = ctx.enter_context(nc.Block())

        @block.sync
        def _(sp):
            n_set = 0
            if sample:
                sp.dma_start(xf[:], a["x"][0]).then_inc(s["x_loaded"], 16)
                sp.dma_start(rows_in[0:8], a["norm1"].rearrange("(c p) -> c p", p=P)).then_inc(s["set_loaded"], 16)
                sp.dma_start(rows_in[8:12], a["gmlp_norm"].rearrange("(c p) -> c p", p=P)).then_inc(s["set_loaded"], 16)
                sp.dma_start(rows_in[12:13], a["gdn_norm"].rearrange("(c p) -> c p", p=P)).then_inc(s["set_loaded"], 16)
                sp.dma_start(rows_in[13:COLS], a["conv_w"].rearrange("i (c p) -> (i c) p", p=P)).then_inc(s["set_loaded"], 16)
                sp.dma_start(sh["dt_bias"][:], a["dt_bias"].rearrange("(a n) -> a n", a=1).to_broadcast([P, H_B])).then_inc(s["set_loaded"], 16)
                sp.dma_start(a_log[:], a["a_log"].rearrange("(a n) -> a n", a=1).to_broadcast([P, H_B])).then_inc(s["set_loaded"], 16)
                sp.dma_start(conv_in[:], a["state_conv"].rearrange("b r n -> (b r) n")).then_inc(s["set_loaded"], 16)
                sp.dma_start(bs_in[:], a["gmlp_bs"].rearrange("(a g) i -> a g i", a=1).to_broadcast([P, G_A, P])).then_inc(s["set_loaded"], 16)
                n_set = 8
                w_dram = a["w_in"].rearrange("(c p) n -> p c n", p=P)
                for i, (lo, hi) in enumerate(CUTS):
                    sp.dma_start(sh["w_in"][:, :, lo:hi], w_dram[:, :, lo:hi]).then_inc(w_cut[i], 16)
                sp.wait_ge(s["set_masks"], 1)
                for b in range(B):
                    sp.dma_start(ws_in[b * C:(b + 1) * C, :, b * C:(b + 1) * C],
                                 a["gmlp_ws"][:, 0:C, 0:C].rearrange("g i j -> i g j")).then_inc(s["ws_loaded"], 16)
                sp.wait_ge(s["tail_ready"], 1)
                sp.wait_ge(silu[2], 1)
                sp.wait_ge(s["h_turned"], 2)
                for h_ in range(H_B):
                    sp.dma_start(S[:, h_], a["state_gdn"][:, h_].rearrange("b k v -> k b v")).then_inc(s["states_in"], 16)
            else:
                sp.dma_start(xf[:], a["x"][0]).then_inc(s["x_loaded"], 16)
                sp.dma_start(ws_in[:], a["gmlp_ws"].rearrange("g i j -> i g j")).then_inc(s["set_loaded"], 16)
                sp.dma_start(bs[:], a["gmlp_bs"].rearrange("(a g) i -> a g i", a=1).to_broadcast([P, G_A, P])).then_inc(s["set_loaded"], 16)
                sp.wait_ge(s["h_ready"], 1)
                sp.dma_start(xf[:], a["x"][1]).then_inc(s["x_loaded"], 16)

            def tile(m, ahead):
                if ahead:
                    sp.wait_ge(s["h_ready"], m + 2)
                    sp.dma_start(xf[:], a["x"][m + 2] if isinstance(m, int) else
                                 a["x"][bass.ds(m + 2, 1)].rearrange("a p n -> (a p) n")).then_inc(s["x_loaded"], 16)
                sp.wait_ge(s["y_ready"], m + 1)
                sp.wait_ge(s["ya_ready"], m + 1)
                dst = a["y"][m] if isinstance(m, int) else a["y"][bass.ds(m, 1)].rearrange("a p n -> (a p) n")
                sp.dma_start(dst, yT[:].rearrange("p c i -> p (c i)")).then_inc(s["y_stored"], 16)

            if sample:
                sp.wait_ge(s["va_done"], 1)
                sp.dma_start(a["new_v"], va[:]).then_inc(s["va_stored"], 16)
                tile(0, False)
                sp.wait_ge(sh_ready, H_B)
                for h_ in range(H_B):
                    sp.dma_start(a["new_gdn"][:, h_].rearrange("b k v -> k b v"), S[:, h_]).then_inc(s["s_stored"], 16)
                sp.wait_ge(s["va_stored"], 16)
            else:
                tile(0, True)
                with sp.Fori(1, TILES - 3, 2) as m:
                    tile(m, True)
                    tile(m + 1, True)
                tile(TILES - 3, True)
                tile(TILES - 2, False)
                tile(TILES - 1, False)
                sp.wait_ge(s["s_ready"], TILES)
                sp.dma_start(a["new_gdn"].rearrange("h k v -> k h v"), S[:, :, 0, :]).then_inc(s["s_stored"], 16)
            sp.wait_ge(s["rows_ready"], 3)
            sp.dma_start(a["new_conv"], tail_rows[:]).then_inc(s["rows_stored"], 16)
            sp.wait_ge(s["y_stored"], 16 * TILES)
            sp.wait_ge(s["s_stored"], 16 * H_B if sample else 16)
            sp.wait_ge(s["rows_stored"], 16)

        @block.gpsimd
        def _(pool):
            steps = [0]

            def step(inst):
                inst.then_inc(mask_step, 1)
                steps[0] += 1
                pool.wait_ge(mask_step, steps[0])

            def keep(view, pattern, base, per_partition, op=ALU.is_ge):
                step(pool.affine_select(out=view, in_=view, compare_op=op, fill=0.0, base=base, pattern=pattern,
                                        channel_multiplier=per_partition))

            if sample:
                step(pool.memset(sh["eps"][:], EPS))
                step(pool.memset(sh["ln_scale"][:], -0.5 * math.log(DK)))
                step(pool.memset(sh["ones"][:], 1.0))
                step(pool.memset(sh["ident"][:], 1.0))
                keep(sh["ident"][:], [[-1, P]], 0, 1)
                keep(sh["ident"][:], [[1, P]], 0, -1)
                pool.memset(ws_in[:], 0.0).then_inc(s["set_masks"], 1)
                step(pool.memset(same[:], 1.0))
                v = same[:].rearrange("p (b r) -> p b r", r=C)
                keep(v, [[-C, B], [0, C]], 0, 1)
                keep(v, [[C, B], [0, C]], C - 1, -1)
                step(pool.memset(stream[:], 1.0))
                keep(stream[:], [[-C, B]], 0, 1)
                keep(stream[:], [[C, B]], C - 1, -1)
                step(pool.memset(sh["link"][:], 0.0))
                for l in range(LEVELS):
                    b = 1 << l
                    v = sh["link"][:, l, :].rearrange("p (n s r) -> p n s r", s=2, r=b)[:, :, 1, :]
                    step(pool.memset(v, 1.0))
                    keep(v, [[-2 * b, P // (2 * b)], [0, b]], 0, 1)
                    keep(v, [[2 * b, P // (2 * b)], [0, b]], b - 1, -1)
            for t_, pat, mul, op in ((sh["upto"], [[1, P]], -1, ALU.is_ge), (sh["after"], [[-1, P]], 1, ALU.is_gt)):
                if sample:
                    step(pool.tensor_copy(t_[:], same[:]))
                else:
                    step(pool.memset(t_[:], 1.0))
                keep(t_[:], pat, 0, mul, op)
            if not sample:
                step(pool.memset(cin[:, :, :, 0:CONV_W - 1], 0.0))
                step(pool.memset(S[:], 0.0))
            for x in LX:
                step(pool.memset(x[:], 0.0))
            pool.memset(small[:], 0.0).then_inc(s["set_masks"], 1)

            def tile(m):
                for l in range(LV):
                    pool.wait_ge(s["mt_ready"], m + 1)
                    if l >= 2:
                        pool.wait_ge(lx_pe, levels(m, l - 2))
                    elif not sample:
                        past(pool, lx_pe, levels(m, l - 2))
                    pool.tensor_tensor(lt[:, l % 2], mt[:], over_heads(sh["link"][:, l + 1, :]), ALU.mult)\
                        .then_inc(lt_ready, 1)

            if sample:
                tile(0)
            else:
                tile(0)
                with pool.Fori(1, TILES - 3, 2) as m:
                    tile(m)
                    tile(m + 1)
                for m in range(TILES - 3, TILES):
                    tile(m)

        @block.scalar
        def _(act):
            def exp_and_ln():
                act.preload_act_table_set("natural_log_exp_and_others")

            def front(m):
                act.wait_ge(s["x_loaded"], 16 * (m + 1))
                past(act, s["h_turned"], 2 * m)
                act.activation(h[:], xf[:], ACT.Square, accum_out=ssum[:]).then_inc(s["squared"], 1)
                act.wait_ge(s["squared"], m + 1)
                act.activation(rstd[:], ssum[:], ACT.Ln, bias=sh["eps"][:], scale=1.0 / D_MODEL).then_inc(s["ln_x"], 1)
                act.wait_ge(s["ln_x"], m + 1)
                act.activation(rstd[:], rstd[:], ACT.Exp, scale=-0.5).then_inc(s["rstd_ready"], 1)

            def gates_raw(m):
                act.wait_ge(s["ba_done"], m + 1)
                past(act, s["b1_ready"], m)
                act.activation(small[:, 0, :], gs[:, 0:H_B], ACT.Exp, scale=-1.0).then_inc(s["eb_raw"], 1)
                act.wait_ge(s["nax_ready"], m + 1)
                act.activation(small[:, 3, :], small[:, 2, :], ACT.Exp).then_inc(s["ex_ready"], 1)
                act.wait_ge(s["ex_ready"], m + 1)
                act.activation(small[:, 4, :], small[:, 3, :], ACT.Ln, bias=1.0).then_inc(s["lnx_ready"], 1)

            def keep_raw(j, m):
                act.wait_ge(qkv_pe[j], m + 1)
                if sample:
                    act.wait_ge(s["bs_ready"], 1)
                else:
                    past(act, head_kept[j], m)
                for c in range(4):
                    last = act.activation(cin[:, 4 * j + c, :, CONV_W - 1:],
                                          pr[j % 2][:, c * P:(c + 1) * P].rearrange("p (b r) -> p b r", b=B), ACT.Copy)
                last.then_inc(raw[j], 1)

            def silu_of(j, m):
                act.wait_ge(tap[j], (m + 1) * CONV_W)
                past(act, [s["qn_ready"], s["kn_ready"], s["v_turned"]][j], m)
                act.activation(act3[j][:], conv[:], ACT.Silu).then_inc(silu[j], 1)
                if j < 2:
                    act.wait_ge(silu[j], m + 1)
                    past(act, [s["ssq_pe"], s["ssa_pe"]][j], m)
                    act.activation(sq[j][:], act3[j][:], ACT.Square).then_inc(sq_ready[j], 1)

            def gelu_v(m):
                act.wait_ge(s["va_pe"], m + 1)
                past(act, s["sa_pe"], m)
                act.activation(va[:], pr[1][:], ACT.Gelu_apprx_tanh).then_inc(s["va_done"], 1)

            def silu_z(m, par):
                act.wait_ge(s["z_pe"], m + 1)
                past(act, s["y_ready"], m - 1)
                act.activation(z[:, par], pr[0][:].rearrange("p (c i) -> p c i", i=P), ACT.Silu).then_inc(s["z_done"], 1)

            def gelu_u(m):
                act.wait_ge(s["u_pe"], m + 1)
                past(act, s["ya_mul"], m)
                act.activation(u[:], pr[1][:].rearrange("p (c i) -> p c i", i=P), ACT.Gelu_apprx_tanh)\
                   .then_inc(s["u_done"], 1)

            def rsqrt(dst, src, count, ln_sem, ready, m, scale, bias):
                act.wait_ge(count, m + 1)
                act.activation(dst[:], src, ACT.Ln, bias=sh["eps"][:], scale=scale).then_inc(ln_sem, 1)
                act.wait_ge(ln_sem, m + 1)
                if bias is None:
                    act.activation(dst[:], dst[:], ACT.Exp, scale=-0.5).then_inc(ready, 1)
                else:
                    act.activation(dst[:], dst[:], ACT.Exp, scale=-0.5, bias=bias).then_inc(ready, 1)

            def decays(m):
                act.wait_ge(s["decay_pe"], m + 1)
                past(act, s["attn_ready"], m)
                act.activation(decay[:], heads[0], ACT.Exp).then_inc(s["decay_exp"], 1)
                act.wait_ge(s["eb_pe"], m + 1)
                past(act, s["y_ready"], m)
                act.activation(eb[:], heads[1], ACT.Exp).then_inc(s["eb_ready"], 1)
                act.wait_ge(s["small_pe"], m + 1)
                past(act, s["s_ready"], m)
                n = gates.shape[1]
                act.activation(gates[:], gs[:, 16:16 + n], ACT.Exp).then_inc(s["gates_ready"], 1)
                past(act, s["kn_ready"], m)
                past(act, s["o_norm_ready"], m)
                rsqrt(r_k, heads[3], s["ssk_pe"], s["ln_k"], s["rk_ready"], m, 1.0, None)
                past(act, s["ya_ready"], m)
                rsqrt(r_q, heads[2], s["ssq_pe"], s["ln_q"], s["rq_ready"], m, 1.0, sh["ln_scale"][:])

            def v_and_x(m, par):
                act.wait_ge(s["v_turned"], m + 1)
                past(act, s["delta_pe"], m)
                for h_ in range(H_B):
                    last = act.activation(v_beta[:, h_], heads[0][:, h_], ACT.Copy, scale=beta[:, par, h_:h_ + 1])
                last.then_inc(s["v_beta_ready"], 1)
                act.wait_ge(s["x_turned"], m + 1)
                act.activation(X[:], heads[4], ACT.Copy).then_inc(s["x_ready"], 1)

            def level(l, m):
                act.wait_ge(lx_pe, levels(m, l))
                act.activation(halves(LX[l][:], l, 0), half_bank(gb[0], l), ACT.Copy).then_inc(lx_ready, 1)

            def gmlp_square(m):
                act.wait_ge(s["ya_mul"], m + 1)
                act.wait_ge(s["ssk_pe"], m + 1)
                act.activation(sq_gmlp[:], ya[:], ACT.Square).then_inc(s["sq_a"], 1)

            def scan(m):
                act.wait_ge(s["w_pe"], m + 1)
                act.activation(w_neg[:], heads[0], ACT.Copy, scale=-1.0).then_inc(s["w_ready"], 1)
                if sample:
                    act.wait_ge(s["delta_pe"], m + 1)
                    act.activation(delta_T[:], heads[1], ACT.Copy).then_inc(s["deltaT_ready"], 1)
                    act.wait_ge(s["deltaT_pe"], m + 1)
                    act.activation(delta[:], heads[0], ACT.Copy).then_inc(s["delta_ready"], 1)
                else:
                    act.wait_ge(s["delta_pe"], m + 1)
                    act.activation(delta[:], heads[1], ACT.Copy).then_inc(s["delta_ready"], 1)

            def out(m):
                act.wait_ge(s["o_pe"], m + 1)
                act.wait_ge(lx_pe, levels(m, LV - 1))
                act.activation(sq_o[:], heads[2], ACT.Square).then_inc(s["sq_o_ready"], 1)
                act.wait_ge(s["kn_ready"], m + 1)
                rsqrt(r_k, heads[4], s["sso_pe"], s["ln_o"], s["ro_ready"], m, 1.0 / DV, None)

            def tile(m, par, project, fronts):
                exp_and_ln()
                decays(m)
                if project:
                    gates_raw(m + 1)
                v_and_x(m, par)
                if fronts:
                    front(m + 2)
                if project:
                    keep_raw(0, m + 1)
                for l in range(LV):
                    level(l, m)
                    if l == 0:
                        gmlp_square(m)
                        if project:
                            keep_raw(1, m + 1)
                    if l == 2:
                        act.wait_ge(s["kn_ready"], m + 1)
                        act.wait_ge(s["qn_ready"], m + 1)
                        rsqrt(r_q, heads[4], s["ssa_pe"], s["ln_a"], s["ra_ready"], m, 1.0 / C_A, None)
                        if project:
                            silu_of(0, m + 1)
                            keep_raw(2, m + 1)
                    if l == 4 and project:
                        gelu_v(m + 1)
                        silu_of(1, m + 1)
                scan(m)
                if project:
                    silu_of(2, m + 1)
                    silu_z(m + 1, 1 - par)
                exp_and_ln()
                out(m)
                if project:
                    gelu_u(m + 1)

            def project_alone(m, par):
                for j in range(3):
                    keep_raw(j, m)
                    silu_of(j, m)
                gelu_v(m)
                silu_z(m, par)
                gelu_u(m)

            if sample:
                act.wait_ge(s["set_loaded"], 16 * 8)
                act.activation(sh["neg_a"][:], a_log[:], ACT.Exp).then_inc(s["a_exp"], 1)
                act.wait_ge(s["set_masks"], 2)
                exp_and_ln()
                front(0)
                for j in range(3):
                    keep_raw(j, 0)
                    silu_of(j, 0)
                gelu_v(0)
                silu_z(0, 0)
                exp_and_ln()
                gates_raw(0)
                gelu_u(0)
                tile(0, 0, False, False)
            else:
                act.wait_ge(s["set_masks"], 1)
                exp_and_ln()
                front(0)
                gates_raw(0)
                front(1)
                project_alone(0, 0)
                tile(0, 0, True, True)
                with act.Fori(1, TILES - 3, 2) as m:
                    tile(m, 1, True, True)
                    tile(m + 1, 0, True, True)
                tile(TILES - 3, 1, True, True)
                tile(TILES - 2, 0, True, False)
                tile(TILES - 1, 1, False, False)
            act.wait_ge(s["tail_turned"], 1)
            for j in range(3):
                act.activation(tail_rows[:, j * D_B:(j + 1) * D_B], gb[j][0:B * (CONV_W - 1), :], ACT.Copy)\
                   .then_inc(s["rows_ready"], 1)

        @block.vector
        def _(dve):
            def front(m):
                dve.wait_ge(s["rstd_ready"], m + 1)
                dve.tensor_scalar(h[:], xf[:], rstd[:, 0:1], None, ALU.mult).then_inc(s["h_ready"], 1)

            def h_columns(i, m, par):
                dve.wait_ge(s["h_turned"], 2 * m + i + 1)
                if i == 0:
                    past(dve, s["u_pe"], m - 1)
                dve.tensor_tensor(hT[:, par, 4 * i:4 * i + 4], pr[0][:].rearrange("p (c i) -> p c i", i=P),
                                  sh["cols"][:, 4 * i:4 * i + 4].rearrange("p (c a) -> p c a", a=1)
                                  .to_broadcast([P, 4, P]), ALU.mult).then_inc(s["hT_ready"], 1)

            def gates_raw(m, par):
                dve.wait_ge(s["eb_raw"], m + 1)
                dve.tensor_tensor(small[:, 1, :], gs[:, H_B:2 * H_B], sh["dt_bias"][:], ALU.add).then_inc(s["xa_ready"], 1)
                dve.wait_ge(s["xa_ready"], m + 1)
                dve.scalar_tensor_tensor(out=small[:, 2, :], in0=small[:, 1, :], scalar=-1.0, in1=small[:, 1, :],
                                         op0=ALU.mult, op1=ALU.min).then_inc(s["nax_ready"], 1)
                dve.wait_ge(s["eb_raw"], m + 1)
                dve.tensor_scalar(small[:, 5, :], small[:, 0, :], 1.0, None, ALU.add).then_inc(s["b1_ready"], 1)
                dve.wait_ge(s["b1_ready"], m + 1)
                past(dve, s["beta_eb_ready"], m - 1)
                past(dve, s["v_beta_ready"], m - 1)
                dve.reciprocal(beta[:, par, :], small[:, 5, :]).then_inc(s["beta_ready"], 1)
                dve.wait_ge(s["lnx_ready"], m + 1)
                dve.scalar_tensor_tensor(out=small[:, 6, :], in0=small[:, 1, :], scalar=0.0, in1=small[:, 4, :],
                                         op0=ALU.max, op1=ALU.add).then_inc(s["sp_ready"], 1)
                dve.wait_ge(s["sp_ready"], m + 1)
                past(dve, s["small_pe"], m - 1)
                dve.tensor_tensor(g[:, par, :], small[:, 6, :], sh["neg_a"][:], ALU.mult).then_inc(s["g_ready"], 1)

            def gates_spread(m, par):
                def wide(x):
                    return x[:, par, :].rearrange("p (h a) -> p h a", a=1).to_broadcast([P, H_B, P])

                dve.wait_ge(s["g_ready"], m + 1)
                past(dve, s["eb_pe"], m)
                past(dve, s["decay_pe"], m)
                dve.tensor_tensor(g_upto[:], over_heads(sh["upto"][:]), wide(g), ALU.mult).then_inc(s["g_upto_ready"], 1)
                dve.wait_ge(s["beta_ready"], m + 1)
                past(dve, s["bb_pe"], m)
                dve.tensor_tensor(beta_diag[:], over_heads(sh["ident"][:]), wide(beta), ALU.mult)\
                   .then_inc(s["beta_diag_ready"], 1)
                if sample:
                    dve.tensor_tensor(g_of[:], stream[:].rearrange("p (a b) -> p a b", a=1).to_broadcast([P, H_B, B]),
                                      g[:, par, :].rearrange("p (h a) -> p h a", a=1).to_broadcast([P, H_B, B]),
                                      ALU.mult).then_inc(s["g_of_ready"], 1)

            def conv_tap(j, i, m):
                if i == 0:
                    dve.wait_ge(raw[j], m + 1)
                    if j > 0:
                        dve.wait_ge(silu[j - 1], m + 1)
                    else:
                        past(dve, silu[2], m)
                else:
                    dve.wait_ge(tap[j], m * CONV_W + i)
                for c in range(4):
                    o = conv[:, c].rearrange("p (b r) -> p b r", b=B)
                    x = cin[:, 4 * j + c, :, i:i + C]
                    w = sh["cols"][:, 13 + 12 * i + 4 * j + c:14 + 12 * i + 4 * j + c]
                    if i == 0:
                        last = dve.tensor_scalar(o, x, w, None, ALU.mult)
                    else:
                        last = dve.scalar_tensor_tensor(out=o, in0=x, scalar=w, in1=o, op0=ALU.mult, op1=ALU.add)
                last.then_inc(tap[j], 1)
                if i == CONV_W - 1 and not sample:
                    dve.wait_ge(tap[j], (m + 1) * CONV_W)
                    dve.tensor_copy(cin[:, 4 * j:4 * j + 4, 0, 0:CONV_W - 1], cin[:, 4 * j:4 * j + 4, 0, C:])\
                       .then_inc(head_kept[j], 1)

            def start(m, par):
                dve.wait_ge(s["decay_exp"], m + 1)
                dve.tensor_tensor(decay[:], decay[:], over_heads(sh["upto"][:]), ALU.mult).then_inc(s["decay_ready"], 1)
                dve.wait_ge(s["gates_ready"], m + 1)
                dve.tensor_tensor(beta_eb[:], beta[:, par, :], gates[:, 0:H_B], ALU.mult).then_inc(s["beta_eb_ready"], 1)
                dve.wait_ge(s["rk_ready"], m + 1)
                past(dve, s["k_turned"], m)
                past(dve, s["qk_pe"], m)
                dve.tensor_tensor(kn[:], act3[1][:], r_k[:], ALU.mult).then_inc(s["kn_ready"], 1)
                dve.wait_ge(s["kn_ready"], m + 1)
                dve.wait_ge(s["bb_pe"], m + 1)
                dve.tensor_tensor(kb[:], heads[4], kn[:], ALU.mult).then_inc(s["kb_ready"], 1)
                dve.wait_ge(s["rq_ready"], m + 1)
                dve.tensor_tensor(qn[:], act3[0][:], r_q[:], ALU.mult).then_inc(s["qn_ready"], 1)
                dve.wait_ge(s["qn_ready"], m + 1)
                dve.wait_ge(s["eb_ready"], m + 1)
                past(dve, s["o_pe"], m)
                dve.tensor_tensor(q_dec[:], qn[:], eb[:], ALU.mult).then_inc(s["q_dec_ready"], 1)

            def products(m):
                dve.wait_ge(s["kk_pe"], m + 1)
                dve.wait_ge(s["decay_ready"], m + 1)
                past(dve, s["delta_pe"], m)
                dve.tensor_tensor(mt[:], heads[2], decay[:], ALU.mult).then_inc(s["mt_ready"], 1)
                dve.wait_ge(s["mt_ready"], m + 1)
                past(dve, s["s_pe"], m)
                dve.scalar_tensor_tensor(out=XT[:], in0=mt[:], scalar=-1.0, in1=over_heads(sh["link"][:, 0, :]),
                                         op0=ALU.mult, op1=ALU.mult).then_inc(s["xt_neg"], 1)
                dve.wait_ge(s["xt_neg"], m + 1)
                dve.tensor_tensor(XT[:], XT[:], over_heads(sh["ident"][:]), ALU.add).then_inc(s["xt_ready"], 1)
                dve.wait_ge(s["k_turned"], m + 1)
                dve.wait_ge(s["beta_eb_ready"], m + 1)
                past(dve, s["w_pe"], m)
                past(dve, s["s_pe"], m)
                for h_ in range(H_B):
                    last = dve.tensor_scalar(k_beta[:, h_], heads[1][:, h_], beta_eb[:, h_:h_ + 1], None, ALU.mult)
                last.then_inc(s["k_beta_ready"], 1)
                for h_ in range(H_B):
                    last = dve.tensor_scalar(k_dec[:, h_], heads[1][:, h_], gates[:, H_B + h_:H_B + h_ + 1], None, ALU.mult)
                last.then_inc(s["k_dec_ready"], 1)
                dve.wait_ge(s["qk_pe"], m + 1)
                past(dve, s["o_pe"], m)
                dve.tensor_tensor(attn[:], heads[3], decay[:], ALU.mult).then_inc(s["attn_ready"], 1)

            def level(l, m):
                if l < LV - 1:
                    dve.wait_ge(xlx_pe, m * (LV - 1) + l + 1)
                    if l == 0:
                        dve.wait_ge(s["x_ready"], m + 1)
                    else:
                        dve.wait_ge(x_new, m * (LV - 1) + l)
                    even = halves(X[:], l, 0)
                    dve.tensor_tensor(even, even, half_bank(gb[1], l), ALU.subtract).then_inc(x_new, 1)
                dve.wait_ge(xlxT_pe, levels(m, l))
                if l == 0:
                    dve.wait_ge(s["xt_ready"], m + 1)
                else:
                    dve.wait_ge(xT_new, levels(m, l - 1))
                odd = halves(XT[:], l, 1)
                dve.tensor_tensor(odd, odd, half_bank(gb[2], l), ALU.subtract).then_inc(xT_new, 1)

            def gmlp(m):
                dve.wait_ge(s["sa_pe"], m + 1)
                past(dve, s["ya_ready"], m)
                dve.tensor_tensor(ya[:], heads[3], bs[:], ALU.add).then_inc(s["ya_bias"], 1)
                dve.wait_ge(s["ya_bias"], m + 1)
                dve.wait_ge(s["u_done"], m + 1)
                dve.tensor_tensor(ya[:], ya[:], u[:], ALU.mult).then_inc(s["ya_mul"], 1)

            def gmlp_out(m):
                dve.wait_ge(s["ra_ready"], m + 1)
                past(dve, s["y_stored"], 16 * m)
                for c in range(G_A):
                    last = dve.scalar_tensor_tensor(out=yT[:, c], in0=ya[:, c], scalar=sh["cols"][:, 8 + c:9 + c],
                                                    in1=r_q[:, c], op0=ALU.mult, op1=ALU.mult)
                last.then_inc(s["ya_ready"], 1)

            def state(m):
                if not sample:
                    dve.wait_ge(s["s_pe"], m + 1)
                    dve.wait_ge(s["o_pe"], m + 1)
                    dve.wait_ge(s["gates_ready"], m + 1)
                    for h_ in range(H_B):
                        last = dve.scalar_tensor_tensor(out=S[:, h_, 0], in0=S[:, h_, 0],
                                                        scalar=gates[:, 2 * H_B + h_:2 * H_B + h_ + 1],
                                                        in1=heads[3][:, h_], op0=ALU.mult, op1=ALU.add)
                    last.then_inc(s["s_ready"], 1)
                    return
                dve.wait_ge(s["delta_ready"], 1)
                for h_ in range(H_B):
                    if h_ > 0:
                        dve.wait_ge(sh_pe, h_)
                    dve.tensor_tensor(delta_of[:], delta[:, h_:h_ + 1].to_broadcast([P, B, P]),
                                      stream[:].rearrange("p (b a) -> p b a", a=1).to_broadcast([P, B, P]), ALU.mult)\
                       .then_inc(dm_ready, 1)
                    dve.wait_ge(sh_pe, h_ + 1)
                    dve.wait_ge(s["o_pe"], 1)
                    for b in range(B):
                        c = 3 * H_B + h_ * B + b
                        last = dve.scalar_tensor_tensor(out=S[:, h_, b], in0=S[:, h_, b], scalar=gates[:, c:c + 1],
                                                        in1=pr[b // 4][:, (b % 4) * P:(b % 4 + 1) * P],
                                                        op0=ALU.mult, op1=ALU.add)
                    last.then_inc(sh_ready, 1)

            def out(m, par):
                dve.wait_ge(s["ro_ready"], m + 1)
                dve.scalar_tensor_tensor(out=o_norm[:], in0=heads[2], scalar=sh["cols"][:, 12:13], in1=r_k[:],
                                         op0=ALU.mult, op1=ALU.mult).then_inc(s["o_norm_ready"], 1)
                dve.wait_ge(s["o_norm_ready"], m + 1)
                dve.wait_ge(s["z_done"], m + 1)
                dve.tensor_tensor(yT[:, G_A:], o_norm[:], z[:, par], ALU.mult).then_inc(s["y_ready"], 1)

            def tile(m, par, project, fronts):
                start(m, par)
                if project:
                    gates_raw(m + 1, 1 - par)
                products(m)
                gmlp(m)
                if fronts:
                    front(m + 2)
                n_taps = 3 * CONV_W
                for l in range(LV):
                    for i in (2 * l, 2 * l + 1):
                        if project and i < n_taps:
                            conv_tap(i // CONV_W, i % CONV_W, m + 1)
                    level(l, m)
                    if l == 3 or (LV < 4 and l == LV - 1):
                        gmlp_out(m)
                if project:
                    gates_spread(m + 1, 1 - par)
                state(m)
                if fronts:
                    h_columns(0, m + 2, par)
                    h_columns(1, m + 2, par)
                out(m, par)

            if sample:
                dve.wait_ge(s["rows_turned"], 1)
                dve.tensor_copy(sh["cols"][:], gb[1][:, 0:COLS]).then_inc(s["cols_ready"], 1)
                dve.wait_ge(s["a_exp"], 1)
                dve.tensor_scalar(sh["neg_a"][:], sh["neg_a"][:], -1.0, None, ALU.mult).then_inc(s["a_ready"], 1)
                dve.wait_ge(s["cin_turned"], 1)
                dve.tensor_copy(cin[:, :, :, 0:CONV_W - 1],
                                gb[2][:, 0:12 * B * (CONV_W - 1)].rearrange("p (c b r) -> p c b r", c=12, b=B))\
                   .then_inc(s["cin_ready"], 1)
                dve.wait_ge(s["set_loaded"], 16 * 8)
                dve.tensor_copy(bs[:].rearrange("p g (b r) -> p g b r", b=B),
                                bs_in[:, :, 0:C].rearrange("p g (a r) -> p g a r", a=1).to_broadcast([P, G_A, B, C]))\
                   .then_inc(s["bs_ready"], 1)
                dve.wait_ge(s["bs_ready"], 1)
                dve.wait_ge(s["cols_ready"], 1)
                dve.wait_ge(s["a_ready"], 1)
            dve.wait_ge(s["ws_turned"], 1)
            dve.tensor_copy(wsT[:], heads[0]).then_inc(s["ws_copied"], 1)
            dve.wait_ge(s["ws_copied"], 1)
            if sample:
                dve.engine_nop().then_inc(s["ws_ready"], 1)
            else:
                for lo in range(CHUNK, P, CHUNK):
                    last = dve.memset(wsT[lo:lo + CHUNK, :, 0:lo], 0.0)
                last.then_inc(s["ws_ready"], 1)
                dve.wait_ge(s["set_loaded"], 32)
            dve.wait_ge(s["set_masks"], 2 if sample else 1)
            front(0)
            h_columns(0, 0, 0)
            h_columns(1, 0, 0)
            if sample:
                for j in range(3):
                    for i in range(CONV_W):
                        conv_tap(j, i, 0)
                dve.tensor_copy(tails[:].rearrange("p c (b r) -> p c b r", b=B), cin[:, :, :, C:]).then_inc(s["tail_ready"], 1)
                gates_raw(0, 0)
                gates_spread(0, 0)
                tile(0, 0, False, False)
            else:
                gates_raw(0, 0)
                gates_spread(0, 0)
                front(1)
                for j in range(3):
                    for i in range(CONV_W):
                        conv_tap(j, i, 0)
                h_columns(0, 1, 1)
                h_columns(1, 1, 1)
                tile(0, 0, True, True)
                with dve.Fori(1, TILES - 3, 2) as m:
                    tile(m, 1, True, True)
                    tile(m + 1, 0, True, True)
                tile(TILES - 3, 1, True, True)
                tile(TILES - 2, 0, True, False)
                tile(TILES - 1, 1, False, False)
                for j in range(3):
                    dve.wait_ge(head_kept[j], TILES)
                dve.tensor_copy(tails[:], cin[:, :, 0, 0:CONV_W - 1]).then_inc(s["tail_ready"], 1)

        @block.tensor
        def _(pe):
            def turn_h(i, m):
                if i == 0:
                    pe.wait_ge(s["h_ready"], m + 1)
                    past(pe, s["z_done"], m)
                else:
                    pe.wait_ge(s["hT_ready"], 2 * m + 1)
                for k in range(4 * i, 4 * i + 4):
                    last = pe.transpose(pr[0][:, (k % 4) * P:(k % 4 + 1) * P], h[:, k * P:(k + 1) * P], sh["ident"][:])
                last.then_inc(s["h_turned"], 1)

            def gate_columns(m, par):
                pe.wait_ge(s["hT_ready"], 2 * m + 2)
                past(pe, s["gates_ready"], m)
                past(pe, s["eb_raw"], m)
                past(pe, s["xa_ready"], m)
                if sample:
                    pe.wait_ge(w_cut[CUT_OF["ba"]], 16)
                for k in range(KC):
                    last = pe.matmul(gs[:, 0:2 * H_B], hT[:, par, k], sh["w_in"][:, k, COL_BA:COL_BA + 2 * H_B],
                                     start=(k == 0), stop=(k == KC - 1))
                last.then_inc(s["ba_done"], 1)

            def columns(bank_, c, col, par):
                for k in range(KC):
                    last = pe.matmul(bank_[:, c * P:(c + 1) * P], sh["w_in"][:, k, col + c * P:col + (c + 1) * P], hT[:, par, k],
                                     start=(k == 0), stop=(k == KC - 1))
                return last

            def qkv_columns(j, c, m, par):
                if c == 0:
                    if j == 0:
                        pe.wait_ge(s["hT_ready"], 2 * m + 2)
                    elif j == 1:
                        past(pe, s["u_done"], m)
                    else:
                        pe.wait_ge(raw[0], m + 1)
                    if sample:
                        pe.wait_ge(w_cut[CUT_OF["qkv"[j]]], 16)
                last = columns(pr[j % 2], c, COL_QKV + j * D_B, par)
                if c == 3:
                    last.then_inc(qkv_pe[j], 1)

            def va_columns(part, m, par):
                if part == 0:
                    pe.wait_ge(raw[1], m + 1)
                    if sample:
                        pe.wait_ge(w_cut[CUT_OF["va"]], 16)
                for k in (2 * part, 2 * part + 1):
                    last = pe.matmul(pr[1][:], hT[:, par, k], sh["w_in"][:, k, COL_VA:COL_VA + D_A],
                                     start=(k == 0), stop=(k == KC - 1))
                if part == 3:
                    last.then_inc(s["va_pe"], 1)

            def z_columns(c, m, par):
                if c == 0:
                    pe.wait_ge(raw[2], m + 1)
                    if sample:
                        pe.wait_ge(w_cut[CUT_OF["z"]], 16)
                last = columns(pr[0], c, COL_Z, par)
                if c == 3:
                    last.then_inc(s["z_pe"], 1)

            def u_columns(c, m, par):
                if c == 0:
                    pe.wait_ge(s["va_done"], m + 1)
                    if sample:
                        pe.wait_ge(w_cut[CUT_OF["u"]], 16)
                last = columns(pr[1], c, COL_U, par)
                if c == 3:
                    last.then_inc(s["u_pe"], 1)

            def start(m, par):
                flat = "p h i -> p (h i)"
                pe.wait_ge(s["g_upto_ready"], m + 1)
                past(pe, s["w_ready"], m)
                pe.matmul(gb[0][:], sh["after"][:], g_upto[:].rearrange(flat), start=True, stop=True).then_inc(s["decay_pe"], 1)
                past(pe, s["delta_ready"], m)
                pe.matmul(gb[1][:], sh["ones"][:], g_upto[:].rearrange(flat), start=True, stop=True).then_inc(s["eb_pe"], 1)
                past(pe, s["gates_ready"], m)
                pe.wait_ge(s["g_ready"], m + 1)
                for i, mask in enumerate((sh["upto"], sh["after"], sh["ones"])):
                    last = pe.matmul(gs[:, 16 + i * H_B:16 + (i + 1) * H_B], mask[:], g[:, par, :], start=True, stop=True)
                if sample:
                    pe.wait_ge(s["g_of_ready"], 1)
                    last = pe.matmul(gs[:, 16 + 3 * H_B:16 + 3 * H_B + H_B * B], sh["ones"][:],
                                     g_of[:].rearrange("p h b -> p (h b)"), start=True, stop=True)
                last.then_inc(s["small_pe"], 1)
                pe.wait_ge(sq_ready[1], m + 1)
                past(pe, s["s_ready"], m)
                pe.matmul(gb[3][:], sh["ones"][:], sq[1][:].rearrange(flat), start=True, stop=True).then_inc(s["ssk_pe"], 1)
                pe.wait_ge(s["beta_diag_ready"], m + 1)
                past(pe, s["ln_o"], m)
                pe.matmul(gb[4][:], sh["ones"][:], beta_diag[:].rearrange(flat), start=True, stop=True).then_inc(s["bb_pe"], 1)
                pe.wait_ge(sq_ready[0], m + 1)
                past(pe, s["o_norm_ready"], m)
                pe.matmul(gb[2][:], sh["ones"][:], sq[0][:].rearrange(flat), start=True, stop=True).then_inc(s["ssq_pe"], 1)

            def products(m):
                pe.wait_ge(silu[2], m + 1)
                pe.wait_ge(s["decay_exp"], m + 1)
                for h_ in range(H_B):
                    last = pe.transpose(heads[0][:, h_], act3[2][:, h_], sh["ident"][:])
                last.then_inc(s["v_turned"], 1)
                pe.wait_ge(s["kn_ready"], m + 1)
                pe.wait_ge(s["eb_ready"], m + 1)
                for h_ in range(H_B):
                    last = pe.transpose(heads[1][:, h_], kn[:, h_], sh["ident"][:])
                last.then_inc(s["k_turned"], 1)
                pe.wait_ge(s["kb_ready"], m + 1)
                pe.wait_ge(s["ln_q"], m + 1)
                for h_ in range(H_B):
                    last = pe.matmul(heads[2][:, h_], kn[:, h_], kb[:, h_], start=True, stop=True)
                last.then_inc(s["kk_pe"], 1)
                pe.wait_ge(s["qn_ready"], m + 1)
                pe.wait_ge(s["ln_k"], m + 1)
                for h_ in range(H_B):
                    last = pe.matmul(heads[3][:, h_], kn[:, h_], qn[:, h_], start=True, stop=True)
                last.then_inc(s["qk_pe"], 1)

            def turn_x(m):
                pe.wait_ge(s["xt_ready"], m + 1)
                pe.wait_ge(s["kb_ready"], m + 1)
                for h_ in range(H_B):
                    last = pe.transpose(heads[4][:, h_], XT[:, h_], sh["ident"][:])
                last.then_inc(s["x_turned"], 1)

            def of_head(bank_, h_):
                return bank_[:, h_ * P // 2:(h_ + 1) * P // 2]

            def level_lx(l, m):
                pe.wait_ge(lt_ready, levels(m, l))
                if l > 0:
                    pe.wait_ge(x_new, m * (LV - 1) + l)
                else:
                    pe.wait_ge(s["x_ready"], m + 1)
                    pe.wait_ge(s["v_beta_ready"], m + 1)
                for h_ in range(H_B):
                    last = pe.matmul(of_head(gb[0], h_), lt[:, l % 2, h_], halves(X[:, h_:h_ + 1], l, 0),
                                     start=True, stop=True)
                last.then_inc(lx_pe, 1)

            def level_xlx(l, m):
                pe.wait_ge(lx_ready, levels(m, l))
                if l == 0:
                    pe.wait_ge(s["xt_ready"], m + 1)
                else:
                    pe.wait_ge(xT_new, levels(m, l - 1))
                if l < LV - 1:
                    if l == 0:
                        pe.wait_ge(s["k_dec_ready"], m + 1)
                    for h_ in range(H_B):
                        last = pe.matmul(of_head(gb[1], h_), XT[:, h_], halves(LX[l][:, h_:h_ + 1], l, 0),
                                         start=True, stop=True)
                    last.then_inc(xlx_pe, 1)
                for h_ in range(H_B):
                    last = pe.matmul(of_head(gb[2], h_), LX[l][:, h_], halves(XT[:, h_:h_ + 1], l, 1),
                                     start=True, stop=True)
                last.then_inc(xlxT_pe, 1)

            def gmlp(m):
                pe.wait_ge(s["va_done"], m + 1)
                pe.wait_ge(s["attn_ready"], m + 1)
                for c in range(G_A):
                    last = pe.matmul(heads[3][:, c], va[:, c * C_A:(c + 1) * C_A], wsT[:, c], start=True, stop=True)
                last.then_inc(s["sa_pe"], 1)

            def gmlp_norm(m):
                pe.wait_ge(s["sq_a"], m + 1)
                pe.wait_ge(s["x_ready"], m + 1)
                pe.matmul(gb[4][:], sh["ones"][:], sq_gmlp[:].rearrange("p h i -> p (h i)"), start=True, stop=True)\
                  .then_inc(s["ssa_pe"], 1)

            def w(m):
                pe.wait_ge(xT_new, levels(m, LV - 1))
                pe.wait_ge(s["k_beta_ready"], m + 1)
                for h_ in range(H_B):
                    last = pe.matmul(heads[0][:, h_], k_beta[:, h_], XT[:, h_], start=True, stop=True)
                last.then_inc(s["w_pe"], 1)

            def scan(m):
                pe.wait_ge(s["w_ready"], m + 1)
                pe.wait_ge(s["v_beta_ready"], m + 1)
                pe.wait_ge(x_new, (m + 1) * (LV - 1))
                if not sample:
                    past(pe, s["s_ready"], m)
                    for h_ in range(H_B):
                        pe.matmul(heads[1][:, h_], XT[:, h_], v_beta[:, h_], start=True, stop=False)
                        last = pe.matmul(heads[1][:, h_], w_neg[:, h_], S[:, h_, 0], start=False, stop=True)
                    last.then_inc(s["delta_pe"], 1)
                    return
                pe.wait_ge(s["states_in"], 16 * H_B)
                for h_ in range(H_B):
                    pe.matmul(heads[1][:, h_], v_beta[:, h_], XT[:, h_], start=True, stop=True)
                    for b in range(B):
                        own = slice(b * C, (b + 1) * C)
                        last = pe.matmul(heads[1][:, h_, own], S[:, h_, b], w_neg[:, h_, own], start=False,
                                         stop=True, skip_group_check=True)
                last.then_inc(s["delta_pe"], 1)
                pe.wait_ge(s["deltaT_ready"], 1)
                for h_ in range(H_B):
                    last = pe.transpose(heads[0][:, h_], delta_T[:, h_], sh["ident"][:])
                last.then_inc(s["deltaT_pe"], 1)

            def outputs(m):
                pe.wait_ge(s["delta_ready"], m + 1)
                pe.wait_ge(s["q_dec_ready"], m + 1)
                pe.wait_ge(s["attn_ready"], m + 1)
                for h_ in range(H_B):
                    pe.matmul(heads[2][:, h_], delta[:, h_], attn[:, h_], start=True, stop=True)
                    for b in range(B):
                        own = slice(b * C, (b + 1) * C)
                        last = pe.matmul(heads[2][:, h_, own], S[:, h_, b], q_dec[:, h_, own], start=False,
                                         stop=True, skip_group_check=True)
                last.then_inc(s["o_pe"], 1)

            def state(m):
                pe.wait_ge(s["k_dec_ready"], m + 1)
                if not sample:
                    pe.wait_ge(s["ya_bias"], m + 1)
                    for h_ in range(H_B):
                        last = pe.matmul(heads[3][:, h_], k_dec[:, h_], delta[:, h_], start=True, stop=True)
                    last.then_inc(s["s_pe"], 1)
                    return
                pe.wait_ge(s["u_done"], 1)
                pe.wait_ge(s["z_done"], 1)
                for h_ in range(H_B):
                    pe.wait_ge(dm_ready, h_ + 1)
                    if h_ > 0:
                        pe.wait_ge(sh_ready, h_)
                    for i in range(2):
                        last = pe.matmul(pr[i][:], k_dec[:, h_],
                                         delta_of[:, 4 * i:4 * i + 4].rearrange("p b i -> p (b i)"), start=True, stop=True)
                    last.then_inc(sh_pe, 1)

            def out_norm(m):
                pe.wait_ge(s["sq_o_ready"], m + 1)
                pe.wait_ge(s["ln_a"], m + 1)
                pe.matmul(gb[4][:], sh["ones"][:], sq_o[:].rearrange("p h i -> p (h i)"), start=True, stop=True)\
                  .then_inc(s["sso_pe"], 1)

            def tile(m, par, project, fronts):
                ahead = (m + 1, 1 - par)
                start(m, par)
                if project:
                    gate_columns(*ahead)
                    for c in range(4):
                        qkv_columns(0, c, *ahead)
                products(m)
                if project:
                    qkv_columns(1, 0, *ahead)
                    qkv_columns(1, 1, *ahead)
                turn_x(m)
                gmlp(m)
                if project:
                    qkv_columns(1, 2, *ahead)
                    qkv_columns(1, 3, *ahead)
                for l in range(LV):
                    level_lx(l, m)
                    if project:
                        between(2 * l, *ahead)
                    level_xlx(l, m)
                    if l == 1:
                        gmlp_norm(m)
                    if project:
                        between(2 * l + 1, *ahead)
                w(m)
                if project:
                    u_columns(0, *ahead)
                scan(m)
                if project:
                    u_columns(1, *ahead)
                outputs(m)
                state(m)
                if fronts:
                    turn_h(0, m + 2)
                if project:
                    u_columns(2, *ahead)
                out_norm(m)
                if fronts:
                    turn_h(1, m + 2)
                if project:
                    u_columns(3, *ahead)

            def between(i, m, par):
                if i < 4:
                    qkv_columns(2, i, m, par)
                elif i < 8:
                    va_columns(i - 4, m, par)
                else:
                    z_columns(i - 8, m, par)

            pe.wait_ge(s["set_masks"], 2 if sample else 1)
            pe.wait_ge(s["set_loaded"], 16 * (8 if sample else 2))
            if sample:
                pe.transpose(gb[1][:, 0:COLS], rows_in[:], sh["ident"][0:COLS, 0:COLS]).then_inc(s["rows_turned"], 1)
                n = B * (CONV_W - 1)
                for c in range(12):
                    last = pe.transpose(gb[2][:, c * n:(c + 1) * n], conv_in[:, c * P:(c + 1) * P], sh["ident"][0:n, 0:n])
                last.then_inc(s["cin_turned"], 1)
                pe.wait_ge(s["ws_loaded"], 16 * B)
            for c in range(G_A):
                last = pe.transpose(heads[0][:, c], ws_in[:, c], sh["ident"][:])
            last.then_inc(s["ws_turned"], 1)
            pe.wait_ge(s["ws_ready"], 1)
            if sample:
                pe.wait_ge(s["cols_ready"], 1)
                pe.wait_ge(s["cin_ready"], 1)
            turn_h(0, 0)
            turn_h(1, 0)
            if not sample:
                gate_columns(0, 0)
            for j in range(3):
                for c in range(4):
                    qkv_columns(j, c, 0, 0)
            for part in range(4):
                va_columns(part, 0, 0)
            for c in range(4):
                z_columns(c, 0, 0)
            if sample:
                gate_columns(0, 0)
            for c in range(4):
                u_columns(c, 0, 0)
            if sample:
                tile(0, 0, False, False)
            else:
                turn_h(0, 1)
                turn_h(1, 1)
                tile(0, 0, True, True)
                with pe.Fori(1, TILES - 3, 2) as m:
                    tile(m, 1, True, True)
                    tile(m + 1, 0, True, True)
                tile(TILES - 3, 1, True, True)
                tile(TILES - 2, 0, True, False)
                tile(TILES - 1, 1, False, False)
            pe.wait_ge(s["tail_ready"], 1)
            pe.wait_ge(s["y_ready"], TILES)
            pe.wait_ge(sh_ready if sample else s["s_ready"], H_B if sample else TILES)
            for c in range(12):
                last = pe.transpose(gb[c // 4][0:B * (CONV_W - 1), (c % 4) * P:(c % 4 + 1) * P], tails[:, c], sh["ident"][:])
            last.then_inc(s["tail_turned"], 1)


def out_phase(nc, x_tiles, mixed, w_o, norm2_row, w_gate, w_up, w_down, final_norm, y_tiles):
    TILES = len(x_tiles)
    KC = D_MODEL // P
    FC = w_gate.shape[1] // P
    PER = 2
    BLOCKS = FC // PER
    GROUP = 6
    QUARTERS = 4
    QC = D_MODEL // QUARTERS
    USES = BLOCKS + QUARTERS // PER
    NH = D_MODEL // 512
    groups = [(g, min(GROUP, TILES - g)) for g in range(0, TILES, GROUP)]

    wg_dram = w_gate.rearrange("(c p) f -> p c f", p=P)
    wu_dram = w_up.rearrange("(c p) f -> p c f", p=P)
    wo_dram = w_o.rearrange("(c p) n -> p c n", p=P)
    wd_dram = w_down.rearrange("(c p) n -> p c n", p=P)

    with nc.cleanup_on_exit(), ExitStack() as ctx:
        def sb(name, shape, dt=F32):
            return ctx.enter_context(nc.sbuf_tensor(name, shape, dt))

        def sem(name):
            return nc.alloc_semaphore(name=name)

        acc = sb("acc", [P, GROUP, D_MODEL])
        h2 = sb("h2", [P, 2, D_MODEL])
        squares = sb("squares_b", [P, D_MODEL])
        mraw = sb("mraw", [P, 2, KC, P])
        y_out = sb("y_out", [P, 2, D_MODEL])
        h2s = sb("h2s", [P, 2, KC, P])
        h2_hi = sb("h2_hi", [P, KC, GROUP * P], F32R)
        h2_lo = sb("h2_lo", [P, KC, GROUP * P], F32R)
        wraw = sb("wraw", [P, PER, 2, KC, P])
        w_hi = sb("w_hi", [P, PER, 2, KC, P], F32R)
        w_lo = sb("w_lo", [P, PER, 2, KC, P], F32R)
        wdraw = sb("wdraw", [P, PER, D_MODEL])
        wd_hi = sb("wd_hi", [P, PER, D_MODEL], F32R)
        wd_lo = sb("wd_lo", [P, PER, D_MODEL], F32R)
        gate_act = sb("gate_act", [P, 2, GROUP * P // 2])
        act = sb("act", [P, 2, GROUP * P // 2])
        act_hi = sb("act_hi", [P, PER, GROUP * P], F32R)
        act_lo = sb("act_lo", [P, PER, GROUP * P], F32R)
        norm2_in = sb("norm2_in", [KC, P])
        norm2 = sb("norm2", [P, KC])
        fnorm = sb("fnorm", [P, D_MODEL])
        ident = sb("ident_b", [P, P])
        eps = sb("eps_b", [P, 1])
        ssum = sb("ssum", [P, GROUP])
        lnv = sb("lnv", [P, GROUP])
        rstd = sb("rstd", [P, GROUP])
        fssum = sb("fssum", [P, GROUP])
        flnv = sb("flnv", [P, GROUP])
        frstd = sb("frstd", [P, GROUP])

        gate_ps = [ctx.enter_context(nc.psum_tensor(f"gate_ps{i}", [P, 512], F32)) for i in range(2)]
        up_ps = [ctx.enter_context(nc.psum_tensor(f"up_ps{i}", [P, 512], F32)) for i in range(2)]
        down_ps = [ctx.enter_context(nc.psum_tensor(f"down_ps{i}", [P, NH, 512], F32)) for i in range(2)]
        wo_ps = gate_ps + up_ps

        setup_loaded = sem("setup_loaded_b")
        zeroed = sem("zeroed_b")
        ident_ready = sem("ident_ready_b")
        norm2_turned = sem("norm2_turned")
        norm2_ready = sem("norm2_ready")
        x_loaded = [sem(f"x_loaded_b{t}") for t in range(GROUP)]
        m_loaded = [sem(f"m_loaded{i}") for i in range(2)]
        m_hi_ready = sem("m_hi_ready")
        m_lo_ready = sem("m_lo_ready")
        wo_pe = sem("wo_pe")
        wo_added = sem("wo_added")
        squared = sem("squared_b")
        ln_done = sem("ln_done_b")
        rstd_ready = sem("rstd_ready_b")
        h2_ready = sem("h2_ready")
        h2_turned = sem("h2_turned")
        h2s_ready = sem("h2s_ready")
        h2_hi_ready = sem("h2_hi_ready")
        h2_lo_ready = sem("h2_lo_ready")
        w_loaded = [sem(f"w_loaded{c}") for c in range(PER)]
        w_hi_ready = [sem(f"w_hi_ready{c}") for c in range(PER)]
        w_lo_ready = [sem(f"w_lo_ready{c}") for c in range(PER)]
        wd_loaded = sem("wd_loaded")
        wd_hi_ready = sem("wd_hi_ready")
        wd_lo_ready = sem("wd_lo_ready")
        gate_done = [[sem(f"gate_done{c}{h}") for h in range(2)] for c in range(PER)]
        up_done = [[sem(f"up_done{c}{h}") for h in range(2)] for c in range(PER)]
        silu_done = [[sem(f"silu_done{c}{h}") for h in range(2)] for c in range(PER)]
        act_ready = [[sem(f"act_ready{c}{h}") for h in range(2)] for c in range(PER)]
        act_hi_ready = [[sem(f"act_hi_ready{c}{h}") for h in range(2)] for c in range(PER)]
        act_lo_ready = [[sem(f"act_lo_ready{c}{h}") for h in range(2)] for c in range(PER)]
        down_done = [sem(f"down_done{t}") for t in range(GROUP)]
        added = [sem(f"added{t}") for t in range(GROUP)]
        fsquared = sem("fsquared")
        fln_done = sem("fln_done")
        frstd_ready = sem("frstd_ready")
        scaled = sem("scaled")
        y_ready = sem("y_ready")
        y_stored = [sem(f"y_stored{i}") for i in range(2)]

        def blocks_of(t, gi):
            return BLOCKS * sum(1 for _, n in groups[:gi] if t < n)

        def last_in(t, n):
            return n - 1 - (n - 1 - t) % 2

        def uses(m, gi):
            return m + (gi + 1) * (USES - BLOCKS)

        block = ctx.enter_context(nc.Block())

        @block.sync
        def _(sp):
            def load_quarter(q, m):
                c = q % PER
                sp.wait_ge(w_lo_ready[c], m) if m > 0 else None
                for a in range(2):
                    half_k = slice(a * KC // 2, (a + 1) * KC // 2)
                    sp.dma_start(wraw[:, c, a].rearrange("p k i -> p (k i)").rearrange("p (k i) -> p k i", k=KC // 2),
                                 wo_dram[:, half_k, q * QC:(q + 1) * QC]).then_inc(w_loaded[c], 16)

            def load_block(b, gi):
                m = b + gi * BLOCKS
                for c in range(PER):
                    sp.wait_ge(w_lo_ready[c], uses(m, gi))
                    cols = bass.ds((b * PER + c) * P, P)
                    sp.dma_start(wraw[:, c, 0], wg_dram[:, :, cols]).then_inc(w_loaded[c], 16)
                    sp.dma_start(wraw[:, c, 1], wu_dram[:, :, cols]).then_inc(w_loaded[c], 16)
                if not (isinstance(m, int) and m == 0):
                    sp.wait_ge(wd_lo_ready, m)
                sp.dma_start(wdraw[:], wd_dram[:, bass.ds(b * PER, PER), :]).then_inc(wd_loaded, 16)

            def load_mixed(k):
                if k >= 2:
                    sp.wait_ge(m_lo_ready, k - 1)
                sp.dma_start(mraw[:, k % 2].rearrange("p k i -> p (k i)"), mixed[k]).then_inc(m_loaded[k % 2], 16)

            sp.dma_start(norm2_in[:], norm2_row.rearrange("(c p) -> c p", p=P)).then_inc(setup_loaded, 16)
            sp.dma_start(fnorm[:], final_norm.rearrange("(a n) -> a n", a=1).to_broadcast([P, D_MODEL]))\
              .then_inc(setup_loaded, 16)
            for gi, (g, n) in enumerate(groups):
                if gi == 0:
                    load_mixed(0)
                    load_quarter(0, 0)
                    for t in range(n):
                        if t > 0:
                            load_mixed(t)
                        if t == 2:
                            load_quarter(1, 0)
                        if t >= 2:
                            sp.dma_start(acc[:, t - 2, :], x_tiles[t - 2]).then_inc(x_loaded[t - 2], 16)
                    for t in range(n - 2, n):
                        sp.dma_start(acc[:, t, :], x_tiles[t]).then_inc(x_loaded[t], 16)
                    for q in range(2, QUARTERS):
                        load_quarter(q, q // PER)
                load_block(0, gi)
                with sp.Fori(1, BLOCKS) as b:
                    load_block(b, gi)
                n_next = groups[gi + 1][1] if gi + 1 < len(groups) else 0
                if n_next:
                    for q in range(2):
                        load_quarter(q, (gi + 1) * USES)
                    load_mixed(g + n)
                    load_mixed(g + n + 1)
                for t in range(n + 1):
                    if 2 <= t + 2 < n_next:
                        load_mixed(g + n + t + 2)
                    if t > 0:
                        sp.wait_ge(y_ready, g + t)
                        sp.dma_start(y_tiles[g + t - 1], y_out[:, (g + t - 1) % 2]).then_inc(y_stored[(g + t - 1) % 2], 16)
                        if t - 1 < n_next:
                            sp.dma_start(acc[:, t - 1, :], x_tiles[g + n + t - 1]).then_inc(x_loaded[t - 1], 16)
                for q in range(2, QUARTERS if n_next else 0):
                    load_quarter(q, (gi + 1) * USES + q // PER)
            for i in range(2):
                sp.wait_ge(y_stored[i], 16 * ((TILES + 1 - i) // 2))

        @block.gpsimd
        def _(pool):
            pool.memset(eps[:], EPS).then_inc(zeroed, 1)
            pool.memset(ident[:], 0.0).then_inc(zeroed, 1)
            pool.wait_ge(zeroed, 2)
            pool.affine_select(out=ident[:], in_=ident[:], compare_op=ALU.not_equal, fill=1.0, base=0,
                               pattern=[[-1, P]], channel_multiplier=1).then_inc(ident_ready, 1)

        @block.scalar
        def _(act_e):
            def split_columns(c, m, used=None, count=0):
                act_e.wait_ge(w_loaded[c], (m + 1) * 32)
                if used is not None:
                    act_e.wait_ge(used, count)
                act_e.activation(w_hi[:, c], wraw[:, c], ACT.Copy).then_inc(w_hi_ready[c], 1)

            def split_rows(m):
                act_e.wait_ge(wd_loaded, (m + 1) * 16)
                act_e.activation(wd_hi[:], wdraw[:], ACT.Copy).then_inc(wd_hi_ready, 1)

            def hidden(c, h, m, half):
                act_e.wait_ge(gate_done[c][h], m + 1)
                act_e.activation(gate_act[:, h, 0:half], gate_ps[h][:, 0:half], ACT.Silu)\
                     .then_inc(silu_done[c][h], 1)
                act_e.wait_ge(act_ready[c][h], m + 1)
                act_e.activation(act_hi[:, c, h * half:(h + 1) * half], act[:, h, 0:half], ACT.Copy)\
                     .then_inc(act_hi_ready[c][h], 1)

            def split_mixed(gi, g, t):
                k = g + t
                act_e.wait_ge(m_loaded[k % 2], 16 * (k // 2 + 1))
                if gi > 0 and t == 0:
                    act_e.wait_ge(up_done[PER - 1][1], gi * BLOCKS)
                act_e.activation(h2_hi[:, :, t * P:(t + 1) * P], mraw[:, k % 2], ACT.Copy).then_inc(m_hi_ready, 1)

            def exp_and_ln():
                act_e.preload_act_table_set("natural_log_exp_and_others")

            def factor(t, count, sums, logs, factors, squared_, ln_, ready):
                own = slice(t, t + 1)
                act_e.activation(squares[:], acc[:, t, :], ACT.Square, accum_out=sums[:, own]).then_inc(squared_, 1)
                act_e.wait_ge(squared_, count)
                act_e.activation(logs[:, own], sums[:, own], ACT.Ln, bias=eps[:], scale=1.0 / D_MODEL).then_inc(ln_, 1)
                act_e.wait_ge(ln_, count)
                act_e.activation(factors[:, own], logs[:, own], ACT.Exp, scale=-0.5).then_inc(ready, 1)

            act_e.wait_ge(zeroed, 1)
            split_mixed(0, 0, 0)
            split_columns(0, 0)
            exp_and_ln()
            for t in range(1, 3):
                split_mixed(0, 0, t)
            split_columns(1, 0)
            for t in range(3, groups[0][1]):
                split_mixed(0, 0, t)
            for gi, (g, n) in enumerate(groups):
                half = n * P // 2
                for q in range(3):
                    split_columns(q % PER, gi * USES + 1 + q // PER, wo_pe, QUARTERS * g + (q + 1) * n)
                for t in range(n + 2):
                    if t < n:
                        act_e.wait_ge(wo_added, QUARTERS * g + (QUARTERS - 1) * n + t + 1)
                        factor(t, g + t + 1, ssum, lnv, rstd, squared, ln_done, rstd_ready)
                    if t >= 2:
                        act_e.wait_ge(h2s_ready, g + t - 1)
                        act_e.activation(h2_hi[:, :, (t - 2) * P:(t - 1) * P], h2s[:, t % 2], ACT.Copy)\
                             .then_inc(h2_hi_ready, 1)
                split_columns(1, gi * USES + 2, wo_pe, QUARTERS * (g + n))
                act_e.preload_act_table_set("silu_and_others")
                if gi > 0:
                    last_tile = groups[gi - 1][1] - 1
                    act_e.wait_ge(down_done[last_tile], blocks_of(last_tile, gi))
                split_rows(gi * BLOCKS)

                def block_of(b, ahead):
                    m = b + gi * BLOCKS
                    hidden(0, 0, m, half)
                    hidden(0, 1, m, half)
                    if ahead:
                        split_columns(0, uses(m, gi) + 1, up_done[0][1], m + 1)
                    hidden(1, 0, m, half)
                    hidden(1, 1, m, half)
                    if ahead:
                        split_columns(1, uses(m, gi) + 1, up_done[1][1], m + 1)
                        if not (isinstance(b, int) and b == BLOCKS - 1):
                            act_e.wait_ge(down_done[n - 1], b + blocks_of(n - 1, gi) + 1)
                            split_rows(m + 1)

                block_of(0, True)
                with act_e.Fori(1, BLOCKS - 1) as b:
                    block_of(b, True)
                block_of(BLOCKS - 1, gi + 1 < len(groups))
                exp_and_ln()
                n_next = groups[gi + 1][1] if gi + 1 < len(groups) else 0
                for t in range(n):
                    if t < n_next:
                        split_mixed(gi + 1, g + n, t)
                    act_e.wait_ge(added[t], blocks_of(t, gi + 1))
                    factor(t, g + t + 1, fssum, flnv, frstd, fsquared, fln_done, frstd_ready)

        @block.vector
        def _(dve):
            def split_columns(c, m):
                dve.wait_ge(w_hi_ready[c], m + 1)
                dve.tensor_tensor(w_lo[:, c], wraw[:, c], w_hi[:, c].bitcast(F32), ALU.subtract)\
                   .then_inc(w_lo_ready[c], 1)

            def split_rows(m):
                dve.wait_ge(wd_hi_ready, m + 1)
                dve.tensor_tensor(wd_lo[:], wdraw[:], wd_hi[:].bitcast(F32), ALU.subtract).then_inc(wd_lo_ready, 1)

            def hidden(c, h, m, half):
                dve.wait_ge(silu_done[c][h], m + 1)
                dve.wait_ge(up_done[c][h], m + 1)
                dve.tensor_tensor(act[:, h, 0:half], up_ps[h][:, 0:half], gate_act[:, h, 0:half], ALU.mult)\
                   .then_inc(act_ready[c][h], 1)
                dve.wait_ge(act_hi_ready[c][h], m + 1)
                dve.wait_ge(act_ready[c][h], m + 1)
                dve.tensor_tensor(act_lo[:, c, h * half:(h + 1) * half], act[:, h, 0:half],
                                  act_hi[:, c, h * half:(h + 1) * half].bitcast(F32), ALU.subtract)\
                   .then_inc(act_lo_ready[c][h], 1)

            def add_tile(t, m):
                dve.wait_ge(down_done[t], m + 1)
                if not (isinstance(m, int) and m == 0):
                    dve.wait_ge(added[t], m)
                dve.tensor_tensor(acc[:, t, :], down_ps[t % 2][:].rearrange("p a b -> p (a b)"), acc[:, t, :],
                                  ALU.add).then_inc(added[t], 1)

            def block_of(b, gi, n, ahead):
                m = b + gi * BLOCKS
                half = n * P // 2
                hidden(0, 0, m, half)
                hidden(0, 1, m, half)
                if ahead:
                    split_columns(0, uses(m, gi) + 1)
                hidden(1, 0, m, half)
                hidden(1, 1, m, half)
                if isinstance(b, int) and b == BLOCKS - 1:
                    return
                for t in range(n):
                    add_tile(t, b + blocks_of(t, gi))
                    if t == 1 and ahead:
                        split_columns(1, uses(m, gi) + 1)
                split_rows(m + 1)

            def split_mixed(g, t):
                dve.wait_ge(m_hi_ready, g + t + 1)
                dve.tensor_tensor(h2_lo[:, :, t * P:(t + 1) * P], mraw[:, (g + t) % 2],
                                  h2_hi[:, :, t * P:(t + 1) * P].bitcast(F32), ALU.subtract).then_inc(m_lo_ready, 1)

            def add_quarter(q, t, gi, g, n):
                if q == 0:
                    dve.wait_ge(x_loaded[t], 16 * (gi + 1))
                i = q * n + t
                dve.wait_ge(wo_pe, QUARTERS * g + i + 1)
                part = acc[:, t, q * QC:(q + 1) * QC]
                dve.tensor_tensor(part, wo_ps[i % 4][:, 0:QC], part, ALU.add).then_inc(wo_added, 1)

            def scale_tile(t, k):
                dve.wait_ge(rstd_ready, k + 1)
                if k >= 2:
                    dve.wait_ge(h2_turned, k - 1)
                dve.tensor_scalar(h2[:, t % 2], acc[:, t, :], rstd[:, t:t + 1], None, ALU.mult).then_inc(h2_ready, 1)

            def take_turned(t, k):
                dve.wait_ge(h2_turned, k + 1)
                if k >= 2:
                    dve.wait_ge(h2_lo_ready, k - 1)
                dve.tensor_tensor(h2s[:, t % 2], down_ps[t % 2][:].rearrange("p a (b c) -> p (a b) c", c=P),
                                  norm2[:].rearrange("p (c a) -> p c a", a=1).to_broadcast([P, KC, P]),
                                  ALU.mult).then_inc(h2s_ready, 1)

            def split_turned(t, k):
                dve.wait_ge(h2_hi_ready, k + 1)
                dve.tensor_tensor(h2_lo[:, :, t * P:(t + 1) * P], h2s[:, t % 2],
                                  h2_hi[:, :, t * P:(t + 1) * P].bitcast(F32), ALU.subtract).then_inc(h2_lo_ready, 1)

            dve.wait_ge(norm2_turned, 1)
            dve.tensor_copy(norm2[:], down_ps[0][:, 0, 0:KC]).then_inc(norm2_ready, 1)
            dve.wait_ge(norm2_ready, 1)
            dve.wait_ge(setup_loaded, 32)
            split_mixed(0, 0)
            split_columns(0, 0)
            for t in range(1, 3):
                split_mixed(0, t)
            split_columns(1, 0)
            for t in range(3, groups[0][1]):
                split_mixed(0, t)
            for gi, (g, n) in enumerate(groups):
                for q in range(QUARTERS - 1):
                    for t in range(n):
                        add_quarter(q, t, gi, g, n)
                    split_columns(q % PER, gi * USES + 1 + q // PER)
                for t in range(n + 3):
                    if t < n:
                        add_quarter(QUARTERS - 1, t, gi, g, n)
                    if 1 <= t <= n:
                        scale_tile(t - 1, g + t - 1)
                    if 2 <= t <= n + 1:
                        take_turned(t - 2, g + t - 2)
                    if t >= 3:
                        split_turned(t - 3, g + t - 3)
                split_columns(1, gi * USES + 2)
                split_rows(gi * BLOCKS)
                block_of(0, gi, n, True)
                with dve.Fori(1, BLOCKS - 1) as b:
                    block_of(b, gi, n, True)
                n_next = groups[gi + 1][1] if gi + 1 < len(groups) else 0
                block_of(BLOCKS - 1, gi, n, n_next > 0)
                for t in range(n + 1):
                    if t < n:
                        add_tile(t, BLOCKS - 1 + blocks_of(t, gi))
                    if t < n_next:
                        split_mixed(g + n, t)
                    if t == 1 and n_next:
                        split_columns(1, (gi + 1) * USES)
                    if t > 0:
                        k = g + t - 1
                        dve.wait_ge(frstd_ready, k + 1)
                        if k >= 2:
                            dve.wait_ge(y_stored[k % 2], 16 * (k // 2))
                        dve.scalar_tensor_tensor(out=y_out[:, k % 2], in0=acc[:, t - 1, :], scalar=frstd[:, t - 1:t],
                                                 in1=fnorm[:], op0=ALU.mult, op1=ALU.mult).then_inc(y_ready, 1)

        @block.tensor
        def _(pe):
            def three(out, w_h, w_l, x_h, x_l, start, stop):
                pe.matmul(out, w_h, x_h, start=start, stop=False)
                pe.matmul(out, w_h, x_l, start=False, stop=False)
                return pe.matmul(out, w_l, x_h, start=False, stop=stop)

            def past(semaphore, count):
                if not (isinstance(count, int) and count == 0):
                    pe.wait_ge(semaphore, count)

            def hidden(c, h, m, half, between=None):
                cols = slice(h * half, (h + 1) * half)
                before = (PER - 1, m) if c == 0 else (c - 1, m + 1)
                past(silu_done[before[0]][h], before[1])
                for k in range(KC):
                    last = three(gate_ps[h][:, 0:half], w_hi[:, c, 0, k], w_lo[:, c, 0, k],
                                 h2_hi[:, k, cols], h2_lo[:, k, cols], k == 0, k == KC - 1)
                last.then_inc(gate_done[c][h], 1)
                if between is not None:
                    between()
                past(act_ready[before[0]][h], before[1])
                for k in range(KC):
                    last = three(up_ps[h][:, 0:half], w_hi[:, c, 1, k], w_lo[:, c, 1, k],
                                 h2_hi[:, k, cols], h2_lo[:, k, cols], k == 0, k == KC - 1)
                last.then_inc(up_done[c][h], 1)

            def down(t, b, gi, n, m):
                half = n * P // 2
                if t >= 2:
                    pe.wait_ge(added[t - 2], b + blocks_of(t - 2, gi) + 1)
                else:
                    past(added[last_in(t, n)], b + blocks_of(last_in(t, n), gi))
                for c in range(PER):
                    for h in range(2):
                        if h * half < (t + 1) * P and (h + 1) * half > t * P:
                            pe.wait_ge(act_lo_ready[c][h], m + 1)
                for a in range(NH):
                    for c in range(PER):
                        last = three(down_ps[t % 2][:, a, :], act_hi[:, c, t * P:(t + 1) * P],
                                     act_lo[:, c, t * P:(t + 1) * P], wd_hi[:, c, a * 512:(a + 1) * 512],
                                     wd_lo[:, c, a * 512:(a + 1) * 512], c == 0, c == PER - 1)
                last.then_inc(down_done[t], 1)

            def block_of(b, g, gi, n):
                m = b + gi * BLOCKS
                half = n * P // 2
                first = isinstance(b, int) and b == 0
                for c in range(PER):
                    pe.wait_ge(w_lo_ready[c], uses(m, gi) + 1)
                    for h in range(2):
                        if first and c == 0:
                            pe.wait_ge(wo_added, QUARTERS * (g + n))
                            pe.wait_ge(h2_lo_ready, g + (-(-half // P) if h == 0 else n))
                            hidden(c, h, m, half, (lambda: turn(n - 1, g, gi)) if h == 0 else None)
                        else:
                            hidden(c, h, m, half)
                pe.wait_ge(wd_lo_ready, m + 1)
                for t in range(n):
                    down(t, b, gi, n, m)

            def wo_product(q, t, g, gi, n):
                c, i = q % PER, q * n + t
                quarter = [w[:, c].rearrange("p a k i -> p (a k i)").rearrange("p (k i) -> p k i", k=KC)
                           for w in (w_hi, w_lo)]
                if i >= 4:
                    pe.wait_ge(wo_added, QUARTERS * g + i - 3)
                elif gi > 0:
                    pe.wait_ge((silu_done if i < 2 else act_ready)[PER - 1][i % 2], gi * BLOCKS)
                if q == 0:
                    pe.wait_ge(m_lo_ready, g + t + 1)
                own = slice(t * P, (t + 1) * P)
                for k in range(KC):
                    last = three(wo_ps[i % 4][:, 0:QC], h2_hi[:, k, own], h2_lo[:, k, own],
                                 quarter[0][:, k], quarter[1][:, k], k == 0, k == KC - 1)
                last.then_inc(wo_pe, 1)

            def turn(t, g, gi):
                pe.wait_ge(h2_ready, g + t + 1)
                if t >= 2:
                    pe.wait_ge(h2s_ready, g + t - 1)
                elif gi > 0:
                    before = last_in(t, groups[gi - 1][1])
                    pe.wait_ge(added[before], blocks_of(before, gi))
                for k in range(KC):
                    last = pe.transpose(down_ps[t % 2][:, k // 4, (k % 4) * P:(k % 4 + 1) * P],
                                        h2[:, t % 2, k * P:(k + 1) * P], ident[:])
                last.then_inc(h2_turned, 1)

            pe.wait_ge(ident_ready, 1)
            pe.wait_ge(setup_loaded, 32)
            pe.transpose(down_ps[0][:, 0, 0:KC], norm2_in[:], ident[0:KC, 0:KC]).then_inc(norm2_turned, 1)
            pe.wait_ge(norm2_ready, 1)
            for gi, (g, n) in enumerate(groups):
                for q in range(QUARTERS):
                    pe.wait_ge(w_lo_ready[q % PER], gi * USES + q // PER + 1)
                    for t in range(n):
                        wo_product(q, t, g, gi, n)
                        if q == QUARTERS - 1 and t >= 2:
                            turn(t - 2, g, gi)
                turn(n - 2, g, gi)
                block_of(0, g, gi, n)
                with pe.Fori(1, BLOCKS) as b:
                    block_of(b, g, gi, n)




def stream_step(nc, t, outs, scratch):
    y_prompt, y_sample, gdn_prompt, conv_prompt, gdn_sample, conv_sample, v_sample = outs
    x_prompt = t["x_prompt"][0].rearrange("(a p) n -> a p n", p=P)
    x_sample = t["x_sample"].rearrange("b t n -> (b t) n").rearrange("(a p) n -> a p n", p=P)
    n_prompt = x_prompt.shape[0]
    weights = {k: t[k][0] for k in ("w_in", "conv_w", "a_log", "dt_bias", "gdn_norm", "gmlp_ws", "gmlp_bs",
                                    "gmlp_norm", "norm1")}
    with ExitStack() as ctx:
        shared = mix_setup(nc, ctx, weights["w_in"])
        mix_phase(nc, shared, dict(
            x=x_sample, y=scratch[n_prompt:], new_gdn=gdn_sample[0], new_conv=conv_sample[0].rearrange("b r n -> (b r) n"),
            new_v=v_sample[0].rearrange("b t n -> (b t) n"), state_gdn=t["state_gdn"][0],
            state_conv=t["state_conv"][0], **weights), True)
        mix_phase(nc, shared, dict(
            x=x_prompt, y=scratch[0:n_prompt], new_gdn=gdn_prompt[0, 0], new_conv=conv_prompt[0, 0], **weights), False)
    y_p = y_prompt[0].rearrange("(a p) n -> a p n", p=P)
    out_phase(nc, [x_prompt[i] for i in range(n_prompt)] + [x_sample[0]], scratch, t["w_o"][0], t["norm2"][0],
              t["w_gate"][0], t["w_up"][0], t["w_down"][0], t["final_norm"],
              [y_p[i] for i in range(n_prompt)] + [y_sample.rearrange("b t n -> (b t) n")])


def kernel(**inputs):
    import concourse.bacc as bacc
    import numpy as np
    from concourse.bass_utils import run_bass_kernel_spmd

    nc = bacc.Bacc("TRN2", target_bir_lowering=False, num_devices=1)
    arrays, tensors = {}, {}
    for name, value in inputs.items():
        arrays["in_" + name] = np.ascontiguousarray(value)
        tensors[name] = nc.dram_tensor("in_" + name, value.shape, F32, kind="ExternalInput").ap()
    shapes = [inputs["x_prompt"].shape, inputs["x_sample"].shape, (1, 1, H_B, DK, DV), (1, 1, CONV_W - 1, 3 * D_B),
              (1, DEC_BATCH, H_B, DK, DV), (1, DEC_BATCH, CONV_W - 1, 3 * D_B), (1, DEC_BATCH, DEC_SEQ, D_A)]
    outs = [nc.dram_tensor(f"out_{i}", shape, F32, kind="ExternalOutput").ap() for i, shape in enumerate(shapes)]
    tiles = SEQ // P + DEC_BATCH * DEC_SEQ // P
    scratch = nc.dram_tensor("mixed_tiles", (tiles, P, D_MODEL), F32, kind="Internal").ap()
    stream_step(nc, tensors, outs, scratch)
    result = run_bass_kernel_spmd(nc, [arrays], core_ids=[0]).results[0]
    return tuple(result[f"out_{i}"] for i in range(len(shapes)))
```

```python
import math
from contextlib import ExitStack

import concourse.bass as bass
from concourse import mybir

P = 128
D_MODEL = 1024
SEQ = 2048
DEC_BATCH, DEC_SEQ = 8, 16
CHUNK = 64
D_A = 512
G_A = 4
C_A = D_A // G_A
H_B = 4
DK = DV = 128
D_B = H_B * DV
CONV_W = 4
EPS = 1e-6
LEVELS = 7
LEVELS_OF = {P: 6, DEC_SEQ: 3}
COLS = 8 + G_A + 1 + CONV_W * 12
CUTS = [(2 * D_A, 2 * D_A + D_B), (2 * D_A + D_B, 2 * D_A + 2 * D_B), (2 * D_A + 2 * D_B, 2 * D_A + 3 * D_B),
        (D_A, 2 * D_A), (2 * D_A + 3 * D_B, 2 * D_A + 4 * D_B + 2 * H_B), (0, D_A)]
CUT_OF = {"q": 0, "k": 1, "v": 2, "va": 3, "z": 4, "ba": 4, "u": 5}
GROUP = 6
PER = 2
QUARTERS = 4
AHEAD_X = 3

ALU = mybir.AluOpType
ACT = mybir.ActivationFunctionType
F32 = mybir.dt.float32
F32R = mybir.dt.float32r


def mix_setup(nc, ctx, w_in_sb):
    def sb(name, shape, dt=F32):
        return ctx.enter_context(nc.sbuf_tensor(name, shape, dt))

    return dict(
        w_in=w_in_sb,
        ident=sb("ident", [P, P]),
        ones=sb("ones", [P, P]),
        upto=sb("upto", [P, P]),
        after=sb("after", [P, P]),
        link=sb("link", [P, LEVELS, P]),
        after_r=sb("after_r", [P, P], F32R),
        ones_r=sb("ones_r", [P, P], F32R),
        cols=sb("cols", [P, COLS]),
        dt_bias=sb("dt_bias_sb", [P, H_B]),
        neg_a=sb("neg_a", [P, H_B]),
        eps=sb("eps", [P, 1]),
        ln_scale=sb("ln_scale", [P, 1]),
    )


def mix_phase(nc, sh, a, sample):
    TILES = 1 if sample else a["x"].shape[0]
    KC = D_MODEL // P
    C = DEC_SEQ if sample else P
    B = P // C
    LV = LEVELS_OF[C]
    COL_U, COL_VA, COL_QKV, COL_Z, COL_BA = 0, D_A, 2 * D_A, 2 * D_A + 3 * D_B, 2 * D_A + 4 * D_B
    W = H_B * P
    tag = "_s" if sample else "_p"

    with nc.cleanup_on_exit(), ExitStack() as ctx:
        def sb(name, shape, dt=F32):
            return ctx.enter_context(nc.sbuf_tensor(name + tag, shape, dt))

        def sem(name):
            return nc.alloc_semaphore(name=name + tag)

        CIN = 12 * B * (CONV_W - 1 + C)
        xf = sb("xf", [P, D_MODEL])
        staging = sb("staging", [P, max(CIN + 4 * P + D_MODEL, H_B * B * P if sample else 0)])
        cin = staging[:, 0:CIN].rearrange("p (c b r) -> p c b r", c=12, b=B)
        conv = staging[:, CIN:CIN + 4 * P].rearrange("p (c i) -> p c i", c=4)
        h = staging[:, CIN + 4 * P:CIN + 4 * P + D_MODEL]
        if sample:
            S = staging[:, 0:H_B * B * P].rearrange("p (h b v) -> p h b v", h=H_B, b=B)
        else:
            S = sb("S", [P, H_B, B, P])[:]
        hT = sb("hT", [P, 1 if sample else 2, KC, P])
        tails = sb("tails", [P, 12, B * (CONV_W - 1)])
        act3 = [sb(f"silu_{x}", [P, H_B, P]) for x in "qkv"]
        sq_hi = [sb(f"sq_hi_{x}", [P, H_B, P], F32R) for x in "qk"]
        sq_lo = [sb(f"sq_lo_{x}", [P, H_B, P], F32R) for x in "qk"]
        z = sb("z", [P, 1 if sample else 2, H_B, P])
        u = sb("u", [P, G_A, P])
        va = sb("va", [P, D_A])
        small = sb("small", [P, 8, H_B])
        g = sb("g", [P, 2, H_B])
        beta = sb("beta", [P, 2, H_B])
        g_parts = sb("g_parts", [P, 2, H_B], F32R)
        g_upto = sb("g_upto", [P, 2, H_B, P], F32R)
        g_of = sb("g_of", [P, H_B, B]) if sample else None
        decay = sb("decay", [P, H_B, P])
        eb = sb("eb", [P, H_B, P])
        gates = sb("gates", [P, 2 * H_B + (H_B * B if sample else 0)])
        r_k = sb("r_k", [P, H_B, P])
        r_q = sb("r_q", [P, H_B, P])
        knq = sb("knq", [P, 3 if sample else 2, H_B, P])
        kn, qn = knq[:, 0], knq[:, 1]
        sq = [qn, kn]
        kq_eb = sb("kq_eb", [P, 2, H_B, P])
        k_eb, q_dec = kq_eb[:, 0], kq_eb[:, 1]
        v_rows = sb("v_rows", [P, H_B, P])
        k_dec = sb("k_dec", [P, H_B, P])
        mt = sb("mt", [P, H_B, P])
        attn = sb("attn", [P, H_B, P])
        lt = sb("lt", [P, 2, H_B, P])
        X = sb("X", [P, H_B, P])
        XT = sb("XT", [P, H_B, P])
        LXs = sb("LX", [P, LV, H_B, P])
        LX = [LXs[:, l] for l in range(LV)]
        tail_rows = knq[0:B * (CONV_W - 1)].rearrange("p a h i -> p (a h i)") if sample else \
            staging[0:CONV_W - 1, CIN:CIN + 12 * P]
        delta = XT
        ya = decay
        sq_o = X
        o_norm = eb
        yT = xf[:].rearrange("p (c i) -> p c i", c=KC) if sample else sb("yT", [P, KC, P])[:]
        ssum = sb("ssum_m", [P, 1])
        rstd = sb("rstd_m", [P, 1])
        ws_in = q_dec
        wsT = sb("wsT", [P, G_A, P])
        bs = sb("bs", [P, G_A, P])
        if sample:
            rows_in = sb("rows_in", [COLS, P])
            a_log = sb("a_log", [P, H_B])
            conv_in = tail_rows
            stream = sb("stream", [P, B])
            same = sb("same", [P, P])
            rest_T = knq[:, 2]
            delta_of = [hT[:, 0], knq[:, 0:2].rearrange("p a h i -> p (a h) i")]
            bs_in = act3[2]

        def bank(name):
            return ctx.enter_context(nc.psum_tensor(name + tag, [P, 512], F32))

        pr = [bank("pr0"), bank("pr1")]
        gb = [bank(f"gb{i}") for i in range(5)]
        gs = bank("gs")
        state_banks = [pr, gb[0:2]]
        ks_qs = [gb[i][:].rearrange("p (h a i) -> p h a i", a=2, i=P) for i in (2, 3)]
        heads = [x[:].rearrange("p (h i) -> p h i", h=H_B) for x in gb]

        o_views = [(slice(2 * i, 2 * i + 2), x[:, :, 1]) for i, x in enumerate(ks_qs)] if sample else \
            [(slice(0, H_B), heads[2])]

        tail_banks = pr + [gs]

        names = """ahead_loaded set_loaded set_masks ws_zeroed ident_ready
            rows_turned cols_ready a_exp a_ready ws_turned ws_copied ws_ready bs_ready
            cin_turned cin_ready ws_loaded states_in x_loaded squared ln_x rstd_ready h_ready h_turned hT_ready
            ba_done xa_ready eb_raw nax_ready ex_ready lnx_ready sp_ready g_ready b1_ready beta_ready
            g_split g_rest g_upto_ready g_of_ready
            va_pe z_pe u_pe va_done z_done u_done
            decay_pe eb_pe small_pe ssk_pe ssq_pe gates_ready decay_exp decay_ready eb_ready
            ln_k rk_ready ln_q rq_ready kn_ready qn_ready q_dec_ready masks_r
            v_turned k_turned kk_pe qk_pe v_rows_ready k_eb_ready k_dec_ready mt_ready attn_ready
            xt_neg xt_ready x_turned x_ready
            sa_pe ya_bias ya_mul sq_a sq_a_hi sq_a_lo ssa_pe lx_zeroed ln_a ra_ready ya_ready
            ks_pe rest_T_ready rest_turned rest_ready delta_pe delta_ready o_pe sq_o_ready sso_pe ln_o ro_ready
            o_norm_ready y_ready s_pe s_ready y_stored va_stored s_stored
            tail_ready tail_turned rows_ready rows_stored""".split()
        s = {x: sem(x) for x in names}
        qkv_pe = [sem(f"{x}_pe") for x in "qkv"]
        raw = [sem(f"raw_{x}") for x in "qkv"]
        tap = [sem(f"taps_{x}") for x in "qkv"]
        head_kept = [sem(f"head_kept_{x}") for x in "qkv"]
        lt_ready, lx_pe, lx_ready = sem("lt_ready"), sem("lx_pe"), sem("lx_ready")
        xlx_pe, xlxT_pe, x_new, xT_new = sem("xlx_pe"), sem("xlxT_pe"), sem("x_new"), sem("xT_new")
        silu = [sem(f"silu_done_{x}") for x in "qkv"]
        sq_ready = [sem(f"sq_ready_{x}") for x in "qk"]
        sq_hi_ready = [sem(f"sq_hi_ready_{x}") for x in "qk"]
        sq_lo_ready = [sem(f"sq_lo_ready_{x}") for x in "qk"]
        w_cut = [sem(f"w_cut{i}") for i in range(len(CUTS))] if sample else []
        mask_step = sem("mask_step")
        if sample:
            dm_ready, sh_pe, sh_ready = sem("dm_ready"), sem("sh_pe"), sem("sh_ready")

        def past(eng, semaphore, count):
            if not (isinstance(count, int) and count <= 0):
                eng.wait_ge(semaphore, count)

        def levels(m, l):
            return m * LV + l + 1

        def halves(x, l, s_):
            return x.rearrange("p h (n s r) -> p (h n) s r", s=2, r=2 << l)[:, :, s_, :]

        def half_bank(bank_, l):
            return bank_[:, 0:W // 2].rearrange("p (n r) -> p n r", r=2 << l)

        def over_heads(mask):
            return mask.rearrange("p (a i) -> p a i", a=1).to_broadcast([P, H_B, P])

        block = ctx.enter_context(nc.Block())

        @block.sync
        def _(sp):
            n_set = 0
            if sample:
                sp.dma_start(xf[:], a["x"][0]).then_inc(s["x_loaded"], 16)
                sp.dma_start(rows_in[0:8], a["norm1"].rearrange("(c p) -> c p", p=P)).then_inc(s["set_loaded"], 16)
                sp.dma_start(rows_in[8:12], a["gmlp_norm"].rearrange("(c p) -> c p", p=P)).then_inc(s["set_loaded"], 16)
                sp.dma_start(rows_in[12:13], a["gdn_norm"].rearrange("(c p) -> c p", p=P)).then_inc(s["set_loaded"], 16)
                sp.dma_start(rows_in[13:COLS], a["conv_w"].rearrange("i (c p) -> (i c) p", p=P)).then_inc(s["set_loaded"], 16)
                for dst, name in ((sh["dt_bias"], "dt_bias"), (a_log, "a_log")):
                    sp.dma_start(dst[:], a[name].rearrange("(a n) -> a n", a=1).to_broadcast([P, H_B]))\
                      .then_inc(s["set_loaded"], 16)
                sp.dma_start(conv_in[:], a["state_conv"].rearrange("b r n -> (b r) n")).then_inc(s["set_loaded"], 16)
                sp.dma_start(bs_in[:], a["gmlp_bs"].rearrange("(a g) i -> a g i", a=1).to_broadcast([P, G_A, P]))\
                  .then_inc(s["set_loaded"], 16)
                n_set = 8
                w_dram = a["w_in"].rearrange("(c p) n -> p c n", p=P)
                for i, (lo, hi) in enumerate(CUTS):
                    if i == 1:
                        sp.wait_ge(s["ws_zeroed"], 1)
                        for b in range(B):
                            sp.dma_start(ws_in[b * C:(b + 1) * C, :, b * C:(b + 1) * C],
                                         a["gmlp_ws"][:, 0:C, 0:C].rearrange("g i j -> i g j")).then_inc(s["ws_loaded"], 16)
                    sp.dma_start(sh["w_in"][:, :, lo:hi], w_dram[:, :, lo:hi]).then_inc(w_cut[i], 16)
                sp.wait_ge(s["tail_ready"], 1)
                sp.wait_ge(silu[2], 1)
                sp.wait_ge(s["h_turned"], 2)
                for h_ in range(H_B):
                    sp.dma_start(S[:, h_], a["state_gdn"][:, h_].rearrange("b k v -> k b v")).then_inc(s["states_in"], 16)
            else:
                sp.dma_start(xf[:], a["x"][0]).then_inc(s["x_loaded"], 16)
                sp.dma_start(ws_in[:], a["gmlp_ws"].rearrange("g i j -> i g j")).then_inc(s["set_loaded"], 16)
                sp.dma_start(bs[:], a["gmlp_bs"].rearrange("(a g) i -> a g i", a=1).to_broadcast([P, G_A, P]))\
                  .then_inc(s["set_loaded"], 16)
                sp.wait_ge(s["h_ready"], 1)
                sp.dma_start(xf[:], a["x"][1]).then_inc(s["x_loaded"], 16)

            def store_tails():
                sp.wait_ge(s["rows_ready"], 3)
                sp.dma_start(a["new_conv"], tail_rows[:]).then_inc(s["rows_stored"], 16)

            def tile(m, ahead):
                if ahead:
                    sp.wait_ge(s["h_ready"], m + 2)
                    sp.dma_start(xf[:], a["x"][m + 2] if isinstance(m, int) else
                                 a["x"][bass.ds(m + 2, 1)].rearrange("a p n -> (a p) n")).then_inc(s["x_loaded"], 16)
                sp.wait_ge(s["y_ready"], m + 1)
                sp.wait_ge(s["ya_ready"], m + 1)
                dst = a["y"][m] if isinstance(m, int) else a["y"][bass.ds(m, 1)].rearrange("a p n -> (a p) n")
                sp.dma_start(dst, yT[:].rearrange("p c i -> p (c i)")).then_inc(s["y_stored"], 16)

            if sample:
                sp.wait_ge(s["va_done"], 1)
                sp.dma_start(a["new_v"], va[:]).then_inc(s["va_stored"], 16)
                for h_ in range(H_B):
                    sp.wait_ge(sh_ready, h_ + 1)
                    sp.dma_start(a["new_gdn"][:, h_].rearrange("b k v -> k b v"), S[:, h_]).then_inc(s["s_stored"], 16)
                tile(0, False)
                sp.wait_ge(s["va_stored"], 16)
            else:
                tile(0, True)
                with sp.Fori(1, TILES - 3, 2) as m:
                    tile(m, True)
                    tile(m + 1, True)
                tile(TILES - 3, True)
                tile(TILES - 2, False)
                sp.wait_ge(s["u_pe"], TILES)
                sp.wait_ge(s["y_stored"], 16 * (TILES - 1))
                for dst, src in a["ahead"]:
                    sp.dma_start(dst, src).then_inc(s["ahead_loaded"], 16)
                store_tails()
                sp.wait_ge(s["s_ready"], TILES)
                sp.dma_start(a["new_gdn"].rearrange("h k v -> k h v"), S[:, :, 0, :]).then_inc(s["s_stored"], 16)
                tile(TILES - 1, False)
            if sample:
                store_tails()
            if not sample:
                sp.wait_ge(s["ahead_loaded"], 16 * len(a["ahead"]))
            sp.wait_ge(s["y_stored"], 16 * TILES)
            sp.wait_ge(s["s_stored"], 16 * H_B if sample else 16)
            sp.wait_ge(s["rows_stored"], 16)

        @block.gpsimd
        def _(pool):
            steps = [0]

            def step(inst):
                inst.then_inc(mask_step, 1)
                steps[0] += 1
                pool.wait_ge(mask_step, steps[0])

            def keep(view, pattern, base, per_partition, op=ALU.is_ge):
                step(pool.affine_select(out=view, in_=view, compare_op=op, fill=0.0, base=base, pattern=pattern,
                                        channel_multiplier=per_partition))

            if sample:
                pool.memset(ws_in[:], 0.0).then_inc(s["ws_zeroed"], 1)
                step(pool.memset(sh["eps"][:], EPS))
                step(pool.memset(sh["ln_scale"][:], -0.5 * math.log(DK)))
                step(pool.memset(sh["ones"][:], 1.0))
                step(pool.memset(sh["ident"][:], 1.0))
                keep(sh["ident"][:], [[-1, P]], 0, 1)
                keep(sh["ident"][:], [[1, P]], 0, -1)
                pool.engine_nop().then_inc(s["ident_ready"], 1)
                step(pool.memset(same[:], 1.0))
                v = same[:].rearrange("p (b r) -> p b r", r=C)
                keep(v, [[-C, B], [0, C]], 0, 1)
                keep(v, [[C, B], [0, C]], C - 1, -1)
                step(pool.memset(stream[:], 1.0))
                keep(stream[:], [[-C, B]], 0, 1)
                keep(stream[:], [[C, B]], C - 1, -1)
                step(pool.memset(sh["link"][:], 0.0))
                for l in range(LEVELS):
                    b = 1 << l
                    v = sh["link"][:, l, :].rearrange("p (n s r) -> p n s r", s=2, r=b)[:, :, 1, :]
                    step(pool.memset(v, 1.0))
                    keep(v, [[-2 * b, P // (2 * b)], [0, b]], 0, 1)
                    keep(v, [[2 * b, P // (2 * b)], [0, b]], b - 1, -1)
            for t_, pat, mul, op in ((sh["upto"], [[1, P]], -1, ALU.is_ge), (sh["after"], [[-1, P]], 1, ALU.is_gt)):
                if sample:
                    step(pool.tensor_copy(t_[:], same[:]))
                else:
                    step(pool.memset(t_[:], 1.0))
                keep(t_[:], pat, 0, mul, op)
            if not sample:
                step(pool.memset(cin[:, :, :, 0:CONV_W - 1], 0.0))
                step(pool.memset(S[:], 0.0))
            pool.memset(small[:], 0.0).then_inc(s["set_masks"], 1)
            pool.memset(LXs[:], 0.0).then_inc(s["lx_zeroed"], 1)

            def tile(m):
                for l in range(LV):
                    pool.wait_ge(s["mt_ready"], m + 1)
                    if l >= 2:
                        pool.wait_ge(lx_pe, levels(m, l - 2))
                    elif not sample:
                        past(pool, lx_pe, levels(m, l - 2))
                    pool.tensor_tensor(lt[:, l % 2], mt[:], over_heads(sh["link"][:, l + 1, :]), ALU.mult)\
                        .then_inc(lt_ready, 1)

            if sample:
                tile(0)
            else:
                tile(0)
                with pool.Fori(1, TILES - 3, 2) as m:
                    tile(m)
                    tile(m + 1)
                for m in range(TILES - 3, TILES):
                    tile(m)

        @block.scalar
        def _(act):
            def exp_and_ln():
                act.preload_act_table_set("natural_log_exp_and_others")

            def front(m):
                act.wait_ge(s["x_loaded"], 16 * (m + 1))
                past(act, s["h_turned"], 2 * m)
                act.activation(h[:], xf[:], ACT.Square, accum_out=ssum[:]).then_inc(s["squared"], 1)
                act.wait_ge(s["squared"], m + 1)
                act.activation(rstd[:], ssum[:], ACT.Ln, bias=sh["eps"][:], scale=1.0 / D_MODEL).then_inc(s["ln_x"], 1)
                act.wait_ge(s["ln_x"], m + 1)
                act.activation(rstd[:], rstd[:], ACT.Exp, scale=-0.5).then_inc(s["rstd_ready"], 1)

            def gates_raw(m):
                act.wait_ge(s["ba_done"], m + 1)
                past(act, s["b1_ready"], m)
                act.activation(small[:, 0, :], gs[:, 0:H_B], ACT.Exp, scale=-1.0).then_inc(s["eb_raw"], 1)
                act.wait_ge(s["nax_ready"], m + 1)
                act.activation(small[:, 3, :], small[:, 2, :], ACT.Exp).then_inc(s["ex_ready"], 1)
                act.wait_ge(s["ex_ready"], m + 1)
                act.activation(small[:, 4, :], small[:, 3, :], ACT.Ln, bias=1.0).then_inc(s["lnx_ready"], 1)

            def keep_raw(j, m):
                act.wait_ge(qkv_pe[j], m + 1)
                if sample:
                    act.wait_ge(s["bs_ready"], 1)
                else:
                    past(act, head_kept[j], m)
                for c in range(4):
                    last = act.activation(cin[:, 4 * j + c, :, CONV_W - 1:],
                                          pr[j % 2][:, c * P:(c + 1) * P].rearrange("p (b r) -> p b r", b=B), ACT.Copy)
                last.then_inc(raw[j], 1)

            def silu_of(j, m):
                act.wait_ge(tap[j], (m + 1) * CONV_W)
                past(act, [s["qn_ready"], s["kn_ready"], s["v_turned"]][j], m)
                act.activation(act3[j][:], conv[:], ACT.Silu).then_inc(silu[j], 1)
                if j < 2:
                    act.wait_ge(silu[j], m + 1)
                    past(act, [s["ssq_pe"], s["ssa_pe"]][j], m)
                    past(act, s["qk_pe"], m)
                    past(act, s["q_dec_ready"], m)
                    act.activation(sq[j], act3[j][:], ACT.Square).then_inc(sq_ready[j], 1)
                    act.activation(sq_hi[j][:], act3[j][:], ACT.Square).then_inc(sq_hi_ready[j], 1)

            def gelu_v(m):
                act.wait_ge(s["va_pe"], m + 1)
                past(act, s["sa_pe"], m)
                act.activation(va[:], pr[1][:], ACT.Gelu_apprx_tanh).then_inc(s["va_done"], 1)

            def silu_z(m, par):
                act.wait_ge(s["z_pe"], m + 1)
                past(act, s["y_ready"], m - 1)
                act.activation(z[:, par], pr[0][:].rearrange("p (c i) -> p c i", i=P), ACT.Silu).then_inc(s["z_done"], 1)

            def gelu_u(m):
                act.wait_ge(s["u_pe"], m + 1)
                past(act, s["ya_mul"], m)
                act.activation(u[:], pr[1][:].rearrange("p (c i) -> p c i", i=P), ACT.Gelu_apprx_tanh)\
                   .then_inc(s["u_done"], 1)

            def rsqrt(dst, src, count, ln_sem, ready, m, scale, bias):
                act.wait_ge(count, m + 1)
                act.activation(dst[:], src, ACT.Ln, bias=sh["eps"][:], scale=scale).then_inc(ln_sem, 1)
                act.wait_ge(ln_sem, m + 1)
                if bias is None:
                    act.activation(dst[:], dst[:], ACT.Exp, scale=-0.5).then_inc(ready, 1)
                else:
                    act.activation(dst[:], dst[:], ACT.Exp, scale=-0.5, bias=bias).then_inc(ready, 1)

            def decays(m):
                act.wait_ge(s["decay_pe"], m + 1)
                past(act, s["ya_ready"], m)
                act.activation(decay[:], heads[0], ACT.Exp).then_inc(s["decay_exp"], 1)
                act.wait_ge(s["eb_pe"], m + 1)
                past(act, s["y_ready"], m)
                act.activation(eb[:], heads[1], ACT.Exp).then_inc(s["eb_ready"], 1)
                act.wait_ge(s["small_pe"], m + 1)
                past(act, s["s_ready"], m)
                n = gates.shape[1]
                act.activation(gates[:], gs[:, 16:16 + n], ACT.Exp).then_inc(s["gates_ready"], 1)
                past(act, s["kn_ready"], m)
                past(act, s["o_norm_ready"], m)
                rsqrt(r_k, heads[3], s["ssk_pe"], s["ln_k"], s["rk_ready"], m, 1.0, None)
                past(act, s["ya_ready"], m)
                rsqrt(r_q, heads[2], s["ssq_pe"], s["ln_q"], s["rq_ready"], m, 1.0, sh["ln_scale"][:])

            def v_and_x(m):
                if not sample:
                    act.wait_ge(s["v_turned"], m + 1)
                    past(act, s["delta_pe"], m)
                    act.activation(v_rows[:], heads[0], ACT.Copy).then_inc(s["v_rows_ready"], 1)
                act.wait_ge(s["x_turned"], m + 1)
                act.activation(X[:], heads[4], ACT.Copy).then_inc(s["x_ready"], 1)

            def level(l, m):
                act.wait_ge(lx_pe, levels(m, l))
                act.activation(halves(LX[l], l, 0), half_bank(gb[0], l), ACT.Copy).then_inc(lx_ready, 1)

            def gmlp_square(m):
                act.wait_ge(s["ya_mul"], m + 1)
                act.wait_ge(s["ssk_pe"], m + 1)
                act.wait_ge(s["qk_pe"], m + 1)
                act.activation(sq[1], ya[:], ACT.Square).then_inc(s["sq_a"], 1)
                act.activation(sq_hi[1][:], ya[:], ACT.Square).then_inc(s["sq_a_hi"], 1)

            def scan(m, par):
                if sample:
                    act.wait_ge(s["rest_turned"], m + 1)
                    act.activation(v_rows[:], heads[0], ACT.Copy).then_inc(s["rest_ready"], 1)
                act.wait_ge(s["delta_pe"], m + 1)
                for h_ in range(H_B):
                    last = act.activation(delta[:, h_], heads[1][:, h_], ACT.Copy, scale=beta[:, par, h_:h_ + 1])
                last.then_inc(s["delta_ready"], 1)

            def out(m):
                act.wait_ge(s["o_pe"], m + 1)
                act.wait_ge(lx_pe, levels(m, LV - 1))
                for two, x in o_views:
                    last = act.activation(sq_o[:, two], x, ACT.Square)
                last.then_inc(s["sq_o_ready"], 1)
                act.wait_ge(s["kn_ready"], m + 1)
                rsqrt(r_k, heads[4], s["sso_pe"], s["ln_o"], s["ro_ready"], m, 1.0 / DV, None)

            def tile(m, par, project, fronts):
                exp_and_ln()
                decays(m)
                if project:
                    gates_raw(m + 1)
                v_and_x(m)
                if isinstance(m, int) and m == 0:
                    act.wait_ge(s["lx_zeroed"], 1)
                if fronts:
                    front(m + 2)
                if project:
                    keep_raw(0, m + 1)
                for l in range(LV):
                    level(l, m)
                    if l == 0:
                        gmlp_square(m)
                        if project:
                            keep_raw(1, m + 1)
                    if l == 2:
                        act.wait_ge(s["kn_ready"], m + 1)
                        act.wait_ge(s["qn_ready"], m + 1)
                        rsqrt(r_q, heads[4], s["ssa_pe"], s["ln_a"], s["ra_ready"], m, 1.0 / C_A, None)
                        if project:
                            silu_of(0, m + 1)
                            keep_raw(2, m + 1)
                    if l == 3 and project:
                        silu_of(1, m + 1)
                    elif l == 3 and not sample:
                        take_tails()
                    if l == 4 and project:
                        gelu_v(m + 1)
                scan(m, par)
                if project:
                    silu_of(2, m + 1)
                    silu_z(m + 1, 1 - par)
                exp_and_ln()
                out(m)
                if project:
                    gelu_u(m + 1)

            def take_tails():
                act.wait_ge(s["tail_turned"], 1)
                for j in range(3):
                    act.activation(tail_rows[:, j * D_B:(j + 1) * D_B], tail_banks[j][0:B * (CONV_W - 1), :], ACT.Copy)\
                       .then_inc(s["rows_ready"], 1)

            def project_alone(m, par):
                for j in range(3):
                    keep_raw(j, m)
                    silu_of(j, m)
                gelu_v(m)
                silu_z(m, par)
                gelu_u(m)

            if sample:
                act.wait_ge(s["set_loaded"], 16 * 8)
                act.activation(sh["neg_a"][:], a_log[:], ACT.Exp).then_inc(s["a_exp"], 1)
                act.wait_ge(s["ident_ready"], 1)
                exp_and_ln()
                front(0)
                for j in range(3):
                    keep_raw(j, 0)
                    silu_of(j, 0)
                gelu_v(0)
                silu_z(0, 0)
                exp_and_ln()
                act.wait_ge(s["set_masks"], 1)
                gates_raw(0)
                gelu_u(0)
                tile(0, 0, False, False)
            else:
                exp_and_ln()
                front(0)
                act.wait_ge(s["set_masks"], 1)
                gates_raw(0)
                front(1)
                project_alone(0, 0)
                tile(0, 0, True, True)
                with act.Fori(1, TILES - 3, 2) as m:
                    tile(m, 1, True, True)
                    tile(m + 1, 0, True, True)
                tile(TILES - 3, 1, True, True)
                tile(TILES - 2, 0, True, False)
                tile(TILES - 1, 1, False, False)
            if sample:
                act.wait_ge(sh_pe, H_B)
                take_tails()

        @block.vector
        def _(dve):
            def front(m):
                dve.wait_ge(s["rstd_ready"], m + 1)
                dve.tensor_scalar(h[:], xf[:], rstd[:, 0:1], None, ALU.mult).then_inc(s["h_ready"], 1)

            def h_columns(i, m, par):
                dve.wait_ge(s["h_turned"], 2 * m + i + 1)
                if i == 0:
                    past(dve, s["u_pe"], m - 1)
                dve.tensor_tensor(hT[:, par, 4 * i:4 * i + 4], pr[0][:].rearrange("p (c i) -> p c i", i=P),
                                  sh["cols"][:, 4 * i:4 * i + 4].rearrange("p (c a) -> p c a", a=1)
                                  .to_broadcast([P, 4, P]), ALU.mult).then_inc(s["hT_ready"], 1)

            def gates_raw(m, par):
                dve.wait_ge(s["eb_raw"], m + 1)
                dve.tensor_tensor(small[:, 1, :], gs[:, H_B:2 * H_B], sh["dt_bias"][:], ALU.add).then_inc(s["xa_ready"], 1)
                dve.wait_ge(s["xa_ready"], m + 1)
                dve.scalar_tensor_tensor(out=small[:, 2, :], in0=small[:, 1, :], scalar=-1.0, in1=small[:, 1, :],
                                         op0=ALU.mult, op1=ALU.min).then_inc(s["nax_ready"], 1)
                dve.wait_ge(s["eb_raw"], m + 1)
                dve.tensor_scalar(small[:, 5, :], small[:, 0, :], 1.0, None, ALU.add).then_inc(s["b1_ready"], 1)
                dve.wait_ge(s["b1_ready"], m + 1)
                past(dve, s["delta_ready"], m - 1)
                dve.reciprocal(beta[:, par, :], small[:, 5, :]).then_inc(s["beta_ready"], 1)
                dve.wait_ge(s["lnx_ready"], m + 1)
                dve.scalar_tensor_tensor(out=small[:, 6, :], in0=small[:, 1, :], scalar=0.0, in1=small[:, 4, :],
                                         op0=ALU.max, op1=ALU.add).then_inc(s["sp_ready"], 1)
                dve.wait_ge(s["sp_ready"], m + 1)
                past(dve, s["small_pe"], m - 1)
                dve.tensor_tensor(g[:, par, :], small[:, 6, :], sh["neg_a"][:], ALU.mult).then_inc(s["g_ready"], 1)

            def gates_spread(m, par):
                def wide(x):
                    return x.bitcast(F32).rearrange("p (h a) -> p h a", a=1).to_broadcast([P, H_B, P])

                dve.wait_ge(s["g_ready"], m + 1)
                dve.tensor_copy(g_parts[:, 0], g[:, par, :]).then_inc(s["g_split"], 1)
                dve.wait_ge(s["g_split"], m + 1)
                dve.tensor_tensor(g_parts[:, 1], g[:, par, :], g_parts[:, 0].bitcast(F32), ALU.subtract)\
                   .then_inc(s["g_rest"], 1)
                dve.wait_ge(s["g_rest"], m + 1)
                past(dve, s["eb_pe"], m)
                past(dve, s["decay_pe"], m)
                for i in range(2):
                    last = dve.tensor_tensor(g_upto[:, i], over_heads(sh["upto"][:]), wide(g_parts[:, i]), ALU.mult)
                last.then_inc(s["g_upto_ready"], 1)
                if sample:
                    dve.tensor_tensor(g_of[:], stream[:].rearrange("p (a b) -> p a b", a=1).to_broadcast([P, H_B, B]),
                                      g[:, par, :].rearrange("p (h a) -> p h a", a=1).to_broadcast([P, H_B, B]),
                                      ALU.mult).then_inc(s["g_of_ready"], 1)

            def conv_tap(j, i, m):
                if i == 0:
                    dve.wait_ge(raw[j], m + 1)
                    if j > 0:
                        dve.wait_ge(silu[j - 1], m + 1)
                    else:
                        past(dve, silu[2], m)
                else:
                    dve.wait_ge(tap[j], m * CONV_W + i)
                for c in range(4):
                    o = conv[:, c].rearrange("p (b r) -> p b r", b=B)
                    x = cin[:, 4 * j + c, :, i:i + C]
                    w = sh["cols"][:, 13 + 12 * i + 4 * j + c:14 + 12 * i + 4 * j + c]
                    if i == 0:
                        last = dve.tensor_scalar(o, x, w, None, ALU.mult)
                    else:
                        last = dve.scalar_tensor_tensor(out=o, in0=x, scalar=w, in1=o, op0=ALU.mult, op1=ALU.add)
                last.then_inc(tap[j], 1)
                if i == CONV_W - 1 and not sample:
                    dve.wait_ge(tap[j], (m + 1) * CONV_W)
                    dve.tensor_copy(cin[:, 4 * j:4 * j + 4, 0, 0:CONV_W - 1], cin[:, 4 * j:4 * j + 4, 0, C:])\
                       .then_inc(head_kept[j], 1)

            def start(m, par):
                dve.wait_ge(s["decay_exp"], m + 1)
                dve.tensor_tensor(decay[:], decay[:], over_heads(sh["upto"][:]), ALU.mult).then_inc(s["decay_ready"], 1)
                dve.wait_ge(s["rk_ready"], m + 1)
                past(dve, s["k_turned"], m)
                past(dve, s["qk_pe"], m)
                dve.tensor_tensor(kn[:], act3[1][:], r_k[:], ALU.mult).then_inc(s["kn_ready"], 1)
                dve.wait_ge(s["rq_ready"], m + 1)
                dve.tensor_tensor(qn[:], act3[0][:], r_q[:], ALU.mult).then_inc(s["qn_ready"], 1)
                dve.wait_ge(s["qn_ready"], m + 1)
                dve.wait_ge(s["eb_ready"], m + 1)
                past(dve, s["o_pe"], m)
                dve.tensor_tensor(q_dec, qn[:], eb[:], ALU.mult).then_inc(s["q_dec_ready"], 1)
                past(dve, s["ks_pe"], m)
                dve.tensor_tensor(k_eb, kn[:], eb[:], ALU.mult).then_inc(s["k_eb_ready"], 1)

            def products(m, par):
                dve.wait_ge(s["kk_pe"], m + 1)
                dve.wait_ge(s["decay_ready"], m + 1)
                dve.wait_ge(s["beta_ready"], m + 1)
                for h_ in range(H_B):
                    last = dve.scalar_tensor_tensor(out=mt[:, h_], in0=heads[2][:, h_], scalar=beta[:, par, h_:h_ + 1],
                                                    in1=decay[:, h_], op0=ALU.mult, op1=ALU.mult)
                last.then_inc(s["mt_ready"], 1)
                dve.wait_ge(s["mt_ready"], m + 1)
                past(dve, s["s_pe"], m)
                dve.scalar_tensor_tensor(out=XT[:], in0=mt[:], scalar=-1.0, in1=over_heads(sh["link"][:, 0, :]),
                                         op0=ALU.mult, op1=ALU.mult).then_inc(s["xt_neg"], 1)
                dve.wait_ge(s["xt_neg"], m + 1)
                dve.tensor_tensor(XT[:], XT[:], over_heads(sh["ident"][:]), ALU.add).then_inc(s["xt_ready"], 1)
                dve.wait_ge(s["qk_pe"], m + 1)
                past(dve, s["o_pe"], m)
                dve.tensor_tensor(attn[:], heads[3], decay[:], ALU.mult).then_inc(s["attn_ready"], 1)
                dve.wait_ge(s["k_turned"], m + 1)
                dve.wait_ge(s["gates_ready"], m + 1)
                past(dve, s["s_pe"], m)
                for h_ in range(H_B):
                    last = dve.tensor_scalar(k_dec[:, h_], heads[1][:, h_], gates[:, h_:h_ + 1], None, ALU.mult)
                last.then_inc(s["k_dec_ready"], 1)

            def level(l, m):
                if l < LV - 1:
                    dve.wait_ge(xlx_pe, m * (LV - 1) + l + 1)
                    if l == 0:
                        dve.wait_ge(s["x_ready"], m + 1)
                    else:
                        dve.wait_ge(x_new, m * (LV - 1) + l)
                    even = halves(X[:], l, 0)
                    dve.tensor_tensor(even, even, half_bank(gb[1], l), ALU.subtract).then_inc(x_new, 1)
                dve.wait_ge(xlxT_pe, levels(m, l))
                if l == 0:
                    dve.wait_ge(s["xt_ready"], m + 1)
                else:
                    dve.wait_ge(xT_new, levels(m, l - 1))
                odd = halves(XT[:], l, 1)
                dve.tensor_tensor(odd, odd, half_bank(gb[2], l), ALU.subtract).then_inc(xT_new, 1)

            def gmlp(m):
                dve.wait_ge(s["sa_pe"], m + 1)
                past(dve, s["ya_ready"], m)
                dve.tensor_tensor(ya[:], heads[3], bs[:], ALU.add).then_inc(s["ya_bias"], 1)
                dve.wait_ge(s["ya_bias"], m + 1)
                dve.wait_ge(s["u_done"], m + 1)
                dve.tensor_tensor(ya[:], ya[:], u[:], ALU.mult).then_inc(s["ya_mul"], 1)

            def split_squares(j, m):
                dve.wait_ge(sq_ready[j], m + 1)
                dve.wait_ge(sq_hi_ready[j], m + 1)
                dve.tensor_tensor(sq_lo[j][:], sq[j], sq_hi[j][:].bitcast(F32), ALU.subtract)\
                   .then_inc(sq_lo_ready[j], 1)

            def split_gmlp_squares(m):
                dve.wait_ge(s["sq_a"], m + 1)
                dve.wait_ge(s["sq_a_hi"], m + 1)
                dve.tensor_tensor(sq_lo[1][:], sq[1], sq_hi[1][:].bitcast(F32), ALU.subtract)\
                   .then_inc(s["sq_a_lo"], 1)

            def rest(m):
                dve.wait_ge(s["ks_pe"], m + 1)
                if sample:
                    for i, x in enumerate(ks_qs):
                        two = slice(2 * i, 2 * i + 2)
                        last = dve.tensor_tensor(rest_T[:, two], act3[2][:, two], x[:, :, 0], ALU.subtract)
                    last.then_inc(s["rest_T_ready"], 1)
                else:
                    dve.wait_ge(s["v_rows_ready"], m + 1)
                    dve.tensor_tensor(v_rows[:], v_rows[:], heads[4], ALU.subtract).then_inc(s["rest_ready"], 1)

            def gmlp_out(m):
                dve.wait_ge(s["ra_ready"], m + 1)
                past(dve, s["y_stored"], 16 * m)
                for c in range(G_A):
                    last = dve.scalar_tensor_tensor(out=yT[:, c], in0=ya[:, c], scalar=sh["cols"][:, 8 + c:9 + c],
                                                    in1=r_q[:, c], op0=ALU.mult, op1=ALU.mult)
                last.then_inc(s["ya_ready"], 1)

            def state(m):
                if not sample:
                    dve.wait_ge(s["s_pe"], m + 1)
                    dve.wait_ge(s["o_pe"], m + 1)
                    dve.wait_ge(s["gates_ready"], m + 1)
                    for h_ in range(H_B):
                        last = dve.scalar_tensor_tensor(out=S[:, h_, 0], in0=S[:, h_, 0],
                                                        scalar=gates[:, H_B + h_:H_B + h_ + 1],
                                                        in1=heads[3][:, h_], op0=ALU.mult, op1=ALU.add)
                    last.then_inc(s["s_ready"], 1)
                    return
                dve.wait_ge(s["delta_ready"], 1)

                def delta_of_streams(h_):
                    if h_ >= 2:
                        dve.wait_ge(sh_pe, h_ - 1)
                    dve.tensor_tensor(delta_of[h_ % 2], delta[:, h_:h_ + 1].to_broadcast([P, B, P]),
                                      stream[:].rearrange("p (b a) -> p b a", a=1).to_broadcast([P, B, P]), ALU.mult)\
                       .then_inc(dm_ready, 1)

                delta_of_streams(0)
                for h_ in range(H_B):
                    if h_ + 1 < H_B:
                        delta_of_streams(h_ + 1)
                    dve.wait_ge(sh_pe, h_ + 1)
                    dve.wait_ge(s["o_pe"], 1)
                    for b in range(B):
                        c = 2 * H_B + h_ * B + b
                        last = dve.scalar_tensor_tensor(out=S[:, h_, b], in0=S[:, h_, b], scalar=gates[:, c:c + 1],
                                                        in1=state_banks[h_ % 2][b // 4][:, (b % 4) * P:(b % 4 + 1) * P],
                                                        op0=ALU.mult, op1=ALU.add)
                    last.then_inc(sh_ready, 1)

            def out(m, par):
                dve.wait_ge(s["ro_ready"], m + 1)
                for two, x in o_views:
                    last = dve.scalar_tensor_tensor(out=o_norm[:, two], in0=x, scalar=sh["cols"][:, 12:13],
                                                    in1=r_k[:, two], op0=ALU.mult, op1=ALU.mult)
                last.then_inc(s["o_norm_ready"], 1)
                dve.wait_ge(s["o_norm_ready"], m + 1)
                dve.wait_ge(s["z_done"], m + 1)
                dve.tensor_tensor(yT[:, G_A:], o_norm[:], z[:, par], ALU.mult).then_inc(s["y_ready"], 1)

            def tile(m, par, project, fronts):
                start(m, par)
                if project:
                    gates_raw(m + 1, 1 - par)
                products(m, par)
                gmlp(m)
                if fronts:
                    front(m + 2)
                n_taps = 3 * CONV_W
                for l in range(LV):
                    if l == 0 and not sample:
                        rest(m)
                    if l == 1:
                        split_gmlp_squares(m)
                    level(l, m)
                    for i in (2 * l, 2 * l + 1):
                        if project and i < n_taps:
                            conv_tap(i // CONV_W, i % CONV_W, m + 1)
                    if l == 3 or (LV < 4 and l == LV - 1):
                        gmlp_out(m)
                    if l == 0 and not project and not sample:
                        for j in range(3):
                            dve.wait_ge(head_kept[j], TILES)
                        dve.tensor_copy(tails[:], cin[:, :, 0, 0:CONV_W - 1]).then_inc(s["tail_ready"], 1)
                    if l in (3, 4) and project:
                        split_squares(l - 3, m + 1)
                if project:
                    gates_spread(m + 1, 1 - par)
                if sample:
                    rest(m)
                state(m)
                if fronts:
                    h_columns(0, m + 2, par)
                    h_columns(1, m + 2, par)
                out(m, par)

            if sample:
                dve.wait_ge(s["rows_turned"], 1)
                dve.tensor_copy(sh["cols"][:], gb[1][:, 0:COLS]).then_inc(s["cols_ready"], 1)
                dve.wait_ge(s["cols_ready"], 1)
            front(0)
            h_columns(0, 0, 0)
            h_columns(1, 0, 0)
            if sample:
                dve.wait_ge(s["cin_turned"], 1)
                dve.tensor_copy(cin[:, :, :, 0:CONV_W - 1],
                                gb[2][:, 0:12 * B * (CONV_W - 1)].rearrange("p (c b r) -> p c b r", c=12, b=B))\
                   .then_inc(s["cin_ready"], 1)
                dve.wait_ge(s["set_loaded"], 16 * 8)
                dve.tensor_copy(bs[:].rearrange("p g (b r) -> p g b r", b=B),
                                bs_in[:, :, 0:C].rearrange("p g (a r) -> p g a r", a=1).to_broadcast([P, G_A, B, C]))\
                   .then_inc(s["bs_ready"], 1)
                dve.wait_ge(s["a_exp"], 1)
                dve.tensor_scalar(sh["neg_a"][:], sh["neg_a"][:], -1.0, None, ALU.mult).then_inc(s["a_ready"], 1)
                dve.wait_ge(s["cin_ready"], 1)
                dve.wait_ge(s["bs_ready"], 1)
                dve.wait_ge(s["a_ready"], 1)
            dve.wait_ge(s["set_masks"], 1)
            for x, x_r in (("after", "after_r"), ("ones", "ones_r")):
                last = dve.tensor_copy(sh[x_r][:], sh[x][:])
            last.then_inc(s["masks_r"], 1)
            dve.wait_ge(s["ws_turned"], 1)
            dve.tensor_copy(wsT[:], heads[0]).then_inc(s["ws_copied"], 1)
            dve.wait_ge(s["ws_copied"], 1)
            if not sample:
                for lo in range(CHUNK, P, CHUNK):
                    last = dve.memset(wsT[lo:lo + CHUNK, :, 0:lo], 0.0)
                last.then_inc(s["ws_ready"], 1)
                dve.wait_ge(s["ws_ready"], 1)
                dve.wait_ge(s["set_loaded"], 32)
            if sample:
                for j in range(3):
                    for i in range(CONV_W):
                        conv_tap(j, i, 0)
                    if j < 2:
                        split_squares(j, 0)
                dve.tensor_copy(tails[:].rearrange("p c (b r) -> p c b r", b=B), cin[:, :, :, C:]).then_inc(s["tail_ready"], 1)
                gates_raw(0, 0)
                gates_spread(0, 0)
                tile(0, 0, False, False)
            else:
                gates_raw(0, 0)
                gates_spread(0, 0)
                front(1)
                for j in range(3):
                    for i in range(CONV_W):
                        conv_tap(j, i, 0)
                    if j < 2:
                        split_squares(j, 0)
                h_columns(0, 1, 1)
                h_columns(1, 1, 1)
                tile(0, 0, True, True)
                with dve.Fori(1, TILES - 3, 2) as m:
                    tile(m, 1, True, True)
                    tile(m + 1, 0, True, True)
                tile(TILES - 3, 1, True, True)
                tile(TILES - 2, 0, True, False)
                tile(TILES - 1, 1, False, False)

        @block.tensor
        def _(pe):
            def turn_h(i, m):
                if i == 0:
                    pe.wait_ge(s["h_ready"], m + 1)
                    past(pe, s["z_done"], m)
                else:
                    pe.wait_ge(s["hT_ready"], 2 * m + 1)
                for k in range(4 * i, 4 * i + 4):
                    last = pe.transpose(pr[0][:, (k % 4) * P:(k % 4 + 1) * P], h[:, k * P:(k + 1) * P], sh["ident"][:])
                last.then_inc(s["h_turned"], 1)

            def gate_columns(k, m, par):
                if k == 0:
                    pe.wait_ge(s["hT_ready"], 2 * m + 2)
                    past(pe, s["gates_ready"], m)
                    past(pe, s["eb_raw"], m)
                    past(pe, s["xa_ready"], m)
                last = pe.matmul(gs[:, 0:2 * H_B], hT[:, par, k], sh["w_in"][:, k, COL_BA:COL_BA + 2 * H_B],
                                 start=(k == 0), stop=(k == KC - 1))
                if k == KC - 1:
                    last.then_inc(s["ba_done"], 1)

            def columns(bank_, c, col, par, gates_of=None):
                for k in range(KC):
                    if gates_of is not None and c >= 2 and k % 2 == 1:
                        gate_columns(4 * (c - 2) + k // 2, gates_of, par)
                    last = pe.matmul(bank_[:, c * P:(c + 1) * P], sh["w_in"][:, k, col + c * P:col + (c + 1) * P], hT[:, par, k],
                                     start=(k == 0), stop=(k == KC - 1))
                return last

            def qkv_columns(j, c, m, par):
                if c == 0:
                    if j == 0:
                        pe.wait_ge(s["hT_ready"], 2 * m + 2)
                    elif j == 1:
                        past(pe, s["u_done"], m)
                    else:
                        pe.wait_ge(raw[0], m + 1)
                    if sample:
                        pe.wait_ge(w_cut[CUT_OF["qkv"[j]]], 16)
                last = columns(pr[j % 2], c, COL_QKV + j * D_B, par, m if j == 0 and not sample else None)
                if c == 3:
                    last.then_inc(qkv_pe[j], 1)

            def va_columns(part, m, par):
                if part == 0:
                    pe.wait_ge(raw[1], m + 1)
                    if sample:
                        pe.wait_ge(w_cut[CUT_OF["va"]], 16)
                for k in (2 * part, 2 * part + 1):
                    last = pe.matmul(pr[1][:], hT[:, par, k], sh["w_in"][:, k, COL_VA:COL_VA + D_A],
                                     start=(k == 0), stop=(k == KC - 1))
                if part == 3:
                    last.then_inc(s["va_pe"], 1)

            def z_columns(c, m, par):
                if c == 0:
                    pe.wait_ge(raw[2], m + 1)
                    if sample:
                        pe.wait_ge(w_cut[CUT_OF["z"]], 16)
                last = columns(pr[0], c, COL_Z, par, m if sample else None)
                if c == 3:
                    last.then_inc(s["z_pe"], 1)

            def u_columns(c, m, par):
                if c == 0:
                    pe.wait_ge(s["va_done"], m + 1)
                    if sample:
                        pe.wait_ge(w_cut[CUT_OF["u"]], 16)
                last = columns(pr[1], c, COL_U, par)
                if c == 3:
                    last.then_inc(s["u_pe"], 1)

            def over_partitions(out, mask, hi, lo):
                pe.matmul(out, sh[mask][:], hi.rearrange("p h i -> p (h i)"), start=True, stop=False)
                return pe.matmul(out, sh[mask][:], lo.rearrange("p h i -> p (h i)"), start=False, stop=True)

            def start(m, par):
                if isinstance(m, int) and m == 0:
                    pe.wait_ge(s["masks_r"], 1)
                pe.wait_ge(s["g_upto_ready"], m + 1)
                past(pe, lx_ready, m * LV)
                over_partitions(gb[0][:], "after_r", g_upto[:, 0], g_upto[:, 1]).then_inc(s["decay_pe"], 1)
                past(pe, s["delta_ready"], m)
                over_partitions(gb[1][:], "ones_r", g_upto[:, 0], g_upto[:, 1]).then_inc(s["eb_pe"], 1)
                past(pe, s["gates_ready"], m)
                pe.wait_ge(s["g_ready"], m + 1)
                for i, mask in enumerate((sh["after"], sh["ones"])):
                    last = pe.matmul(gs[:, 16 + i * H_B:16 + (i + 1) * H_B], mask[:], g[:, par, :], start=True, stop=True)
                if sample:
                    pe.wait_ge(s["g_of_ready"], 1)
                    last = pe.matmul(gs[:, 16 + 2 * H_B:16 + 2 * H_B + H_B * B], sh["ones"][:],
                                     g_of[:].rearrange("p h b -> p (h b)"), start=True, stop=True)
                last.then_inc(s["small_pe"], 1)
                pe.wait_ge(sq_lo_ready[1], m + 1)
                past(pe, s["s_ready"], m)
                over_partitions(gb[3][:], "ones_r", sq_hi[1][:], sq_lo[1][:]).then_inc(s["ssk_pe"], 1)
                pe.wait_ge(sq_lo_ready[0], m + 1)
                past(pe, s["o_norm_ready"], m)
                over_partitions(gb[2][:], "ones_r", sq_hi[0][:], sq_lo[0][:]).then_inc(s["ssq_pe"], 1)

            def products(m):
                pe.wait_ge(silu[2], m + 1)
                pe.wait_ge(s["decay_exp"], m + 1)
                if not sample:
                    for h_ in range(H_B):
                        last = pe.transpose(heads[0][:, h_], act3[2][:, h_], sh["ident"][:])
                    last.then_inc(s["v_turned"], 1)
                pe.wait_ge(s["kn_ready"], m + 1)
                pe.wait_ge(s["eb_ready"], m + 1)
                for h_ in range(H_B):
                    last = pe.transpose(heads[1][:, h_], kn[:, h_], sh["ident"][:])
                last.then_inc(s["k_turned"], 1)
                pe.wait_ge(s["ln_q"], m + 1)
                for h_ in range(H_B):
                    last = pe.matmul(heads[2][:, h_], kn[:, h_], kn[:, h_], start=True, stop=True)
                last.then_inc(s["kk_pe"], 1)
                pe.wait_ge(s["qn_ready"], m + 1)
                pe.wait_ge(s["ln_k"], m + 1)
                for h_ in range(H_B):
                    last = pe.matmul(heads[3][:, h_], kn[:, h_], qn[:, h_], start=True, stop=True)
                last.then_inc(s["qk_pe"], 1)

            def turn_x(m):
                pe.wait_ge(s["xt_ready"], m + 1)
                past(pe, s["ln_o"], m)
                for h_ in range(H_B):
                    last = pe.transpose(heads[4][:, h_], XT[:, h_], sh["ident"][:])
                last.then_inc(s["x_turned"], 1)

            def of_head(bank_, h_):
                return bank_[:, h_ * P // 2:(h_ + 1) * P // 2]

            def level_lx(l, m):
                pe.wait_ge(lt_ready, levels(m, l))
                if l > 0:
                    pe.wait_ge(x_new, m * (LV - 1) + l)
                else:
                    pe.wait_ge(s["x_ready"], m + 1)
                    if not sample:
                        pe.wait_ge(s["v_rows_ready"], m + 1)
                for h_ in range(H_B):
                    last = pe.matmul(of_head(gb[0], h_), lt[:, l % 2, h_], halves(X[:, h_:h_ + 1], l, 0),
                                     start=True, stop=True)
                last.then_inc(lx_pe, 1)

            def level_xlx(l, m):
                pe.wait_ge(lx_ready, levels(m, l))
                if l == 0:
                    pe.wait_ge(s["xt_ready"], m + 1)
                else:
                    pe.wait_ge(xT_new, levels(m, l - 1))
                if l < LV - 1:
                    if l == 0:
                        pe.wait_ge(s["k_dec_ready"], m + 1)
                    for h_ in range(H_B):
                        last = pe.matmul(of_head(gb[1], h_), XT[:, h_], halves(LX[l][:, h_:h_ + 1], l, 0),
                                         start=True, stop=True)
                    last.then_inc(xlx_pe, 1)
                for h_ in range(H_B):
                    last = pe.matmul(of_head(gb[2], h_), LX[l][:, h_], halves(XT[:, h_:h_ + 1], l, 1),
                                     start=True, stop=True)
                last.then_inc(xlxT_pe, 1)

            def gmlp(m):
                pe.wait_ge(s["va_done"], m + 1)
                pe.wait_ge(s["attn_ready"], m + 1)
                for c in range(G_A):
                    last = pe.matmul(heads[3][:, c], va[:, c * C_A:(c + 1) * C_A], wsT[:, c], start=True, stop=True)
                last.then_inc(s["sa_pe"], 1)

            def gmlp_norm(m):
                pe.wait_ge(s["sq_a_lo"], m + 1)
                pe.wait_ge(s["x_ready"] if sample else s["rest_ready"], m + 1)
                over_partitions(gb[4][:], "ones_r", sq_hi[1][:], sq_lo[1][:]).then_inc(s["ssa_pe"], 1)

            def state_part(m):
                pe.wait_ge(s["k_eb_ready"], m + 1)
                if not sample:
                    past(pe, s["s_ready"], m)
                    pe.wait_ge(s["x_ready"], m + 1)
                    for h_ in range(H_B):
                        last = pe.matmul(heads[4][:, h_], k_eb[:, h_], S[:, h_, 0], start=True, stop=True)
                    last.then_inc(s["ks_pe"], 1)
                    return
                pe.wait_ge(s["q_dec_ready"], m + 1)
                pe.wait_ge(xT_new, levels(m, LV - 1))
                pe.wait_ge(s["ya_bias"], m + 1)
                pe.wait_ge(s["states_in"], 16 * H_B)
                for h_ in range(H_B):
                    for b in range(B):
                        own = slice(b * C, (b + 1) * C)
                        last = pe.matmul(ks_qs[h_ // 2][:, h_ % 2, :, own], S[:, h_, b], kq_eb[:, :, h_, own],
                                         start=(h_ % 2 == 0 and b == 0), stop=True, skip_group_check=True)
                last.then_inc(s["ks_pe"], 1)
                pe.wait_ge(s["rest_T_ready"], 1)
                pe.wait_ge(lx_ready, levels(m, LV - 1))
                for h_ in range(H_B):
                    last = pe.transpose(heads[0][:, h_], rest_T[:, h_], sh["ident"][:])
                last.then_inc(s["rest_turned"], 1)

            def scan(m):
                pe.wait_ge(s["rest_ready"], m + 1)
                pe.wait_ge(x_new, (m + 1) * (LV - 1))
                pe.wait_ge(xT_new, levels(m, LV - 1))
                for h_ in range(H_B):
                    last = pe.matmul(heads[1][:, h_], XT[:, h_], v_rows[:, h_], start=True, stop=True)
                last.then_inc(s["delta_pe"], 1)

            def outputs(m):
                pe.wait_ge(s["delta_ready"], m + 1)
                pe.wait_ge(s["q_dec_ready"], m + 1)
                pe.wait_ge(s["attn_ready"], m + 1)
                if sample:
                    pe.wait_ge(s["rest_T_ready"], 1)
                for h_ in range(H_B):
                    if sample:
                        last = pe.matmul(ks_qs[h_ // 2][:, h_ % 2, 1], delta[:, h_], attn[:, h_], start=False,
                                         stop=True, skip_group_check=True)
                    else:
                        pe.matmul(heads[2][:, h_], delta[:, h_], attn[:, h_], start=True, stop=False)
                        last = pe.matmul(heads[2][:, h_], S[:, h_, 0], q_dec[:, h_], start=False, stop=True)
                last.then_inc(s["o_pe"], 1)

            def state(m):
                pe.wait_ge(s["k_dec_ready"], m + 1)
                if not sample:
                    pe.wait_ge(s["ya_bias"], m + 1)
                    for h_ in range(H_B):
                        last = pe.matmul(heads[3][:, h_], k_dec[:, h_], delta[:, h_], start=True, stop=True)
                    last.then_inc(s["s_pe"], 1)
                    return
                pe.wait_ge(s["u_done"], 1)
                pe.wait_ge(s["z_done"], 1)
                for h_ in range(H_B):
                    pe.wait_ge(dm_ready, h_ + 1)
                    if h_ >= 2:
                        pe.wait_ge(sh_ready, h_ - 1)
                    for i in range(2):
                        last = pe.matmul(state_banks[h_ % 2][i][:], k_dec[:, h_],
                                         delta_of[h_ % 2][:, 4 * i:4 * i + 4].rearrange("p b i -> p (b i)"),
                                         start=True, stop=True)
                    last.then_inc(sh_pe, 1)

            def out_norm(m):
                pe.wait_ge(s["sq_o_ready"], m + 1)
                pe.wait_ge(s["ln_a"], m + 1)
                pe.matmul(gb[4][:], sh["ones"][:], sq_o[:].rearrange("p h i -> p (h i)"), start=True, stop=True)\
                  .then_inc(s["sso_pe"], 1)

            def turn_tails():
                pe.wait_ge(s["tail_ready"], 1)
                for c in range(12):
                    last = pe.transpose(tail_banks[c // 4][0:B * (CONV_W - 1), (c % 4) * P:(c % 4 + 1) * P], tails[:, c],
                                        sh["ident"][:])
                last.then_inc(s["tail_turned"], 1)

            def tile(m, par, project, fronts):
                ahead = (m + 1, 1 - par)
                start(m, par)
                if project:
                    for c in range(4):
                        qkv_columns(0, c, *ahead)
                products(m)
                if project:
                    qkv_columns(1, 0, *ahead)
                    qkv_columns(1, 1, *ahead)
                turn_x(m)
                gmlp(m)
                if project:
                    qkv_columns(1, 2, *ahead)
                    qkv_columns(1, 3, *ahead)
                for l in range(LV):
                    level_lx(l, m)
                    if l == 0 and not sample:
                        state_part(m)
                    if project:
                        between(2 * l, *ahead)
                    level_xlx(l, m)
                    if l == 1:
                        gmlp_norm(m)
                    if l == 2 and not project and not sample:
                        pe.wait_ge(s["z_done"], TILES)
                        pe.wait_ge(s["u_done"], TILES)
                        pe.wait_ge(s["gates_ready"], TILES)
                        turn_tails()
                    if project:
                        between(2 * l + 1, *ahead)
                if sample:
                    state_part(m)
                if project:
                    u_columns(0, *ahead)
                scan(m)
                if project:
                    u_columns(1, *ahead)
                outputs(m)
                state(m)
                if fronts:
                    turn_h(0, m + 2)
                if project:
                    u_columns(2, *ahead)
                out_norm(m)
                if fronts:
                    turn_h(1, m + 2)
                if project:
                    u_columns(3, *ahead)

            def between(i, m, par):
                if i < 4:
                    qkv_columns(2, i, m, par)
                elif i < 8:
                    va_columns(i - 4, m, par)
                else:
                    z_columns(i - 8, m, par)

            if sample:
                pe.wait_ge(s["ident_ready"], 1)
                pe.wait_ge(s["set_loaded"], 16 * 8)
                pe.transpose(gb[1][:, 0:COLS], rows_in[:], sh["ident"][0:COLS, 0:COLS]).then_inc(s["rows_turned"], 1)
            turn_h(0, 0)
            turn_h(1, 0)
            if sample:
                n = B * (CONV_W - 1)
                for c in range(12):
                    last = pe.transpose(gb[2][:, c * n:(c + 1) * n], conv_in[:, c * P:(c + 1) * P], sh["ident"][0:n, 0:n])
                last.then_inc(s["cin_turned"], 1)
            for j in range(3):
                for c in range(4):
                    qkv_columns(j, c, 0, 0)
                if j == 0:
                    pe.wait_ge(s["ws_loaded"] if sample else s["set_loaded"], 16 * B if sample else 32)
                    for c in range(G_A):
                        last = pe.transpose(heads[0][:, c], ws_in[:, c], sh["ident"][:])
                    last.then_inc(s["ws_turned"], 1)
            for part in range(4):
                va_columns(part, 0, 0)
            for c in range(4):
                z_columns(c, 0, 0)
            for c in range(4):
                u_columns(c, 0, 0)
            if sample:
                tile(0, 0, False, False)
            else:
                turn_h(0, 1)
                turn_h(1, 1)
                tile(0, 0, True, True)
                with pe.Fori(1, TILES - 3, 2) as m:
                    tile(m, 1, True, True)
                    tile(m + 1, 0, True, True)
                tile(TILES - 3, 1, True, True)
                tile(TILES - 2, 0, True, False)
                tile(TILES - 1, 1, False, False)
            if sample:
                pe.wait_ge(sh_ready, H_B - 1)
                pe.wait_ge(s["gates_ready"], 1)
                turn_tails()


def out_buffers(region):
    KC = D_MODEL // P
    flat = region[:].rearrange("p c n -> p (c n)")
    taken, views = 0, {}
    for name, shape, axes in (
            ("acc", (GROUP, D_MODEL), "p (a b) -> p a b"),
            ("mraw", (2, KC, P), "p (a b c) -> p a b c"),
            ("wraw", (PER, 2, KC, P), "p (a b c d) -> p a b c d"),
            ("wdraw", (PER, D_MODEL), "p (a b) -> p a b"),
            ("h2", (2, D_MODEL), "p (a b) -> p a b"),
            ("h2s", (2, KC, P), "p (a b c) -> p a b c"),
            ("y_out", (2, D_MODEL), "p (a b) -> p a b"),
            ("squares", (D_MODEL,), None),
            ("fnorm", (D_MODEL,), None),
            ("gate_act", (2, GROUP * P // 2), "p (a b) -> p a b"),
            ("act", (2, GROUP * P // 2), "p (a b) -> p a b"),
            ("ident", (P,), None)):
        n = math.prod(shape)
        view = flat[:, taken:taken + n]
        if axes:
            view = view.rearrange(axes, **dict(zip("abcd", shape)))
        views[name] = view
        taken += n
    return views


def quarter_loads(wraw, w_o, q):
    KC, QC = D_MODEL // P, D_MODEL // QUARTERS
    wo_dram = w_o.rearrange("(c p) n -> p c n", p=P)
    return [(wraw[:, q % PER, i].rearrange("p k i -> p (k i)").rearrange("p (k i) -> p k i", k=KC // 2),
             wo_dram[:, i * KC // 2:(i + 1) * KC // 2, q * QC:(q + 1) * QC]) for i in range(2)]


def loads_ahead(bufs, x_tiles, mixed, w_o):
    return ([(bufs["mraw"][:, k].rearrange("p k i -> p (k i)"), mixed[k]) for k in range(2)] +
            quarter_loads(bufs["wraw"], w_o, 0) + quarter_loads(bufs["wraw"], w_o, 1) +
            [(bufs["acc"][:, t, :], x_tiles[t]) for t in range(AHEAD_X)])


def out_phase(nc, bufs, x_tiles, mixed, w_o, norm2_row, w_gate, w_up, w_down, final_norm, y_tiles):
    TILES = len(x_tiles)
    KC = D_MODEL // P
    FC = w_gate.shape[1] // P
    BLOCKS = FC // PER
    QC = D_MODEL // QUARTERS
    USES = BLOCKS + QUARTERS // PER
    NH = D_MODEL // 512
    groups = [(g, min(GROUP, TILES - g)) for g in range(0, TILES, GROUP)]

    wg_dram = w_gate.rearrange("(c p) f -> p c f", p=P)
    wu_dram = w_up.rearrange("(c p) f -> p c f", p=P)
    wd_dram = w_down.rearrange("(c p) n -> p c n", p=P)

    with nc.cleanup_on_exit(), ExitStack() as ctx:
        def sb(name, shape, dt=F32):
            return ctx.enter_context(nc.sbuf_tensor(name, shape, dt))

        def sem(name):
            return nc.alloc_semaphore(name=name)

        acc, h2, y_out, squares, mraw, h2s = (bufs[x] for x in ("acc", "h2", "y_out", "squares", "mraw", "h2s"))
        wraw, wdraw, gate_act, act, fnorm, ident = (bufs[x] for x in ("wraw", "wdraw", "gate_act", "act", "fnorm", "ident"))
        h2_hi = sb("h2_hi", [P, KC, GROUP * P], F32R)
        h2_lo = sb("h2_lo", [P, KC, GROUP * P], F32R)
        w_hi = sb("w_hi", [P, PER, 2, KC, P], F32R)
        w_lo = sb("w_lo", [P, PER, 2, KC, P], F32R)
        wd_hi = sb("wd_hi", [P, PER, D_MODEL], F32R)
        wd_lo = sb("wd_lo", [P, PER, D_MODEL], F32R)
        act_hi = sb("act_hi", [P, PER, GROUP * P], F32R)
        act_lo = sb("act_lo", [P, PER, GROUP * P], F32R)
        norm2_in = sb("norm2_in", [KC, P])
        norm2 = sb("norm2", [P, KC])
        eps = sb("eps_b", [P, 1])
        ssum = sb("ssum", [P, GROUP])
        lnv = sb("lnv", [P, GROUP])
        rstd = sb("rstd", [P, GROUP])
        fssum = sb("fssum", [P, GROUP])
        flnv = sb("flnv", [P, GROUP])
        frstd = sb("frstd", [P, GROUP])

        gate_ps = [ctx.enter_context(nc.psum_tensor(f"gate_ps{i}", [P, 512], F32)) for i in range(2)]
        up_ps = [ctx.enter_context(nc.psum_tensor(f"up_ps{i}", [P, 512], F32)) for i in range(2)]
        down_ps = [ctx.enter_context(nc.psum_tensor(f"down_ps{i}", [P, NH, 512], F32)) for i in range(2)]
        wo_ps = gate_ps + up_ps

        setup_loaded = sem("setup_loaded_b")
        zeroed = sem("zeroed_b")
        ident_ready = sem("ident_ready_b")
        norm2_turned = sem("norm2_turned")
        norm2_ready = sem("norm2_ready")
        x_loaded = [sem(f"x_loaded_b{t}") for t in range(GROUP)]
        m_loaded = [sem(f"m_loaded{i}") for i in range(2)]
        m_hi_ready = sem("m_hi_ready")
        m_lo_ready = sem("m_lo_ready")
        wo_pe = sem("wo_pe")
        wo_added = sem("wo_added")
        squared = sem("squared_b")
        ln_done = sem("ln_done_b")
        rstd_ready = sem("rstd_ready_b")
        h2_ready = sem("h2_ready")
        h2_turned = sem("h2_turned")
        h2s_ready = sem("h2s_ready")
        h2_hi_ready = sem("h2_hi_ready")
        h2_lo_ready = sem("h2_lo_ready")
        w_loaded = [sem(f"w_loaded{c}") for c in range(PER)]
        w_hi_ready = [sem(f"w_hi_ready{c}") for c in range(PER)]
        w_lo_ready = [sem(f"w_lo_ready{c}") for c in range(PER)]
        wd_loaded = sem("wd_loaded")
        wd_hi_ready = sem("wd_hi_ready")
        wd_lo_ready = sem("wd_lo_ready")
        gate_done = [[sem(f"gate_done{c}{h}") for h in range(2)] for c in range(PER)]
        up_done = [[sem(f"up_done{c}{h}") for h in range(2)] for c in range(PER)]
        silu_done = [[sem(f"silu_done{c}{h}") for h in range(2)] for c in range(PER)]
        act_ready = [[sem(f"act_ready{c}{h}") for h in range(2)] for c in range(PER)]
        act_hi_ready = [[sem(f"act_hi_ready{c}{h}") for h in range(2)] for c in range(PER)]
        act_lo_ready = [[sem(f"act_lo_ready{c}{h}") for h in range(2)] for c in range(PER)]
        down_done = [sem(f"down_done{t}") for t in range(GROUP)]
        added = [sem(f"added{t}") for t in range(GROUP)]
        fsquared = sem("fsquared")
        fln_done = sem("fln_done")
        frstd_ready = sem("frstd_ready")
        scaled = sem("scaled")
        y_ready = sem("y_ready")
        y_stored = [sem(f"y_stored{i}") for i in range(2)]

        def blocks_of(t, gi):
            return BLOCKS * sum(1 for _, n in groups[:gi] if t < n)

        def last_in(t, n):
            return n - 1 - (n - 1 - t) % 2

        def uses(m, gi):
            return m + (gi + 1) * (USES - BLOCKS)

        block = ctx.enter_context(nc.Block())

        @block.sync
        def _(sp):
            def load_quarter(q, m):
                c = q % PER
                sp.wait_ge(w_lo_ready[c], m) if m > 0 else None
                for dst, src in quarter_loads(wraw, w_o, q):
                    sp.dma_start(dst, src).then_inc(w_loaded[c], 16)

            def load_block(b, gi):
                m = b + gi * BLOCKS
                for c in range(PER):
                    sp.wait_ge(w_lo_ready[c], uses(m, gi))
                    cols = bass.ds((b * PER + c) * P, P)
                    sp.dma_start(wraw[:, c, 0], wg_dram[:, :, cols]).then_inc(w_loaded[c], 16)
                    sp.dma_start(wraw[:, c, 1], wu_dram[:, :, cols]).then_inc(w_loaded[c], 16)
                if not (isinstance(m, int) and m == 0):
                    sp.wait_ge(wd_lo_ready, m)
                sp.dma_start(wdraw[:], wd_dram[:, bass.ds(b * PER, PER), :]).then_inc(wd_loaded, 16)

            def load_mixed(k):
                if k >= 2:
                    sp.wait_ge(m_lo_ready, k - 1)
                sp.dma_start(mraw[:, k % 2].rearrange("p k i -> p (k i)"), mixed[k]).then_inc(m_loaded[k % 2], 16)

            for semaphore, count in ([(m_loaded[k], 16) for k in range(2)] + [(w_loaded[c], 32) for c in range(PER)] +
                                     [(x_loaded[t], 16) for t in range(AHEAD_X)]):
                sp.sem_inc(semaphore, count)
            sp.dma_start(norm2_in[:], norm2_row.rearrange("(c p) -> c p", p=P)).then_inc(setup_loaded, 16)
            sp.dma_start(fnorm[:], final_norm.rearrange("(a n) -> a n", a=1).to_broadcast([P, D_MODEL]))\
              .then_inc(setup_loaded, 16)
            for gi, (g, n) in enumerate(groups):
                if gi == 0:
                    for t in range(2, n):
                        load_mixed(t)
                    for t in range(AHEAD_X, n):
                        sp.dma_start(acc[:, t, :], x_tiles[t]).then_inc(x_loaded[t], 16)
                    for q in range(2, QUARTERS):
                        load_quarter(q, q // PER)
                load_block(0, gi)
                with sp.Fori(1, BLOCKS) as b:
                    load_block(b, gi)
                n_next = groups[gi + 1][1] if gi + 1 < len(groups) else 0
                if n_next:
                    for q in range(2):
                        load_quarter(q, (gi + 1) * USES)
                    load_mixed(g + n)
                    load_mixed(g + n + 1)
                for t in range(n + 1):
                    if 2 <= t + 2 < n_next:
                        load_mixed(g + n + t + 2)
                    if t > 0:
                        sp.wait_ge(y_ready, g + t)
                        sp.dma_start(y_tiles[g + t - 1], y_out[:, (g + t - 1) % 2]).then_inc(y_stored[(g + t - 1) % 2], 16)
                        if t - 1 < n_next:
                            sp.dma_start(acc[:, t - 1, :], x_tiles[g + n + t - 1]).then_inc(x_loaded[t - 1], 16)
                for q in range(2, QUARTERS if n_next else 0):
                    load_quarter(q, (gi + 1) * USES + q // PER)
            for i in range(2):
                sp.wait_ge(y_stored[i], 16 * ((TILES + 1 - i) // 2))

        @block.gpsimd
        def _(pool):
            pool.memset(eps[:], EPS).then_inc(zeroed, 1)
            pool.memset(ident[:], 0.0).then_inc(zeroed, 1)
            pool.wait_ge(zeroed, 2)
            pool.affine_select(out=ident[:], in_=ident[:], compare_op=ALU.not_equal, fill=1.0, base=0,
                               pattern=[[-1, P]], channel_multiplier=1).then_inc(ident_ready, 1)

        @block.scalar
        def _(act_e):
            def split_columns(c, m, used=None, count=0):
                act_e.wait_ge(w_loaded[c], (m + 1) * 32)
                if used is not None:
                    act_e.wait_ge(used, count)
                act_e.activation(w_hi[:, c], wraw[:, c], ACT.Copy).then_inc(w_hi_ready[c], 1)

            def split_rows(m):
                act_e.wait_ge(wd_loaded, (m + 1) * 16)
                act_e.activation(wd_hi[:], wdraw[:], ACT.Copy).then_inc(wd_hi_ready, 1)

            def hidden(c, h, m, half):
                act_e.wait_ge(gate_done[c][h], m + 1)
                act_e.activation(gate_act[:, h, 0:half], gate_ps[h][:, 0:half], ACT.Silu)\
                     .then_inc(silu_done[c][h], 1)
                act_e.wait_ge(act_ready[c][h], m + 1)
                act_e.activation(act_hi[:, c, h * half:(h + 1) * half], act[:, h, 0:half], ACT.Copy)\
                     .then_inc(act_hi_ready[c][h], 1)

            def split_mixed(gi, g, t):
                k = g + t
                act_e.wait_ge(m_loaded[k % 2], 16 * (k // 2 + 1))
                if gi > 0 and t == 0:
                    act_e.wait_ge(up_done[PER - 1][1], gi * BLOCKS)
                act_e.activation(h2_hi[:, :, t * P:(t + 1) * P], mraw[:, k % 2], ACT.Copy).then_inc(m_hi_ready, 1)

            def exp_and_ln():
                act_e.preload_act_table_set("natural_log_exp_and_others")

            def factor(t, count, sums, logs, factors, squared_, ln_, ready):
                own = slice(t, t + 1)
                act_e.activation(squares[:], acc[:, t, :], ACT.Square, accum_out=sums[:, own]).then_inc(squared_, 1)
                act_e.wait_ge(squared_, count)
                act_e.activation(logs[:, own], sums[:, own], ACT.Ln, bias=eps[:], scale=1.0 / D_MODEL).then_inc(ln_, 1)
                act_e.wait_ge(ln_, count)
                act_e.activation(factors[:, own], logs[:, own], ACT.Exp, scale=-0.5).then_inc(ready, 1)

            act_e.wait_ge(zeroed, 1)
            split_mixed(0, 0, 0)
            split_columns(0, 0)
            exp_and_ln()
            for t in range(1, 3):
                split_mixed(0, 0, t)
            split_columns(1, 0)
            for t in range(3, groups[0][1]):
                split_mixed(0, 0, t)
            for gi, (g, n) in enumerate(groups):
                half = n * P // 2
                for q in range(3):
                    split_columns(q % PER, gi * USES + 1 + q // PER, wo_pe, QUARTERS * g + (q + 1) * n)
                for t in range(n + 2):
                    if t < n:
                        act_e.wait_ge(wo_added, QUARTERS * g + (QUARTERS - 1) * n + t + 1)
                        factor(t, g + t + 1, ssum, lnv, rstd, squared, ln_done, rstd_ready)
                    if t >= 2:
                        act_e.wait_ge(h2s_ready, g + t - 1)
                        act_e.activation(h2_hi[:, :, (t - 2) * P:(t - 1) * P], h2s[:, t % 2], ACT.Copy)\
                             .then_inc(h2_hi_ready, 1)
                split_columns(1, gi * USES + 2, wo_pe, QUARTERS * (g + n))
                act_e.preload_act_table_set("silu_and_others")
                if gi > 0:
                    last_tile = groups[gi - 1][1] - 1
                    act_e.wait_ge(down_done[last_tile], blocks_of(last_tile, gi))
                split_rows(gi * BLOCKS)

                def block_of(b, ahead):
                    m = b + gi * BLOCKS
                    hidden(0, 0, m, half)
                    hidden(0, 1, m, half)
                    if ahead:
                        split_columns(0, uses(m, gi) + 1, up_done[0][1], m + 1)
                    hidden(1, 0, m, half)
                    hidden(1, 1, m, half)
                    if ahead:
                        split_columns(1, uses(m, gi) + 1, up_done[1][1], m + 1)
                        if not (isinstance(b, int) and b == BLOCKS - 1):
                            act_e.wait_ge(down_done[n - 1], b + blocks_of(n - 1, gi) + 1)
                            split_rows(m + 1)

                block_of(0, True)
                with act_e.Fori(1, BLOCKS - 1) as b:
                    block_of(b, True)
                block_of(BLOCKS - 1, gi + 1 < len(groups))
                exp_and_ln()
                n_next = groups[gi + 1][1] if gi + 1 < len(groups) else 0
                for t in range(n):
                    if t < n_next:
                        split_mixed(gi + 1, g + n, t)
                    act_e.wait_ge(added[t], blocks_of(t, gi + 1))
                    factor(t, g + t + 1, fssum, flnv, frstd, fsquared, fln_done, frstd_ready)

        @block.vector
        def _(dve):
            def split_columns(c, m):
                dve.wait_ge(w_hi_ready[c], m + 1)
                dve.tensor_tensor(w_lo[:, c], wraw[:, c], w_hi[:, c].bitcast(F32), ALU.subtract)\
                   .then_inc(w_lo_ready[c], 1)

            def split_rows(m):
                dve.wait_ge(wd_hi_ready, m + 1)
                dve.tensor_tensor(wd_lo[:], wdraw[:], wd_hi[:].bitcast(F32), ALU.subtract).then_inc(wd_lo_ready, 1)

            def hidden(c, h, m, half):
                dve.wait_ge(silu_done[c][h], m + 1)
                dve.wait_ge(up_done[c][h], m + 1)
                dve.tensor_tensor(act[:, h, 0:half], up_ps[h][:, 0:half], gate_act[:, h, 0:half], ALU.mult)\
                   .then_inc(act_ready[c][h], 1)
                dve.wait_ge(act_hi_ready[c][h], m + 1)
                dve.wait_ge(act_ready[c][h], m + 1)
                dve.tensor_tensor(act_lo[:, c, h * half:(h + 1) * half], act[:, h, 0:half],
                                  act_hi[:, c, h * half:(h + 1) * half].bitcast(F32), ALU.subtract)\
                   .then_inc(act_lo_ready[c][h], 1)

            def add_tile(t, m):
                dve.wait_ge(down_done[t], m + 1)
                if not (isinstance(m, int) and m == 0):
                    dve.wait_ge(added[t], m)
                dve.tensor_tensor(acc[:, t, :], down_ps[t % 2][:].rearrange("p a b -> p (a b)"), acc[:, t, :],
                                  ALU.add).then_inc(added[t], 1)

            def block_of(b, gi, n, ahead):
                m = b + gi * BLOCKS
                half = n * P // 2
                hidden(0, 0, m, half)
                hidden(0, 1, m, half)
                if ahead:
                    split_columns(0, uses(m, gi) + 1)
                hidden(1, 0, m, half)
                hidden(1, 1, m, half)
                if isinstance(b, int) and b == BLOCKS - 1:
                    return
                for t in range(n):
                    add_tile(t, b + blocks_of(t, gi))
                    if t == 1 and ahead:
                        split_columns(1, uses(m, gi) + 1)
                split_rows(m + 1)

            def split_mixed(g, t):
                dve.wait_ge(m_hi_ready, g + t + 1)
                dve.tensor_tensor(h2_lo[:, :, t * P:(t + 1) * P], mraw[:, (g + t) % 2],
                                  h2_hi[:, :, t * P:(t + 1) * P].bitcast(F32), ALU.subtract).then_inc(m_lo_ready, 1)

            def add_quarter(q, t, gi, g, n):
                if q == 0:
                    dve.wait_ge(x_loaded[t], 16 * (gi + 1))
                i = q * n + t
                dve.wait_ge(wo_pe, QUARTERS * g + i + 1)
                part = acc[:, t, q * QC:(q + 1) * QC]
                dve.tensor_tensor(part, wo_ps[i % 4][:, 0:QC], part, ALU.add).then_inc(wo_added, 1)

            def scale_tile(t, k):
                dve.wait_ge(rstd_ready, k + 1)
                if k >= 2:
                    dve.wait_ge(h2_turned, k - 1)
                dve.tensor_scalar(h2[:, t % 2], acc[:, t, :], rstd[:, t:t + 1], None, ALU.mult).then_inc(h2_ready, 1)

            def take_turned(t, k):
                dve.wait_ge(h2_turned, k + 1)
                if k >= 2:
                    dve.wait_ge(h2_lo_ready, k - 1)
                dve.tensor_tensor(h2s[:, t % 2], down_ps[t % 2][:].rearrange("p a (b c) -> p (a b) c", c=P),
                                  norm2[:].rearrange("p (c a) -> p c a", a=1).to_broadcast([P, KC, P]),
                                  ALU.mult).then_inc(h2s_ready, 1)

            def split_turned(t, k):
                dve.wait_ge(h2_hi_ready, k + 1)
                dve.tensor_tensor(h2_lo[:, :, t * P:(t + 1) * P], h2s[:, t % 2],
                                  h2_hi[:, :, t * P:(t + 1) * P].bitcast(F32), ALU.subtract).then_inc(h2_lo_ready, 1)

            split_mixed(0, 0)
            split_columns(0, 0)
            for t in range(1, 3):
                split_mixed(0, t)
            split_columns(1, 0)
            for t in range(3, groups[0][1]):
                split_mixed(0, t)
            for gi, (g, n) in enumerate(groups):
                for q in range(QUARTERS - 1):
                    for t in range(n):
                        add_quarter(q, t, gi, g, n)
                    if gi == 0 and q == 1:
                        dve.wait_ge(norm2_turned, 1)
                        dve.tensor_copy(norm2[:], down_ps[0][:, 0, 0:KC]).then_inc(norm2_ready, 1)
                        dve.wait_ge(norm2_ready, 1)
                        dve.wait_ge(setup_loaded, 32)
                    split_columns(q % PER, gi * USES + 1 + q // PER)
                for t in range(n + 3):
                    if t >= 3:
                        split_turned(t - 3, g + t - 3)
                    if t < n:
                        add_quarter(QUARTERS - 1, t, gi, g, n)
                    if 1 <= t <= n:
                        scale_tile(t - 1, g + t - 1)
                    if 2 <= t <= n + 1:
                        take_turned(t - 2, g + t - 2)
                split_columns(1, gi * USES + 2)
                split_rows(gi * BLOCKS)
                block_of(0, gi, n, True)
                with dve.Fori(1, BLOCKS - 1) as b:
                    block_of(b, gi, n, True)
                n_next = groups[gi + 1][1] if gi + 1 < len(groups) else 0
                block_of(BLOCKS - 1, gi, n, n_next > 0)
                for t in range(n + 1):
                    if t < n:
                        add_tile(t, BLOCKS - 1 + blocks_of(t, gi))
                    if t < n_next:
                        split_mixed(g + n, t)
                    if t == n and n_next:
                        split_columns(1, (gi + 1) * USES)
                    if t > 0:
                        k = g + t - 1
                        dve.wait_ge(frstd_ready, k + 1)
                        if k >= 2:
                            dve.wait_ge(y_stored[k % 2], 16 * (k // 2))
                        dve.scalar_tensor_tensor(out=y_out[:, k % 2], in0=acc[:, t - 1, :], scalar=frstd[:, t - 1:t],
                                                 in1=fnorm[:], op0=ALU.mult, op1=ALU.mult).then_inc(y_ready, 1)

        @block.tensor
        def _(pe):
            def three(out, w_h, w_l, x_h, x_l, start, stop):
                pe.matmul(out, w_h, x_h, start=start, stop=False)
                pe.matmul(out, w_h, x_l, start=False, stop=False)
                return pe.matmul(out, w_l, x_h, start=False, stop=stop)

            def past(semaphore, count):
                if not (isinstance(count, int) and count == 0):
                    pe.wait_ge(semaphore, count)

            def hidden(c, h, m, half, between=None):
                cols = slice(h * half, (h + 1) * half)
                before = (PER - 1, m) if c == 0 else (c - 1, m + 1)
                past(silu_done[before[0]][h], before[1])
                for k in range(KC):
                    last = three(gate_ps[h][:, 0:half], w_hi[:, c, 0, k], w_lo[:, c, 0, k],
                                 h2_hi[:, k, cols], h2_lo[:, k, cols], k == 0, k == KC - 1)
                last.then_inc(gate_done[c][h], 1)
                if between is not None:
                    between()
                past(act_ready[before[0]][h], before[1])
                for k in range(KC):
                    last = three(up_ps[h][:, 0:half], w_hi[:, c, 1, k], w_lo[:, c, 1, k],
                                 h2_hi[:, k, cols], h2_lo[:, k, cols], k == 0, k == KC - 1)
                last.then_inc(up_done[c][h], 1)

            def down(t, b, gi, n, m):
                half = n * P // 2
                if t >= 2:
                    pe.wait_ge(added[t - 2], b + blocks_of(t - 2, gi) + 1)
                else:
                    past(added[last_in(t, n)], b + blocks_of(last_in(t, n), gi))
                for c in range(PER):
                    for h in range(2):
                        if h * half < (t + 1) * P and (h + 1) * half > t * P:
                            pe.wait_ge(act_lo_ready[c][h], m + 1)
                for a in range(NH):
                    for c in range(PER):
                        last = three(down_ps[t % 2][:, a, :], act_hi[:, c, t * P:(t + 1) * P],
                                     act_lo[:, c, t * P:(t + 1) * P], wd_hi[:, c, a * 512:(a + 1) * 512],
                                     wd_lo[:, c, a * 512:(a + 1) * 512], c == 0, c == PER - 1)
                last.then_inc(down_done[t], 1)

            def block_of(b, g, gi, n):
                m = b + gi * BLOCKS
                half = n * P // 2
                first = isinstance(b, int) and b == 0
                for c in range(PER):
                    pe.wait_ge(w_lo_ready[c], uses(m, gi) + 1)
                    for h in range(2):
                        if first and c == 0:
                            pe.wait_ge(wo_added, QUARTERS * (g + n))
                            pe.wait_ge(h2_lo_ready, g + (-(-half // P) if h == 0 else n))
                            hidden(c, h, m, half, (lambda: turn(n - 1, g, gi)) if h == 0 else None)
                        else:
                            hidden(c, h, m, half)
                pe.wait_ge(wd_lo_ready, m + 1)
                for t in range(n):
                    down(t, b, gi, n, m)

            def wo_product(q, t, g, gi, n):
                c, i = q % PER, q * n + t
                quarter = [w[:, c].rearrange("p a k i -> p (a k i)").rearrange("p (k i) -> p k i", k=KC)
                           for w in (w_hi, w_lo)]
                if i >= 4:
                    pe.wait_ge(wo_added, QUARTERS * g + i - 3)
                elif gi > 0:
                    pe.wait_ge((silu_done if i < 2 else act_ready)[PER - 1][i % 2], gi * BLOCKS)
                if q == 0:
                    pe.wait_ge(m_lo_ready, g + t + 1)
                own = slice(t * P, (t + 1) * P)
                for k in range(KC):
                    last = three(wo_ps[i % 4][:, 0:QC], h2_hi[:, k, own], h2_lo[:, k, own],
                                 quarter[0][:, k], quarter[1][:, k], k == 0, k == KC - 1)
                last.then_inc(wo_pe, 1)

            def turn(t, g, gi):
                pe.wait_ge(h2_ready, g + t + 1)
                if t >= 2:
                    pe.wait_ge(h2s_ready, g + t - 1)
                elif gi > 0:
                    before = last_in(t, groups[gi - 1][1])
                    pe.wait_ge(added[before], blocks_of(before, gi))
                for k in range(KC):
                    last = pe.transpose(down_ps[t % 2][:, k // 4, (k % 4) * P:(k % 4 + 1) * P],
                                        h2[:, t % 2, k * P:(k + 1) * P], ident[:])
                last.then_inc(h2_turned, 1)

            for gi, (g, n) in enumerate(groups):
                for q in range(QUARTERS):
                    if gi == 0 and q == 1:
                        pe.wait_ge(ident_ready, 1)
                        pe.wait_ge(setup_loaded, 32)
                        pe.transpose(down_ps[0][:, 0, 0:KC], norm2_in[:], ident[0:KC, 0:KC]).then_inc(norm2_turned, 1)
                    if gi == 0 and q == QUARTERS - 1:
                        pe.wait_ge(norm2_ready, 1)
                    pe.wait_ge(w_lo_ready[q % PER], gi * USES + q // PER + 1)
                    for t in range(n):
                        wo_product(q, t, g, gi, n)
                        if q == QUARTERS - 1 and t >= 2:
                            turn(t - 2, g, gi)
                turn(n - 2, g, gi)
                block_of(0, g, gi, n)
                with pe.Fori(1, BLOCKS) as b:
                    block_of(b, g, gi, n)




def stream_step(nc, t, outs, scratch):
    y_prompt, y_sample, gdn_prompt, conv_prompt, gdn_sample, conv_sample, v_sample = outs
    x_prompt = t["x_prompt"][0].rearrange("(a p) n -> a p n", p=P)
    x_sample = t["x_sample"].rearrange("b t n -> (b t) n").rearrange("(a p) n -> a p n", p=P)
    n_prompt = x_prompt.shape[0]
    weights = {k: t[k][0] for k in ("w_in", "conv_w", "a_log", "dt_bias", "gdn_norm", "gmlp_ws", "gmlp_bs",
                                    "gmlp_norm", "norm1")}
    y_p = y_prompt[0].rearrange("(a p) n -> a p n", p=P)
    x_tiles = [x_prompt[i] for i in range(n_prompt)] + [x_sample[0]]
    y_tiles = [y_p[i] for i in range(n_prompt)] + [y_sample.rearrange("b t n -> (b t) n")]
    w_o = t["w_o"][0]
    with nc.sbuf_tensor("w_in_sb", [P, D_MODEL // P, weights["w_in"].shape[1]], F32) as region:
        bufs = out_buffers(region)
        with ExitStack() as ctx:
            shared = mix_setup(nc, ctx, region)
            mix_phase(nc, shared, dict(
                x=x_sample, y=scratch[n_prompt:], new_gdn=gdn_sample[0], new_conv=conv_sample[0].rearrange("b r n -> (b r) n"),
                new_v=v_sample[0].rearrange("b t n -> (b t) n"), state_gdn=t["state_gdn"][0],
                state_conv=t["state_conv"][0], **weights), True)
            mix_phase(nc, shared, dict(
                x=x_prompt, y=scratch[0:n_prompt], new_gdn=gdn_prompt[0, 0], new_conv=conv_prompt[0, 0],
                ahead=loads_ahead(bufs, x_tiles, scratch, w_o), **weights), False)
        out_phase(nc, bufs, x_tiles, scratch, w_o, t["norm2"][0], t["w_gate"][0], t["w_up"][0], t["w_down"][0],
                  t["final_norm"], y_tiles)


def kernel(**inputs):
    import concourse.bacc as bacc
    import numpy as np
    from concourse.bass_utils import run_bass_kernel_spmd

    nc = bacc.Bacc("TRN2", target_bir_lowering=False, num_devices=1)
    arrays, tensors = {}, {}
    for name, value in inputs.items():
        arrays["in_" + name] = np.ascontiguousarray(value)
        tensors[name] = nc.dram_tensor("in_" + name, value.shape, F32, kind="ExternalInput").ap()
    shapes = [inputs["x_prompt"].shape, inputs["x_sample"].shape, (1, 1, H_B, DK, DV), (1, 1, CONV_W - 1, 3 * D_B),
              (1, DEC_BATCH, H_B, DK, DV), (1, DEC_BATCH, CONV_W - 1, 3 * D_B), (1, DEC_BATCH, DEC_SEQ, D_A)]
    outs = [nc.dram_tensor(f"out_{i}", shape, F32, kind="ExternalOutput").ap() for i, shape in enumerate(shapes)]
    tiles = SEQ // P + DEC_BATCH * DEC_SEQ // P
    scratch = nc.dram_tensor("mixed_tiles", (tiles, P, D_MODEL), F32, kind="Internal").ap()
    stream_step(nc, tensors, outs, scratch)
    result = run_bass_kernel_spmd(nc, [arrays], core_ids=[0]).results[0]
    return tuple(result[f"out_{i}"] for i in range(len(shapes)))
```
